# Optimizing a Trainium2 kernel written in Bass

```python
import jax
import jax.numpy as jnp
from jax import lax
import numpy as np

D_MODEL = 2048
BATCH = 1
SEQ = 256
DEPTH = 1

GRID_W = 64
NA_HEADS = 16
NA_HEAD_DIM = 64
NA_WIDTH = NA_HEADS * NA_HEAD_DIM
NA_WIN_R = 8
NA_WIN_C = 16
GLA_HEADS = 4
GLA_DK = D_MODEL // (2 * GLA_HEADS)
GLA_DV = D_MODEL // GLA_HEADS
GLA_K = GLA_HEADS * GLA_DK
GLA_V = GLA_HEADS * GLA_DV
GLA_GATE_RANK = 16
GLA_TAU = 16.0
GLA_CHUNK = 64
PEER_HEADS = 8
PEER_NKEYS = 128
PEER_N = PEER_NKEYS * PEER_NKEYS
PEER_DKEY = 256
PEER_TOPK = 16
PEER_BLOCK = 128
PLE_DIM = 256
LN_EPS = 1e-5
DEEPNORM_ALPHA = (2.0 * DEPTH) ** 0.25
DEEPNORM_BETA = (8.0 * DEPTH) ** -0.25

IN_SPLITS = (NA_WIDTH, NA_WIDTH, NA_WIDTH, GLA_K, GLA_K, GLA_V, GLA_V, GLA_GATE_RANK, GLA_GATE_RANK, D_MODEL, D_MODEL)
IN_WIDTH = sum(IN_SPLITS)
IN_SPLIT_POINTS = tuple(int(c) for c in np.cumsum(IN_SPLITS)[:-1])

kernel_name = 'hybrid_natten_gla_peer_encoder'

def layer_norm(x, g, b):
    xf = x.astype(jnp.float32)
    mu = jnp.mean(xf, axis=-1, keepdims=True)
    var = jnp.mean(jnp.square(xf - mu), axis=-1, keepdims=True)
    y = (xf - mu) * lax.rsqrt(var + LN_EPS)
    return (y * g.astype(jnp.float32) + b.astype(jnp.float32)).astype(x.dtype)

def to_heads(t, n_heads):
    bsz, s, _ = t.shape
    return t.reshape(bsz, s, n_heads, -1).transpose(0, 2, 1, 3)

def neighbourhood_attention(q, k, v, rpb):
    bsz, s, h, dh = q.shape
    rows = s // GRID_W
    kr = min(NA_WIN_R, rows)
    kc = NA_WIN_C

    def to_grid(t):
        return t.reshape(bsz, rows, GRID_W, h, dh).transpose(1, 0, 3, 2, 4)

    qg = to_grid(q * (dh ** -0.5))
    kg = to_grid(k)
    vg = to_grid(v)
    cols = jnp.arange(GRID_W)
    col_idx = jnp.clip(cols - kc // 2, 0, GRID_W - kc)[:, None] + jnp.arange(kc)[None, :]
    dc = col_idx - cols[:, None] + (NA_WIN_C - 1)

    def row_block(r):
        r0 = jnp.clip(r - kr // 2, 0, rows - kr)
        k_win = lax.dynamic_slice_in_dim(kg, r0, kr, axis=0)[:, :, :, col_idx, :]
        v_win = lax.dynamic_slice_in_dim(vg, r0, kr, axis=0)[:, :, :, col_idx, :]
        dr = r0 + jnp.arange(kr) - r + (NA_WIN_R - 1)
        bias = rpb[:, dr[:, None, None], dc[None, :, :]].transpose(0, 2, 1, 3)
        scores = jnp.einsum('bhwd,ibhwjd->bhwij', qg[r], k_win).astype(jnp.float32)
        scores = scores + bias.astype(jnp.float32)[None]
        probs = jax.nn.softmax(scores.reshape(bsz, h, GRID_W, kr * kc), axis=-1)
        probs = probs.reshape(bsz, h, GRID_W, kr, kc).astype(v.dtype)
        return jnp.einsum('bhwij,ibhwjd->bhwd', probs, v_win)

    out = lax.map(row_block, jnp.arange(rows))
    return out.transpose(1, 0, 3, 2, 4).reshape(bsz, s, h * dh)

def gla_chunked(q, k, v, log_a, include_diag):
    bsz, h, s, dk = q.shape
    dv = v.shape[-1]
    c = GLA_CHUNK
    n = s // c
    f32 = jnp.float32
    qc = q.astype(f32).reshape(bsz, h, n, c, dk)
    kc = k.astype(f32).reshape(bsz, h, n, c, dk)
    vc = v.astype(f32).reshape(bsz, h, n, c, dv)
    b = jnp.cumsum(log_a.astype(f32).reshape(bsz, h, n, c, dk), axis=3)
    b_last = b[:, :, :, -1:, :]
    q_dec = qc * jnp.exp(b)
    k_intra = kc * jnp.exp(-b)
    k_state = kc * jnp.exp(b_last - b)
    mask = jnp.tril(jnp.ones((c, c), dtype=bool), 0 if include_diag else -1)
    attn = jnp.where(mask, jnp.einsum('bhnik,bhnjk->bhnij', q_dec, k_intra), 0.0)
    o_intra = jnp.einsum('bhnij,bhnjv->bhniv', attn, vc)

    def step(state, xs):
        q_d, k_s, v_n, decay = xs
        o = jnp.einsum('bhck,bhkv->bhcv', q_d, state)
        state = decay[..., None] * state + jnp.einsum('bhck,bhcv->bhkv', k_s, v_n)
        return state, o

    xs = (jnp.moveaxis(q_dec, 2, 0), jnp.moveaxis(k_state, 2, 0), jnp.moveaxis(vc, 2, 0),
          jnp.moveaxis(jnp.exp(b_last[:, :, :, 0, :]), 2, 0))
    _, o_inter = lax.scan(step, jnp.zeros((bsz, h, dk, dv), f32), xs)
    o = o_intra + jnp.moveaxis(o_inter, 0, 2)
    return o.reshape(bsz, h, s, dv)

def peer(x, w_q, sub_keys, u, v):
    bsz, s, d = x.shape
    kk = PEER_TOPK
    q = (x @ w_q).reshape(bsz, s, PEER_HEADS, 2, PEER_DKEY // 2)
    sc = jnp.einsum('bshpk,hpnk->bshpn', q, sub_keys).astype(jnp.float32)
    val, idx = lax.top_k(sc, kk)
    cand = val[..., 0, :, None] + val[..., 1, None, :]
    cand_idx = idx[..., 0, :, None] * PEER_NKEYS + idx[..., 1, None, :]
    top_val, top_pos = lax.top_k(cand.reshape(bsz, s, PEER_HEADS, kk * kk), kk)
    expert = jnp.take_along_axis(cand_idx.reshape(bsz, s, PEER_HEADS, kk * kk), top_pos, axis=-1)
    gate = jax.nn.softmax(top_val, axis=-1)
    n_blocks = (bsz * s) // PEER_BLOCK
    xb = x.reshape(n_blocks, PEER_BLOCK, d)
    eb = expert.reshape(n_blocks, PEER_BLOCK, PEER_HEADS * kk)
    gb = gate.reshape(n_blocks, PEER_BLOCK, PEER_HEADS * kk).astype(x.dtype)

    def block(args):
        xt, et, gt = args
        hid = jnp.einsum('td,ted->te', xt, u[et])
        w = gt * jax.nn.gelu(hid, approximate=False)
        return jnp.einsum('te,ted->td', w, v[et])

    y = lax.map(block, (xb, eb, gb))
    return y.reshape(bsz, s, d)

def setup_inputs(seed: int = 0) -> dict:
    key = jax.random.key(seed)
    ks = jax.random.split(key, 25)

    def nrm(k, shape, scale):
        return jax.random.normal(k, shape, jnp.float32) * scale

    L, D = DEPTH, D_MODEL
    return {
        'x': nrm(ks[0], (BATCH, SEQ, D), 1.0),
        'p': nrm(ks[1], (L, BATCH, SEQ, PLE_DIM), 1.0),
        'ln_emb_g': 1.0 + nrm(ks[2], (D,), 0.02),
        'ln_emb_b': nrm(ks[3], (D,), 0.02),
        'w_in': nrm(ks[4], (L, D, IN_WIDTH), D ** -0.5),
        'b_in': nrm(ks[5], (L, IN_WIDTH), 0.01),
        'na_rpb': nrm(ks[6], (L, NA_HEADS, 2 * NA_WIN_R - 1, 2 * NA_WIN_C - 1), 0.1),
        'gla_gk_up_f': nrm(ks[7], (L, GLA_GATE_RANK, GLA_K), GLA_GATE_RANK ** -0.5),
        'gla_gk_bias_f': nrm(ks[8], (L, GLA_K), 0.01),
        'gla_gk_up_b': nrm(ks[9], (L, GLA_GATE_RANK, GLA_K), GLA_GATE_RANK ** -0.5),
        'gla_gk_bias_b': nrm(ks[10], (L, GLA_K), 0.01),
        'gla_norm_g': 1.0 + nrm(ks[11], (L, GLA_DV), 0.02),
        'w_proj_a': nrm(ks[12], (L, NA_WIDTH, D), NA_WIDTH ** -0.5),
        'w_proj_b': nrm(ks[13], (L, GLA_V, D), GLA_V ** -0.5),
        'w_out': nrm(ks[14], (L, D, D), DEEPNORM_BETA * D ** -0.5),
        'ln_a_g': 1.0 + nrm(ks[15], (L, D), 0.02),
        'ln_a_b': nrm(ks[16], (L, D), 0.02),
        'peer_wq': nrm(ks[17], (L, D, PEER_HEADS * PEER_DKEY), D ** -0.5),
        'peer_sub_keys': nrm(ks[18], (L, PEER_HEADS, 2, PEER_NKEYS, PEER_DKEY // 2), (PEER_DKEY // 2) ** -0.5),
        'peer_u': nrm(ks[19], (L, PEER_N, D), D ** -0.5),
        'peer_v': nrm(ks[20], (L, PEER_N, D), DEEPNORM_BETA),
        'w_ple': nrm(ks[21], (L, PLE_DIM, D), DEEPNORM_BETA * PLE_DIM ** -0.5),
        'w_ple_gate': nrm(ks[22], (L, D, D), D ** -0.5),
        'ln_b_g': 1.0 + nrm(ks[23], (L, D), 0.02),
        'ln_b_b': nrm(ks[24], (L, D), 0.02),
    }

def reference(x, p, ln_emb_g, ln_emb_b, w_in, b_in, na_rpb, gla_gk_up_f, gla_gk_bias_f,
              gla_gk_up_b, gla_gk_bias_b, gla_norm_g, w_proj_a, w_proj_b, w_out, ln_a_g, ln_a_b,
              peer_wq, peer_sub_keys, peer_u, peer_v, w_ple, w_ple_gate, ln_b_g, ln_b_b):
    bsz, s, d = x.shape
    f32 = jnp.float32
    h = layer_norm(x, ln_emb_g, ln_emb_b)
    for i in range(DEPTH):
        z = h @ w_in[i] + b_in[i]
        (na_q, na_k, na_v, g_q, g_k, g_v, g_out, gk_f_lr, gk_b_lr, gate_a, gate_b) = jnp.split(
            z, IN_SPLIT_POINTS, axis=-1)
        hd = (bsz, s, NA_HEADS, NA_HEAD_DIM)
        y_na = neighbourhood_attention(na_q.reshape(hd), na_k.reshape(hd), na_v.reshape(hd), na_rpb[i])
        y_a = y_na @ w_proj_a[i]
        gq = to_heads(g_q, GLA_HEADS) * (GLA_DK ** -0.5)
        gk = to_heads(g_k, GLA_HEADS)
        gv = to_heads(g_v, GLA_HEADS)
        la_f = to_heads(jax.nn.log_sigmoid((gk_f_lr @ gla_gk_up_f[i] + gla_gk_bias_f[i]).astype(f32)) / GLA_TAU, GLA_HEADS)
        la_b = to_heads(jax.nn.log_sigmoid((gk_b_lr @ gla_gk_up_b[i] + gla_gk_bias_b[i]).astype(f32)) / GLA_TAU, GLA_HEADS)
        o_f = gla_chunked(gq, gk, gv, la_f, True)
        o_b = jnp.flip(gla_chunked(jnp.flip(gq, 2), jnp.flip(gk, 2), jnp.flip(gv, 2), jnp.flip(la_b, 2), False), 2)
        o = (o_f + o_b).transpose(0, 2, 1, 3)
        o = o * lax.rsqrt(jnp.mean(o * o, axis=-1, keepdims=True) + LN_EPS) * gla_norm_g[i].astype(f32)
        o = o.astype(x.dtype) * jax.nn.silu(g_out.reshape(bsz, s, GLA_HEADS, GLA_DV))
        y_b = o.reshape(bsz, s, GLA_V) @ w_proj_b[i]
        merged = jax.nn.sigmoid(gate_a) * y_a + jax.nn.sigmoid(gate_b) * y_b
        h = layer_norm(DEEPNORM_ALPHA * h + merged @ w_out[i], ln_a_g[i], ln_a_b[i])
        ple = (p[i] @ w_ple[i]) * jax.nn.sigmoid(h @ w_ple_gate[i])
        y_c = peer(h, peer_wq[i], peer_sub_keys[i], peer_u[i], peer_v[i])
        h = layer_norm(DEEPNORM_ALPHA * h + y_c + ple, ln_b_g[i], ln_b_b[i])
    return h


_drawn_inputs = setup_inputs


def setup_inputs(seed=0):
    import zlib

    import numpy as np

    out = dict(_drawn_inputs(seed))
    spreads = {}
    factors = {'b_in': 2.969,
     'na_rpb': 2.956,
     'gla_gk_bias_f': 8.0,
     'gla_gk_bias_b': 8.0,
     'gla_norm_g': 3.68,
     'ln_b_g': 2.88,
     'ln_b_b': 2.837}
    for name, (base, spread) in spreads.items():
        noise = np.random.default_rng([zlib.crc32(name.encode()), seed]).standard_normal(out[name].shape)
        drawn = base * np.exp(spread * noise) if base else spread * noise
        out[name] = jnp.asarray(drawn.astype(out[name].dtype))
    for name, factor in factors.items():
        out[name] = (out[name] * factor).astype(out[name].dtype)
    return out
```

```python
from contextlib import ExitStack

import concourse.bass as bass
from concourse import mybir

P = 128
D = 2048
T = 256
KC = D // P
NA_HEADS, NA_DIM, GRID_W, WIN_R, WIN_C = 16, 64, 64, 8, 16
NA_PAIRS = NA_HEADS // 2
GLA_HEADS, DK, DV, CHUNK, RANK = 4, 256, 512, 64, 16
NKB, NVB = DK // P, DV // P
N_CHUNKS = T // CHUNK
PEER_HEADS, NKEYS, TOPK = 8, 128, 16
HP = 2 * PEER_HEADS
PLE = 256
EPS = 1e-5
ALPHA = 2.0 ** 0.25
LOWEST = -3.0e38
MASKED = -1.0e30

TILE = 8 * P
RING = 4
AHEAD = 1
NA_TILES = NA_PAIRS * 6
RANK_TILES = 2
QK_TILES = 8
VG_TILES = 16
HEAD_TILES = VG_TILES + QK_TILES
MERGE_TILES = 7
T_NA = 0
T_RANK = T_NA + NA_TILES
T_GLA = T_RANK + RANK_TILES
T_MERGE = T_GLA + GLA_HEADS * HEAD_TILES
T_OUT = T_MERGE + KC * MERGE_TILES
T_PQ = T_OUT + 2 * KC
T_PLE = T_PQ + 2 * KC
T_PGATE = T_PLE + 4
T_U = T_PGATE + 2 * KC
T_V = T_U + 2 * NKEYS
T_END = T_V + 2 * NKEYS

V_LN = 0
V_NA = V_LN + 6 * KC
V_RANK = V_NA + 3 * NA_PAIRS
V_GLA = V_RANK + 1
GLA_BLOCKS = 2 * NKB + 2 * NVB
V_GATES = V_GLA + GLA_HEADS * GLA_BLOCKS
V_NORM = V_GATES + 2 * KC
V_DECAY = V_NORM + NVB
V_COLS = V_DECAY + 4 * GLA_HEADS


class Pos:

    def __init__(self, const, per=0, i=None):
        self.const, self.per, self.i = const, per, i

    def __add__(self, n):
        return Pos(self.const + n, self.per, self.i)

    def times(self, each, plus=0):
        fixed = self.const * each + plus
        return fixed if self.i is None else self.i * (self.per * each) + fixed

    def over(self, n):
        assert self.per % n == 0
        return Pos(self.const // n, self.per // n, self.i)


def wait(eng, sem, value):
    if isinstance(value, int) and value <= 0:
        return
    eng.wait_ge(sem, value)


class Chain:

    def __init__(self, eng, sem, per, nop=False):
        self.eng, self.sem, self.per, self.turn, self.n = eng, sem, per, None, 0
        self.nop = nop

    def begin(self, turn):
        self.turn, self.n = turn, 0

    def step(self, ins):
        self.n += 1
        ins.then_inc(self.sem, 1)
        self.eng.wait_ge(self.sem, self.turn.times(self.per, self.n))
        if self.nop:
            self.eng.nop(nofuse=True)

    def end(self):
        assert self.n == self.per


def encoder_layer(nc, stream, vectors, x_t, p_t, rpb, decay_up, keys, out):
    F32, F32R, BF16, U32, U8 = (mybir.dt.float32, mybir.dt.float32r, mybir.dt.bfloat16,
                                mybir.dt.uint32, mybir.dt.uint8)
    ALU, ACT, AX = mybir.AluOpType, mybir.ActivationFunctionType, mybir.AxisListType
    ds = bass.ds

    residual_dram = nc.dram_tensor("residual_spill", (P, KC * T), F32, kind="Internal").ap()
    gelu_dram = nc.dram_tensor("gelu_spill", (NKEYS, P, T), F32, kind="Internal").ap()

    with ExitStack() as ctx:
        def sb(name, cols, dt=F32, group=ctx):
            return group.enter_context(nc.sbuf_tensor(name, [P, cols], dt))

        def sem(name):
            return ctx.enter_context(nc.semaphore(name))

        xs = sb("act_split", KC * 2 * T, F32R)
        with ExitStack() as g:
            w_in = sb("weights_in", RING * TILE, group=g)
        w_low = sb("weights_lower", RING * TILE, F32R)
        w_up = sb("weights_upper", RING * TILE, F32R)
        vec = sb("vec_table", V_COLS)
        ident = sb("identity", P)
        mean_w = sb("mean_weights", P)
        iota_key = sb("iota_key", NKEYS)
        iota_top = sb("iota_top", TOPK)
        eps_t = sb("eps", 1)
        zeros = sb("zeros", P, BF16)
        gst = sb("gelu_ring", 4 * T)

        with ExitStack() as g:
            idx0_t = sb("expert_row_t", T, group=g)
            idx1_t = sb("expert_col_t", T, group=g)
            gate_t = sb("expert_gate_t", T, group=g)
            hot0 = sb("hot_rows", 4 * NKEYS, group=g)
            hot1 = sb("hot_cols", 4 * NKEYS, group=g)
        with ExitStack() as g:
            ys = sb("last_split", 2 * 2 * T, F32R, group=g)
            wexp = sb("expert_weight", 2 * T, group=g)
        sb("shared_small", 3 * T + 8 * NKEYS)

        region = ExitStack()
        with region as g:
            nas = sb("na_split", NA_PAIRS * 2 * T, F32R, group=g)
            gls = sb("gla_split", KC * 2 * T, F32R, group=g)
            with ExitStack() as h:
                x_in = sb("x_in", KC * T, group=h)
                sq_in = sb("sq_in", KC * T, group=h)
            with ExitStack() as h:
                na_qkv = sb("na_qkv", 2 * 3 * T, group=h)
                na_bias = sb("na_bias", 2 * 4 * T, group=h)
                na_s = sb("na_scores", 4 * T, group=h)
                na_pt = sb("na_probs_t", 4 * T, group=h)
                na_v = sb("na_v", 2 * P, group=h)
                na_small = sb("na_small", 16, group=h)
            with ExitStack() as h:
                g_z = sb("gla_z", 4 * T, group=h)
                g_a = sb("gla_a", 4 * T, group=h)
                g_c = sb("gla_cum", 4 * T, group=h)
                g_qd = sb("gla_q_decayed", 4 * T, group=h)
                g_ki = sb("gla_k_intra", 4 * T, group=h)
                g_ks = sb("gla_k_state", 4 * T, group=h)
                g_kt = sb("gla_k_state_t", 4 * T, group=h)
                g_q = sb("gla_q", NKB * T, group=h)
                g_k = sb("gla_k", NKB * T, group=h)
                g_vt = sb("gla_v_t", NVB * T, group=h)
                g_rank = sb("gla_rank", T, group=h)
                g_up = sb("gla_up", DK, group=h)
                g_v = sb("gla_v", 2 * DV, group=h)
                g_att = sb("gla_att", 2 * CHUNK, group=h)
                g_state = sb("gla_state", 4 * DV, group=h)
                g_dec = sb("gla_chunk_decay", 16, group=h)
                g_x = sb("gla_gate_in", NVB * T, group=h)
                g_sg = sb("gla_gate_sig", NVB * T, group=h)
                g_on = sb("gla_out_normed", 2 * DV, group=h)
                g_ot = sb("gla_out_t", NVB * T, group=h)
                g_small = sb("gla_small", 8, group=h)
                g_reset = sb("gla_reset", 2 * T, group=h)
                g_mask = sb("gla_mask", 2 * CHUNK, U8, group=h)
                g_maskf = sb("gla_mask_f", 2 * CHUNK, group=h)
            with ExitStack() as h:
                ms = sb("merged_split", KC * 2 * T, F32R, group=h)
                res = sb("residual", KC * T, group=h)
                sq_a = sb("sq_a", KC * T, group=h)
                m_sa = sb("merge_sig_a", 2 * T, group=h)
                m_sb = sb("merge_sig_b", 2 * T, group=h)
                m_a = sb("merge_a", 2 * T, group=h)
                m_m = sb("merge_sum", 2 * T, group=h)
        with ExitStack() as g:
            sc = sb("key_scores", 2 * HP * NKEYS, group=g)
            key_t = sb("keys_t", HP * NKEYS, group=g)
            pq = sb("peer_q", 2 * T, group=g)
            ple = sb("ple", KC * T, group=g)
            p_in = sb("p_in", 2 * T, group=g)
            sgm = sb("ple_sig", 2 * T, group=g)
            ple_g = sb("ple_gated", 2 * T, group=g)
            tk_in = sb("top_scores", 2 * NKEYS, group=g)
            tk_w = sb("top_rest", 2 * NKEYS, group=g)
            tk_v = sb("top_values", 2 * TOPK, group=g)
            tk_i = sb("top_index", 2 * TOPK, U32, group=g)
            tk_if = sb("top_index_f", 2 * TOPK, group=g)
            tk_c = sb("pair_sums", TOPK * TOPK, group=g)
            tk_cw = sb("pair_rest", TOPK * TOPK, group=g)
            tk_cv = sb("pair_values", TOPK, group=g)
            tk_cp = sb("pair_pos", TOPK, U32, group=g)
            tk_ab = sb("pair_ranks", 2 * TOPK, U32, group=g)
            tk_abf = sb("pair_ranks_f", 2 * TOPK, group=g)
            tk_eq = sb("pair_match", 2 * TOPK * TOPK, group=g)
            tk_g = sb("pair_gate", TOPK, group=g)
            tk_s = sb("pair_small", 4, group=g)
            ex = sb("expert_row_col", 4 * P, group=g)
            exg = sb("expert_gate", 2 * P, group=g)
        gates = sb("expert_gates", T * NKEYS)
        fin = gates[:, 0:KC * T]
        fin_sq = gates[:, KC * T:2 * KC * T]

        ps = ctx.enter_context(nc.psum_tensor("psum", [P, 8 * 512], F32))

        def bank(n, a=0, b=512, p0=0, p1=P):
            return ps[p0:p1, n * 512 + a:n * 512 + b]

        landed = [sem(f"tile_landed_{i}") for i in range(4)]
        hi_ready, split_ready, tile_used = sem("hi_ready"), sem("split_ready"), sem("tile_used")
        consts_ready, pool_chain = sem("consts_ready"), sem("pool_chain")
        vec_landed, x_landed, up_landed = sem("vec_landed"), sem("x_landed"), sem("up_landed")
        bias_landed = [sem("na_bias_landed_0"), sem("na_bias_landed_1")]
        ln_sum, ln_centered, ln_sq, ln_var, ln_std = (sem(n) for n in (
            "ln_sum", "ln_centered", "ln_squared", "ln_var", "ln_std"))
        ln_normed, ln_hi, ln_lo, ln_chain = (sem(n) for n in ("ln_normed", "ln_hi", "ln_lo", "ln_chain"))
        proj_taken = sem("proj_taken")
        na_qk, na_s_read, na_negmax, na_exp, na_rinv, na_probs = (sem(n) for n in (
            "na_qk", "na_scores_read", "na_negmax", "na_exp", "na_rinv", "na_probs"))
        na_pt_done, na_pt_copied, na_vt_done, na_v_copied, na_pv, na_hi, na_lo, na_chain = (
            sem(n) for n in ("na_pt_done", "na_pt_copied", "na_vt_done", "na_v_copied", "na_pv",
                             "na_hi", "na_lo", "na_chain"))
        la_done, z_done, gap_done, exp_done, decayed, kt_done, kt_copied = (sem(n) for n in (
            "gla_la_done", "gla_z_done", "gla_gap_done", "gla_exp_done", "gla_decayed",
            "gla_kt_done", "gla_kt_copied"))
        att_done, att_masked, vt_done, v_copied, gain_done, state_done, o_done = (sem(n) for n in (
            "gla_att_done", "gla_att_masked", "gla_vt_done", "gla_v_copied", "gla_gain_done",
            "gla_state_done", "gla_o_done"))
        rms_done, on_done, ot_done, gated, o_hi, o_lo, gla_act, gla_dve, sig_ready = (
            sem(n) for n in ("gla_rms_done", "gla_on_done", "gla_ot_done", "gla_gated", "gla_o_hi",
                             "gla_o_lo", "gla_act_chain", "gla_dve_chain", "gla_sig_ready"))
        sig_a, sig_b, a_gated, merged, m_hi, m_lo, m_chain = (sem(n) for n in (
            "merge_sig_a", "merge_sig_b", "merge_a_gated", "merge_sum_ready", "merge_hi", "merge_lo",
            "merge_chain"))
        res_done, res_chain = sem("residual_done"), sem("residual_chain")
        keys_landed, pq_taken, sc_done, sc_taken = (sem(n) for n in (
            "keys_landed", "peer_q_taken", "scores_done", "scores_taken"))
        p_landed, p_hi, p_lo, ple_taken, gsig, res2_done, res2_chain, res_spilled = (
            sem(n) for n in ("p_landed", "p_hi", "p_lo", "ple_taken", "ple_sig_ready",
                             "residual2_done", "residual2_chain", "residual_spilled"))
        tk_chain, tk_neg, tk_exp, ex_done, ex_t_done, ex_t_taken = (sem(n) for n in (
            "topk_chain", "topk_negmax", "topk_exp", "experts_done", "experts_turned",
            "experts_taken"))
        gelu_done = sem("gelu_done")
        gelu_stored = [sem(f"gelu_stored_{i}") for i in range(4)]
        hot_ready, gate_mm, gate_taken = sem("hot_ready"), sem("gate_spread"), sem("gate_taken")
        gelu_landed = [sem(f"gelu_landed_{i}") for i in range(4)]
        w_ready, w_hi, w_lo, y_used, y_done = (sem(n) for n in (
            "expert_weight_ready", "expert_weight_hi", "expert_weight_lo", "expert_weight_used",
            "y_done"))
        res_back, fin_added, out_ready, out_stored = (sem(n) for n in (
            "residual_back", "final_added", "out_ready", "out_stored"))

        block = ctx.enter_context(nc.Block())

        @block.sync
        def _(sp):
            def load(t, slot):
                wait(sp, tile_used, t.times(1, 1 - RING))
                src = stream[ds(t.times(1), 1)].rearrange("n p f -> (n p) f")
                sp.dma_start(w_in[:, slot * TILE:(slot + 1) * TILE], src).then_inc(landed[slot], 16)

            for s in range(4):
                load(Pos(s), s)
            with sp.Fori(0, T_END // 4 - 1) as i:
                for s in range(4):
                    load(Pos(4 + s, 4, i), s)
            for t in range(T_END // 4 * 4, T_END):
                load(Pos(t), t % 4)

        @block.gpsimd
        def _(pool):
            pool.dma_start(x_in[:], x_t).then_inc(x_landed, 16)
            pool.dma_start(vec[:], vectors).then_inc(vec_landed, 16)
            n = [0]

            def const(ins):
                n[0] += 1
                ins.then_inc(pool_chain, 1)
                pool.wait_ge(pool_chain, n[0])

            const(pool.memset(mean_w[:], 1.0 / D))
            const(pool.memset(eps_t[:], EPS))
            const(pool.memset(zeros[:], 0.0))
            const(pool.memset(ident[:], 0.0))
            const(pool.affine_select(out=ident[:], in_=ident[:], compare_op=ALU.not_equal, fill=1.0,
                                     base=0, pattern=[[-1, P]], channel_multiplier=1))
            const(pool.iota(iota_key[:], [[1, NKEYS]], base=0, channel_multiplier=0,
                            allow_small_or_imprecise_dtypes=True))
            const(pool.iota(iota_top[:], [[1, TOPK]], base=0, channel_multiplier=0,
                            allow_small_or_imprecise_dtypes=True))
            pool.engine_nop().then_inc(consts_ready, 1)

            def load_bias(s, slot):
                wait(pool, na_s_read, s.times(1, -1))
                src = rpb[ds(s.times(1), 1)].rearrange("n p f -> (n p) f")
                pool.dma_start(na_bias[:, slot * 4 * T:(slot + 1) * 4 * T], src).then_inc(
                    bias_landed[slot], 16)

            pool.wait_ge(ln_lo, 4)
            load_bias(Pos(0), 0)
            load_bias(Pos(1), 1)
            with pool.Fori(0, NA_PAIRS // 2 - 1) as i:
                load_bias(Pos(2, 2, i), 0)
                load_bias(Pos(3, 2, i), 1)

            pool.wait_ge(na_lo, NA_PAIRS)
            const(pool.memset(g_reset[:], 1.0))
            reset0 = g_reset[:].rearrange("p (n c) -> p n c", c=CHUNK)[:, :, 0:1]
            const(pool.memset(reset0, 0.0))
            const(pool.memset(g_maskf[:], 1.0))
            for half in range(2):
                m = g_maskf[64 * half:64 * half + 64, :].rearrange("p (a c) -> p a c", a=2)
                const(pool.affine_select(out=m, in_=m, compare_op=ALU.is_ge, fill=0.0, base=0,
                                         pattern=[[0, 2], [1, CHUNK]], channel_multiplier=-1))
            const(pool.tensor_copy(g_mask[:], g_maskf[:]))
            pool.engine_nop().then_inc(consts_ready, 1)

            def load_up(h):
                wait(pool, la_done, h.times(1))
                src = decay_up[ds(h.times(1), 1)].rearrange("n p f -> (n p) f")
                pool.dma_start(g_up[0:64, :], src).then_inc(up_landed, 16)

            load_up(Pos(0))
            with pool.Fori(0, GLA_HEADS - 1) as i:
                load_up(Pos(1, 1, i))

            pool.wait_ge(ln_lo, 8)
            pool.dma_start(key_t[:], keys).then_inc(keys_landed, 16)
            pool.dma_start(p_in[:], p_t).then_inc(p_landed, 16)
            pool.wait_ge(res2_done, KC)
            pool.dma_start(residual_dram, res[:]).then_inc(res_spilled, 16)

            def store_gelu(j, slot):
                pool.wait_ge(gelu_done, j.times(1, 1))
                dst = gelu_dram[ds(j.times(1), 1)].rearrange("n p f -> (n p) f")
                pool.dma_start(dst, gst[:, slot * T:(slot + 1) * T]).then_inc(gelu_stored[slot], 16)

            with pool.Fori(0, NKEYS // 4) as i:
                for s in range(4):
                    store_gelu(Pos(s, 4, i), s)
            for s in range(4):
                pool.wait_ge(gelu_stored[s], 16 * (NKEYS // 4))

            def load_gelu(j, slot):
                wait(pool, w_ready, j.times(1, -3))
                src = gelu_dram[ds(j.times(1), 1)].rearrange("n p f -> (n p) f")
                pool.dma_start(gst[:, slot * T:(slot + 1) * T], src).then_inc(gelu_landed[slot], 16)

            for s in range(4):
                load_gelu(Pos(s), s)
            with pool.Fori(0, NKEYS // 4 - 1) as i:
                for s in range(4):
                    load_gelu(Pos(4 + s, 4, i), s)
            pool.wait_ge(w_ready, NKEYS)
            pool.wait_ge(res_spilled, 16)
            pool.dma_start(fin, residual_dram).then_inc(res_back, 16)
            pool.wait_ge(out_ready, 4)
            pool.dma_start(out, fin).then_inc(out_stored, 16)
            pool.wait_ge(out_stored, 16)

        @block.tensor
        def _(pe):
            def norm_sums(n, r, sq):
                for c in range(KC):
                    mm = pe.matmul(bank(0, 0, T), mean_w[:], r[:, c * T:(c + 1) * T],
                                   start=c == 0, stop=c == KC - 1)
                mm.then_inc(ln_sum, 1)
                for c in range(KC):
                    if c % 4 == 0:
                        pe.wait_ge(ln_sq, 4 * n + c // 4 + 1)
                    mm = pe.matmul(bank(1, 0, T), mean_w[:], sq[:, c * T:(c + 1) * T],
                                   start=c == 0, stop=c == KC - 1)
                mm.then_inc(ln_var, 1)

            def products(t, slot, pieces, last_of=None):
                pe.wait_ge(split_ready, t.times(1, 1))
                base = slot % RING * TILE
                for dst, col, act, start, stop in pieces:
                    w_h = w_up[:, base + col * P:base + (col + 1) * P]
                    w_l = w_low[:, base + col * P:base + (col + 1) * P]
                    pe.matmul(dst, w_h, act[:, 0:T], start=start, stop=False, skip_group_check=True)
                    pe.matmul(dst, w_h, act[:, T:2 * T], start=False, stop=False,
                              skip_group_check=True)
                    mm = pe.matmul(dst, w_l, act[:, 0:T], start=False, stop=stop,
                                   skip_group_check=True)
                mm.then_inc(tile_used, 1)

            def chunk(acts, c):
                return acts[:, c * 2 * T:(c + 1) * 2 * T]

            def half_block(t, slot, dst, acts, first, last, k0=0):
                products(t, slot, [(dst, c, chunk(acts, k0 + c), first and c == 0, last and c == 7)
                                   for c in range(8)])

            def two_tiles(t, slot, dst, acts):
                half_block(t, slot, dst, acts, True, False)
                half_block(t + 1, slot + 1, dst, acts, False, True, k0=8)

            pe.wait_ge(x_landed, 16)
            pe.wait_ge(consts_ready, 1)
            norm_sums(0, x_in, sq_in)
            pe.wait_ge(ln_lo, 4)

            def na_block(s, k, t, slot, parity):
                wait(pe, proj_taken, s.times(3, k - 1))
                two_tiles(t, slot, bank((3 * parity + k) % 2, 0, T), xs)

            def qkv(parity, k):
                a = (parity * 3 + k) * T
                return na_qkv[:, a:a + T]

            def na_scores(s, parity):
                pe.wait_ge(proj_taken, s.times(3, 3))
                wait(pe, na_s_read, s.times(1))
                for e in range(2):
                    rows = slice(64 * e, 64 * e + 64)
                    for tq in range(2):
                        mm = pe.matmul(bank(2 + e, tq * T, (tq + 1) * T),
                                       qkv(parity, 0)[rows, tq * P:(tq + 1) * P],
                                       qkv(parity, 1)[rows, :], start=True, stop=True)
                mm.then_inc(na_qk, 1)
                wait(pe, na_v_copied, s.times(1))
                for tk in range(2):
                    mm = pe.transpose(bank(6, tk * P, (tk + 1) * P),
                                      qkv(parity, 2)[:, tk * P:(tk + 1) * P], ident[:])
                mm.then_inc(na_vt_done, 1)

            def na_turn(s):
                pe.wait_ge(na_probs, s.times(1, 1))
                wait(pe, na_pt_copied, s.times(2))
                for e in range(2):
                    for tk in range(2):
                        for tq in range(2):
                            a = (2 * e + tq) * T + tk * P
                            mm = pe.transpose(bank(4 + e, tk * T + tq * P, tk * T + (tq + 1) * P),
                                              na_s[:, a:a + P], ident[:])
                mm.then_inc(na_pt_done, 1)

            def na_values(s):
                pe.wait_ge(na_pt_copied, s.times(2, 2))
                pe.wait_ge(na_v_copied, s.times(1, 1))
                wait(pe, na_lo, s.times(1))
                for e in range(2):
                    for tk in range(2):
                        mm = pe.matmul(bank(7, 0, T, 64 * e, 64 * e + 64),
                                       na_v[:, tk * P + 64 * e:tk * P + 64 * e + 64],
                                       na_pt[:, (2 * e + tk) * T:(2 * e + tk + 1) * T],
                                       start=tk == 0, stop=tk == 1, skip_group_check=True)
                mm.then_inc(na_pv, 1)

            def na_step(s, slot, parity, prev2):
                t = Pos(s.const * 6, s.per * 6, s.i)
                if prev2:
                    na_values(s + -2)
                na_scores(s + -1, 1 - parity)
                na_block(s, 0, t, slot, parity)
                na_block(s, 1, t + 2, slot + 2, parity)
                na_turn(s + -1)
                na_block(s, 2, t + 4, slot + 4, parity)

            for k in range(3):
                na_block(Pos(0), k, Pos(2 * k), 2 * k, 0)
            na_step(Pos(1), 6, 1, False)
            na_step(Pos(2), 0, 0, True)
            na_step(Pos(3), 2, 1, True)
            with pe.Fori(0, (NA_PAIRS - 4) // 2) as i:
                na_step(Pos(4, 2, i), 0, 0, True)
                na_step(Pos(5, 2, i), 2, 1, True)

            def gla_block(b, t, slot, n):
                wait(pe, proj_taken, b.times(1, -1))
                two_tiles(t, slot, bank(n % 2, 0, T), xs)

            B0 = 3 * NA_PAIRS
            na_values(Pos(NA_PAIRS - 2))
            na_scores(Pos(NA_PAIRS - 1), 1)
            gla_block(Pos(B0), Pos(T_RANK), T_RANK, B0)
            gla_block(Pos(B0 + 1), Pos(T_GLA), T_GLA, B0 + 1)
            na_turn(Pos(NA_PAIRS - 1))
            gla_block(Pos(B0 + 2), Pos(T_GLA + 2), T_GLA + 2, B0 + 2)
            na_values(Pos(NA_PAIRS - 1))
            gla_block(Pos(B0 + 3), Pos(T_GLA + 4), T_GLA + 4, B0 + 3)
            gla_block(Pos(B0 + 4), Pos(T_GLA + 6), T_GLA + 6, B0 + 4)
            B1 = B0 + 5

            def decay_inputs(h):
                pe.wait_ge(up_landed, h.times(16, 16))
                pe.wait_ge(consts_ready, 2)
                pe.wait_ge(proj_taken, B0 + 1)
                for d in range(2):
                    for kb in range(NKB):
                        mm = pe.matmul(bank(2 + d, kb * T, (kb + 1) * T),
                                       g_up[32 * d:32 * d + 32, kb * P:(kb + 1) * P],
                                       g_rank[32 * d:32 * d + 32, :], start=True, stop=True)
                mm.then_inc(la_done, 1)

            def turn_outputs(h):
                pe.wait_ge(on_done, h.times(1, 1))
                if h.i is not None or h.const < GLA_HEADS - 1:
                    pe.wait_ge(z_done, h.times(1, 2))
                for vb in range(NVB):
                    for tt in range(2):
                        mm = pe.transpose(bank(2 + vb // 2, vb % 2 * T + tt * P, vb % 2 * T + (tt + 1) * P),
                                          g_on[:, tt * DV + vb * P:tt * DV + (vb + 1) * P], ident[:])
                mm.then_inc(ot_done, 1)

            def intra(h):
                pe.wait_ge(decayed, h.times(1, 1))
                wait(pe, gated, h.times(1))
                pe.wait_ge(z_done, h.times(1, 1))
                for d in range(2):
                    for tt in range(2):
                        for kb in range(NKB):
                            a = (d * NKB + kb) * T + tt * P
                            mm = pe.transpose(bank(2 + d, tt * DK + kb * P, tt * DK + (kb + 1) * P),
                                              g_ks[:, a:a + P], ident[:])
                mm.then_inc(kt_done, 1)
                for d in range(2):
                    for n in range(N_CHUNKS):
                        rows, tt = 64 * (n % 2), n // 2
                        dst = bank(4, (d * 2 + tt) * CHUNK, (d * 2 + tt + 1) * CHUNK, rows, rows + 64)
                        for kb in range(NKB):
                            a = (d * NKB + kb) * T + n * CHUNK
                            mm = pe.matmul(dst, g_ki[:, a:a + CHUNK], g_qd[:, a:a + CHUNK],
                                           start=kb == 0, stop=kb == NKB - 1, skip_group_check=True)
                mm.then_inc(att_done, 1)

            def turn_values(h, b):
                pe.wait_ge(proj_taken, b)
                pe.wait_ge(kt_copied, h.times(2, 2))
                for tt in range(2):
                    for vb in range(NVB):
                        mm = pe.transpose(bank(2 + tt, vb * P, (vb + 1) * P),
                                          g_vt[:, vb * T + tt * P:vb * T + (tt + 1) * P], ident[:])
                mm.then_inc(vt_done, 1)

            def recur(h, m):
                if m == 0:
                    pe.wait_ge(v_copied, h.times(2, 2))
                    pe.wait_ge(att_masked, h.times(1, 1))
                    wait(pe, on_done, h.times(1))
                    for tt in range(2):
                        pe.matmul(bank(6 + tt), zeros[:], zeros[:].unsqueeze(1).to_broadcast([P, 4, P]),
                                  start=True, stop=False, skip_group_check=True)
                    for n in range(N_CHUNKS):
                        r0, tt = 64 * (n % 2), n // 2
                        pe.matmul(bank(6 + tt, 0, DV, r0, r0 + 64),
                                  g_att[r0:r0 + 64, tt * CHUNK:(tt + 1) * CHUNK],
                                  g_v[r0:r0 + 64, tt * DV:(tt + 1) * DV],
                                  start=False, stop=False, skip_group_check=True)
                else:
                    pe.wait_ge(state_done, h.times(3, m))
                for d in range(2):
                    n = m if d == 0 else N_CHUNKS - 1 - m
                    r0, tt = 64 * (n % 2), n // 2
                    if m > 0:
                        for kb in range(NKB):
                            a = (d * NKB + kb) * T + n * CHUNK
                            mm = pe.matmul(bank(6 + tt, 0, DV, r0, r0 + 64), g_qd[:, a:a + CHUNK],
                                           g_state[:, (d * NKB + kb) * DV:(d * NKB + kb + 1) * DV],
                                           start=False, stop=False, skip_group_check=True)
                if m < N_CHUNKS - 1:
                    for d in range(2):
                        n = m if d == 0 else N_CHUNKS - 1 - m
                        r0, tt = 64 * (n % 2), n // 2
                        for kb in range(NKB):
                            a = (d * 2 + tt) * DK + kb * P
                            mm = pe.matmul(bank(2 + d * NKB + kb), g_kt[r0:r0 + 64, a:a + P],
                                           g_v[r0:r0 + 64, tt * DV:(tt + 1) * DV],
                                           start=True, stop=True, skip_group_check=True)
                    mm.then_inc(gain_done, 1)
                else:
                    mm.then_inc(o_done, 1)

            def gla_head(h, t, b, last, first):
                decay_inputs(h)
                for k in range(8 if last else 12):
                    if k == 2 and not first:
                        turn_outputs(h + -1)
                    if k == 4:
                        intra(h)
                    if k == 5:
                        turn_values(h, b.times(1, 4))
                    if k == 7:
                        recur(h, 0)
                    if k == 9:
                        recur(h, 1)
                    if k == 10:
                        recur(h, 2)
                    gla_block(b + k, t + 2 * k, T_GLA + QK_TILES + 2 * k, B1 + k)
                for m in ((1, 2, 3) if last else (3,)):
                    recur(h, m)

            gla_head(Pos(0), Pos(T_GLA + QK_TILES), Pos(B1), False, True)
            with pe.Fori(0, GLA_HEADS - 2) as i:
                gla_head(Pos(1, 1, i), Pos(T_GLA + QK_TILES + HEAD_TILES, HEAD_TILES, i),
                         Pos(B1 + 12, 12, i), False, False)
            H = GLA_HEADS - 1
            gla_head(Pos(H), Pos(T_GLA + QK_TILES + H * HEAD_TILES), Pos(B1 + 12 * H), True, False)
            turn_outputs(Pos(H))

            def merge_step(c, t, slot, parity):
                wait(pe, merged, c.times(1, -1))
                b = 4 * parity
                two_tiles(t, slot, bank(b, 0, T), xs)
                half_block(t + 2, slot + 2, bank(b + 1, 0, T), nas, True, True)
                two_tiles(t + 3, slot + 3, bank(b + 2, 0, T), xs)
                two_tiles(t + 5, slot + 5, bank(b + 3, 0, T), gls)

            pe.wait_ge(proj_taken, B1 + 12 * GLA_HEADS - 4)
            pe.wait_ge(o_lo, GLA_HEADS)
            for k in range(4):
                merge_step(Pos(k), Pos(T_MERGE + 7 * k), T_MERGE + 7 * k, k % 2)
            with pe.Fori(0, KC // 4 - 1) as i:
                for k in range(4):
                    merge_step(Pos(4 + k, 4, i), Pos(T_MERGE + 28 + 7 * k, 28, i), T_MERGE + 7 * k, k % 2)

            pe.wait_ge(m_lo, KC)

            def out_block(c, t, slot, parity):
                wait(pe, res_done, c.times(1, -1))
                two_tiles(t, slot, bank(parity, 0, T), ms)

            out_block(Pos(0), Pos(T_OUT), T_OUT, 0)
            out_block(Pos(1), Pos(T_OUT + 2), T_OUT + 2, 1)
            with pe.Fori(0, KC // 2 - 1) as i:
                out_block(Pos(2, 2, i), Pos(T_OUT + 4, 4, i), T_OUT, 0)
                out_block(Pos(3, 2, i), Pos(T_OUT + 6, 4, i), T_OUT + 2, 1)
            pe.wait_ge(res_done, KC)
            norm_sums(1, res, sq_a)
            pe.wait_ge(ln_lo, 8)

            pe.wait_ge(keys_landed, 16)

            def query_block(c, t, slot, parity):
                wait(pe, pq_taken, c.times(1, -1))
                two_tiles(t, slot, bank(parity, 0, T), xs)

            def key_scores(c, parity):
                pe.wait_ge(pq_taken, c.times(1, 1))
                wait(pe, sc_taken, c.times(1, -1))
                for tt in range(2):
                    a = parity * T + tt * P
                    mm = pe.matmul(bank(2 + parity, tt * NKEYS, (tt + 1) * NKEYS), pq[:, a:a + P],
                                   key_t[:, ds(c.times(NKEYS), NKEYS)], start=True, stop=True)
                mm.then_inc(sc_done, 1)

            query_block(Pos(0), Pos(T_PQ), T_PQ, 0)
            query_block(Pos(1), Pos(T_PQ + 2), T_PQ + 2, 1)
            key_scores(Pos(0), 0)

            def two_queries(c, t):
                query_block(c, t, T_PQ, 0)
                key_scores(c + -1, 1)
                query_block(c + 1, t + 2, T_PQ + 2, 1)
                key_scores(c, 0)

            two_queries(Pos(2), Pos(T_PQ + 4))
            with pe.Fori(0, KC // 2 - 2) as i:
                two_queries(Pos(4, 2, i), Pos(T_PQ + 8, 4, i))
            key_scores(Pos(KC - 1), 1)

            pe.wait_ge(p_lo, 1)
            pe.wait_ge(sc_taken, HP)
            for w in range(4):
                products(Pos(T_PLE + w), T_PLE + w,
                         [(bank(2 * w + b // 2, b % 2 * T, (b % 2 + 1) * T), 2 * b + k,
                           ys[:, k * 2 * T:(k + 1) * 2 * T], k == 0, k == 1)
                          for b in range(4) for k in range(2)])

            def ple_gate_block(c, t, slot, parity):
                if c.i is None:
                    pe.wait_ge(ple_taken, 8)
                else:
                    pe.wait_ge(gsig, c.times(1, -1))
                two_tiles(t, slot, bank(parity, 0, T), xs)

            ple_gate_block(Pos(0), Pos(T_PGATE), T_PGATE, 0)
            ple_gate_block(Pos(1), Pos(T_PGATE + 2), T_PGATE + 2, 1)
            with pe.Fori(0, KC // 2 - 1) as i:
                ple_gate_block(Pos(2, 2, i), Pos(T_PGATE + 4, 4, i), T_PGATE, 0)
                ple_gate_block(Pos(3, 2, i), Pos(T_PGATE + 6, 4, i), T_PGATE + 2, 1)

            pe.wait_ge(gsig, KC)

            def hidden(j, t, slot, n):
                wait(pe, gelu_done, j.times(1, -1))
                two_tiles(t, slot, bank(n % 2, 0, T), xs)

            for n in range(4):
                hidden(Pos(n), Pos(T_U + 2 * n), T_U + 2 * n, n)
            with pe.Fori(0, 15) as i:
                for n in range(4):
                    hidden(Pos(4 + n, 4, i), Pos(T_U + 8 + 2 * n, 8, i), T_U + 2 * n, n)
            pe.wait_ge(ex_done, 16)
            for tt in range(2):
                for k, src in enumerate((ex[:, 0:2 * P], ex[:, 2 * P:4 * P], exg)):
                    mm = pe.transpose(bank(2 + k // 2, k % 2 * T + tt * P, k % 2 * T + (tt + 1) * P),
                                      src[:, tt * P:(tt + 1) * P], ident[:])
            mm.then_inc(ex_t_done, 1)

            def spread_gates(g, n):
                pe.wait_ge(hot_ready, g.times(8, 8))
                wait(pe, gate_taken, g.times(1, -1))
                for q in range(4):
                    mm = pe.matmul(bank(2 + n % 2, q * NKEYS, (q + 1) * NKEYS),
                                   hot0[:, q * NKEYS:(q + 1) * NKEYS], hot1[:, q * NKEYS:(q + 1) * NKEYS],
                                   start=True, stop=True)
                mm.then_inc(gate_mm, 1)

            pe.wait_ge(ex_t_taken, 3)
            for n in range(4):
                hidden(Pos(64 + n), Pos(T_U + 128 + 2 * n), T_U + 2 * n, n)
                spread_gates(Pos(n), n)
            with pe.Fori(0, 15) as i:
                for n in range(4):
                    hidden(Pos(68 + n, 4, i), Pos(T_U + 136 + 2 * n, 8, i), T_U + 2 * n, n)
                    spread_gates(Pos(4 + n, 4, i), n)

            pe.wait_ge(gelu_done, NKEYS)
            pe.wait_ge(gate_taken, T // 4)
            for n in range(8):
                pe.matmul(bank(n), zeros[:], zeros[:].unsqueeze(1).to_broadcast([P, 4, P]),
                          start=True, stop=False, skip_group_check=True)

            def expert_out(j, t, slot, parity):
                pe.wait_ge(w_lo, j.times(1, 1))
                act = ys[:, parity * 2 * T:(parity + 1) * 2 * T]
                for half in range(2):
                    products(t + half, slot + half,
                             [(ps[:, (8 * half + c) * T:(8 * half + c + 1) * T], c, act, False, False)
                              for c in range(8)])

            with pe.Fori(0, NKEYS // 2) as i:
                expert_out(Pos(0, 2, i), Pos(T_V, 4, i), T_V, 0)
                expert_out(Pos(1, 2, i), Pos(T_V + 2, 4, i), T_V + 2, 1)

            pe.wait_ge(fin_added, 8)
            norm_sums(2, fin, fin_sq)

        @block.scalar
        def _(act):
            def upper(t, slot):
                act.wait_ge(landed[slot % RING], t.over(RING).times(16, 16))
                s = slice(slot % RING * TILE, (slot % RING + 1) * TILE)
                act.activation(w_up[:, s], w_in[:, s], ACT.Copy).then_inc(hi_ready, 1)

            def hi(t, slot):
                if t.i is not None or t.const + AHEAD < T_END:
                    upper(t + AHEAD, slot + AHEAD)

            def norm_act(n, r, sq, split):
                for g in range(4):
                    a, b = g * 4 * T, (g + 1) * 4 * T
                    act.wait_ge(ln_centered, 4 * n + g + 1)
                    act.activation(sq[:, a:b], r[:, a:b], ACT.Square).then_inc(ln_sq, 1)
                act.wait_ge(ln_var, n + 1)
                act.activation(sq[:, 0:T], bank(1, 0, T), ACT.Sqrt, bias=eps_t[:]).then_inc(ln_std, 1)
                if split:
                    for g in range(4):
                        act.wait_ge(ln_normed, 4 * n + g + 1)
                        dst = xs[:, g * 8 * T:(g + 1) * 8 * T].rearrange(
                            "p (c s t) -> p c s t", c=4, s=2)[:, :, 0, :]
                        src = r[:, g * 4 * T:(g + 1) * 4 * T].rearrange("p (c t) -> p c t", c=4)
                        act.activation(dst, src, ACT.Copy).then_inc(ln_hi, 1)

            act.wait_ge(consts_ready, 1)
            for k in range(AHEAD):
                upper(Pos(k), k)
            hi(Pos(0), 0)
            hi(Pos(1), 1)
            norm_act(0, x_in, sq_in, True)

            act.wait_ge(vec_landed, 16)

            def na_take(s, k, t, parity):
                act.wait_ge(tile_used, t.times(1, 2))
                if k == 0:
                    wait(act, na_pv, s.times(1, -1))
                    if s.i is None and s.const < 2:
                        act.wait_ge(ln_lo, 4)
                a = (parity * 3 + k) * T
                act.activation(na_qkv[:, a:a + T], bank((3 * parity + k) % 2, 0, T), ACT.Identity,
                               bias=vec[:, ds(s.times(3, V_NA + k), 1)]).then_inc(proj_taken, 1)

            def na_exps(s):
                act.wait_ge(na_negmax, s.times(1, 1))
                for k in range(4):
                    act.activation(na_s[:, k * T:(k + 1) * T], na_s[:, k * T:(k + 1) * T], ACT.Exp,
                                   bias=na_small[:, 4 + k:5 + k],
                                   accum_out=na_small[:, 8 + k:9 + k]).then_inc(na_exp, 1)
                act.wait_ge(na_vt_done, s.times(1, 1))
                wait(act, na_pv, s.times(1))
                act.activation(na_v[:], bank(6, 0, 2 * P), ACT.Copy).then_inc(na_v_copied, 1)

            def na_norm(s):
                act.wait_ge(na_rinv, s.times(1, 1))
                act.wait_ge(na_exp, s.times(4, 4))
                for k in range(4):
                    ins = act.activation(na_s[:, k * T:(k + 1) * T], na_s[:, k * T:(k + 1) * T],
                                         ACT.Copy, scale=na_small[:, 12 + k:13 + k])
                ins.then_inc(na_probs, 1)

            def na_out(s):
                act.wait_ge(na_pv, s.times(1, 1))
                act.activation(nas[:, ds(s.times(2 * T), T)], bank(7, 0, T), ACT.Copy).then_inc(na_hi, 1)

            def na_step(s, slot, parity, prev2):
                t = Pos(s.const * 6, s.per * 6, s.i)
                hi(t, slot)
                na_take(s + -1, 2, t + -2, 1 - parity)
                if prev2:
                    na_out(s + -2)
                hi(t + 1, slot + 1)
                na_exps(s + -1)
                hi(t + 2, slot + 2)
                na_take(s, 0, t, parity)
                hi(t + 3, slot + 3)
                na_norm(s + -1)
                hi(t + 4, slot + 4)
                na_take(s, 1, t + 2, parity)
                hi(t + 5, slot + 5)

            hi(Pos(2), 2)
            na_take(Pos(0), 0, Pos(0), 0)
            hi(Pos(3), 3)
            hi(Pos(4), 4)
            na_take(Pos(0), 1, Pos(2), 0)
            hi(Pos(5), 5)
            na_step(Pos(1), 6, 1, False)
            with act.Fori(0, (NA_PAIRS - 2) // 2) as i:
                na_step(Pos(2, 2, i), 0, 0, True)
                na_step(Pos(3, 2, i), 2, 1, True)

            B0 = 3 * NA_PAIRS
            B1 = B0 + 5
            chain = Chain(act, gla_act, 6)

            def take(dst, n, t, col):
                act.wait_ge(tile_used, t.times(1, 2))
                act.activation(dst, bank(n % 2, 0, T), ACT.Identity,
                               bias=vec[:, ds(col.times(1), 1)]).then_inc(proj_taken, 1)

            def take_gate(vb, n, t, col):
                act.wait_ge(tile_used, t.times(1, 2))
                a, b = vb * T, (vb + 1) * T
                act.activation(g_x[:, a:b], bank(n % 2, 0, T), ACT.Identity,
                               bias=vec[:, ds(col.times(1), 1)])
                act.activation(g_sg[:, a:b], bank(n % 2, 0, T), ACT.Sigmoid,
                               bias=vec[:, ds(col.times(1), 1)]).then_inc(proj_taken, 1)

            def decay_logs(h):
                chain.begin(h)
                act.wait_ge(la_done, h.times(1, 1))
                for k in range(4):
                    chain.step(act.activation(g_z[:, k * T:(k + 1) * T],
                                              bank(2 + k // 2, k % 2 * T, (k % 2 + 1) * T), ACT.Identity,
                                              bias=vec[:, ds(h.times(4, V_DECAY + k), 1)]))
                chain.step(act.activation(g_a[:], g_z[:], ACT.Abs))
                chain.step(act.activation(g_a[:], g_a[:], ACT.Exp, scale=-1.0))
                act.activation(g_a[:], g_a[:], ACT.Ln, bias=1.0).then_inc(z_done, 1)
                chain.end()

            def decay_exps(h):
                act.wait_ge(gap_done, h.times(1, 1))
                wait(act, o_done, h.times(1))
                act.activation(g_qd[:], g_c[:], ACT.Exp, scale=1.0 / 16)
                act.activation(g_ki[:], g_c[:], ACT.Exp, scale=-1.0 / 16)
                act.activation(g_ks[:], g_a[:], ACT.Exp, scale=1.0 / 16)
                c = g_c[:].rearrange("p (d k c) -> p d k c", d=2, c=CHUNK)
                dec = g_dec[:].rearrange("p (d k c) -> p d k c", d=2, c=1)
                act.activation(dec[:, 0], c[:, 0, :, CHUNK - 1:CHUNK], ACT.Exp, scale=1.0 / 16)
                act.activation(dec[:, 1], c[:, 1, :, 0:1], ACT.Exp, scale=1.0 / 16).then_inc(exp_done, 1)

            def keys_taken(h):
                act.wait_ge(kt_done, h.times(1, 1))
                for d in range(2):
                    act.activation(g_kt[:, d * 2 * DK:(d + 1) * 2 * DK], bank(2 + d),
                                   ACT.Copy).then_inc(kt_copied, 1)

            def values_taken(h):
                act.wait_ge(vt_done, h.times(1, 1))
                for tt in range(2):
                    act.activation(g_v[:, tt * DV:(tt + 1) * DV], bank(2 + tt), ACT.Copy).then_inc(v_copied, 1)

            def out_rms(h):
                act.wait_ge(o_done, h.times(1, 1))
                for tt in range(2):
                    ins = act.activation(g_on[:, tt * DV:(tt + 1) * DV], bank(6 + tt), ACT.Square,
                                         accum_out=g_small[:, tt:tt + 1])
                ins.then_inc(rms_done, 1)
                act.wait_ge(rms_done, h.times(2, 1))
                act.activation(g_small[:, 2:4], g_small[:, 0:2], ACT.Sqrt, bias=eps_t[:],
                               scale=1.0 / DV).then_inc(rms_done, 1)

            def out_hi(h):
                act.wait_ge(gated, h.times(1, 1))
                dst = gls[:, ds(h.times(NVB * 2 * T), NVB * 2 * T)].rearrange(
                    "p (c s t) -> p c s t", c=NVB, s=2)[:, :, 0, :]
                act.activation(dst, g_ot[:].rearrange("p (c t) -> p c t", c=NVB), ACT.Copy).then_inc(o_hi, 1)

            NL = NA_PAIRS - 1
            hi(Pos(T_RANK), T_RANK)
            na_take(Pos(NL), 2, Pos(T_RANK - 2), NL % 2)
            na_out(Pos(NL - 1))
            hi(Pos(T_RANK + 1), T_RANK + 1)
            na_exps(Pos(NL))
            hi(Pos(T_RANK + 2), T_RANK + 2)
            na_norm(Pos(NL))
            hi(Pos(T_RANK + 3), T_RANK + 3)

            def gla_take(h, k, n, t):
                col = Pos(V_GLA + k + GLA_BLOCKS * h.const, GLA_BLOCKS * h.per, h.i)
                if k < 2:
                    take(g_q[:, k * T:(k + 1) * T], n, t, col)
                elif k < 4:
                    take(g_k[:, (k - 2) * T:(k - 1) * T], n, t, col)
                elif k < 8:
                    take(g_vt[:, (k - 4) * T:(k - 3) * T], n, t, col)
                else:
                    take_gate(k - 8, n, t, col)

            take(g_rank[:], B0, Pos(T_RANK), Pos(V_RANK))
            hi(Pos(T_GLA + 2), T_GLA + 2)
            gla_take(Pos(0), 0, B0 + 1, Pos(T_GLA))
            hi(Pos(T_GLA + 3), T_GLA + 3)
            hi(Pos(T_GLA + 4), T_GLA + 4)
            gla_take(Pos(0), 1, B0 + 2, Pos(T_GLA + 2))
            na_out(Pos(NL))
            hi(Pos(T_GLA + 5), T_GLA + 5)
            hi(Pos(T_GLA + 6), T_GLA + 6)
            gla_take(Pos(0), 2, B0 + 3, Pos(T_GLA + 4))
            hi(Pos(T_GLA + 7), T_GLA + 7)

            def gla_head(h, t, last, first):
                s0 = T_GLA + QK_TILES
                for k in range(8 if last else 12):
                    if k == 6:
                        values_taken(h)
                    hi(t + 2 * k, s0 + 2 * k)
                    if k == 0:
                        gla_take(h, 3, B1 - 1, t + -2)
                    elif k <= 8:
                        gla_take(h, 3 + k, B1 + k - 1, t + 2 * (k - 1))
                    else:
                        gla_take(h + 1, k - 9, B1 + k - 1, t + 2 * (k - 1))
                    hi(t + 2 * k + 1, s0 + 2 * k + 1)
                    if k == 0:
                        if not first:
                            out_rms(h + -1)
                        decay_logs(h)
                    if k == 2:
                        decay_exps(h)
                    if k == 3 and not first:
                        out_hi(h + -1)
                    if k == 4:
                        keys_taken(h)

            s_h = T_GLA + QK_TILES
            gla_head(Pos(0), Pos(s_h), False, True)
            with act.Fori(0, GLA_HEADS - 2) as i:
                gla_head(Pos(1, 1, i), Pos(s_h + HEAD_TILES, HEAD_TILES, i), False, False)
            H = GLA_HEADS - 1
            gla_head(Pos(H), Pos(s_h + H * HEAD_TILES), True, False)
            hi(Pos(T_MERGE), T_MERGE)
            gla_take(Pos(H), 11, B1 + 7, Pos(T_MERGE - 2))
            hi(Pos(T_MERGE + 1), T_MERGE + 1)
            out_rms(Pos(H))
            out_hi(Pos(H))

            def sigmoid(dst, parity, n, t, col, done, c, freed):
                act.wait_ge(tile_used, t.times(1, 2))
                wait(act, freed, c.times(1, -1))
                act.activation(dst[:, parity * T:(parity + 1) * T], bank(4 * parity + n, 0, T),
                               ACT.Sigmoid, bias=vec[:, ds(col.times(1), 1)]).then_inc(done, 1)

            def merged_hi(c, parity):
                act.wait_ge(merged, c.times(1, 1))
                act.activation(ms[:, ds(c.times(2 * T), T)], m_m[:, parity * T:(parity + 1) * T],
                               ACT.Copy).then_inc(m_hi, 1)

            def merge_step(c, t, slot, parity, prev, ahead=0):
                for k in range(ahead, MERGE_TILES):
                    hi(t + k, slot + k)
                    if k == 3:
                        sigmoid(m_sa, parity, 0, t, Pos(V_GATES + 2 * c.const, 2 * c.per, c.i),
                                sig_a, c, a_gated)
                        if prev:
                            merged_hi(c + -1, 1 - parity)
                    if k == 6:
                        sigmoid(m_sb, parity, 2, t + 3, Pos(V_GATES + 1 + 2 * c.const, 2 * c.per, c.i),
                                sig_b, c, merged)

            for k in range(4):
                merge_step(Pos(k), Pos(T_MERGE + 7 * k), T_MERGE + 7 * k, k % 2, k > 0, 0 if k else 2)
            with act.Fori(0, KC // 4 - 1) as i:
                for k in range(4):
                    merge_step(Pos(4 + k, 4, i), Pos(T_MERGE + 28 + 7 * k, 28, i), T_MERGE + 7 * k,
                               k % 2, True)
            hi(Pos(T_OUT), T_OUT)
            hi(Pos(T_OUT + 1), T_OUT + 1)
            merged_hi(Pos(KC - 1), 1)

            hi(Pos(T_OUT + 2), T_OUT + 2)
            hi(Pos(T_OUT + 3), T_OUT + 3)
            with act.Fori(0, KC // 2 - 1) as i:
                for k in range(4):
                    hi(Pos(T_OUT + 4 + k, 4, i), T_OUT + k)
            hi(Pos(T_PQ), T_PQ)
            hi(Pos(T_PQ + 1), T_PQ + 1)
            norm_act(1, res, sq_a, True)

            def take_query(c, t, parity):
                act.wait_ge(tile_used, t.times(1, 2))
                wait(act, sc_done, c.times(1, -1))
                act.activation(pq[:, parity * T:(parity + 1) * T], bank(parity, 0, T),
                               ACT.Copy).then_inc(pq_taken, 1)

            def take_scores(c, parity):
                act.wait_ge(sc_done, c.times(1, 1))
                for tt in range(2):
                    ins = act.activation(sc[:, ds(c.times(NKEYS, tt * HP * NKEYS), NKEYS)],
                                         bank(2 + parity, tt * NKEYS, (tt + 1) * NKEYS), ACT.Copy)
                ins.then_inc(sc_taken, 1)

            hi(Pos(T_PQ + 2), T_PQ + 2)
            take_query(Pos(0), Pos(T_PQ), 0)
            hi(Pos(T_PQ + 3), T_PQ + 3)

            def two_queries(c, t):
                hi(t + 2, T_PQ)
                take_query(c, t, 1)
                take_scores(c + -1, 0)
                hi(t + 3, T_PQ + 1)
                hi(t + 4, T_PQ + 2)
                take_query(c + 1, t + 2, 0)
                take_scores(c, 1)
                hi(t + 5, T_PQ + 3)

            two_queries(Pos(1), Pos(T_PQ + 2))
            with act.Fori(0, KC // 2 - 2) as i:
                two_queries(Pos(3, 2, i), Pos(T_PQ + 6, 4, i))
            hi(Pos(T_PLE), T_PLE)
            take_query(Pos(KC - 1), Pos(T_PQ + 30), 1)
            take_scores(Pos(KC - 2), 0)
            take_scores(Pos(KC - 1), 1)

            act.wait_ge(p_landed, 16)
            p_dst = ys[:].rearrange("p (c s t) -> p c s t", c=2, s=2)[:, :, 0, :]
            act.activation(p_dst, p_in[:].rearrange("p (c t) -> p c t", c=2), ACT.Copy).then_inc(p_hi, 1)
            for k in range(1, 4):
                hi(Pos(T_PLE + k), T_PLE + k)
            for n in range(8):
                act.wait_ge(tile_used, T_PLE + n // 2 + 1)
                act.activation(ple[:, n * 512:(n + 1) * 512], bank(n), ACT.Copy).then_inc(ple_taken, 1)
                if n == 3:
                    hi(Pos(T_PGATE), T_PGATE)
                if n == 5:
                    hi(Pos(T_PGATE + 1), T_PGATE + 1)

            def take_ple_gate(c, t, parity):
                act.wait_ge(tile_used, t.times(1, 2))
                wait(act, res2_done, c.times(1, -1))
                act.activation(sgm[:, parity * T:(parity + 1) * T], bank(parity, 0, T),
                               ACT.Sigmoid).then_inc(gsig, 1)

            hi(Pos(T_PGATE + 2), T_PGATE + 2)
            take_ple_gate(Pos(0), Pos(T_PGATE), 0)
            hi(Pos(T_PGATE + 3), T_PGATE + 3)

            def two_ple_gates(c, t):
                hi(t + 2, T_PGATE)
                take_ple_gate(c, t, 1)
                hi(t + 3, T_PGATE + 1)
                hi(t + 4, T_PGATE + 2)
                take_ple_gate(c + 1, t + 2, 0)
                hi(t + 5, T_PGATE + 3)

            two_ple_gates(Pos(1), Pos(T_PGATE + 2))
            with act.Fori(0, KC // 2 - 2) as i:
                two_ple_gates(Pos(3, 2, i), Pos(T_PGATE + 6, 4, i))
            take_ple_gate(Pos(KC - 1), Pos(T_PGATE + 30), 1)

            def gelu(j, t, n):
                act.wait_ge(tile_used, t.times(1, 2))
                wait(act, gelu_stored[n], j.over(4).times(16))
                act.activation(gst[:, n * T:(n + 1) * T], bank(n % 2, 0, T), ACT.Gelu).then_inc(gelu_done, 1)

            def gate_exp(u):
                act.wait_ge(tk_neg, u.times(1, 1))
                act.activation(tk_g[:], tk_cv[:], ACT.Exp, bias=tk_s[:, 0:1],
                               accum_out=tk_s[:, 1:2]).then_inc(tk_exp, 1)

            def take_gates(g, n):
                act.wait_ge(gate_mm, g.times(1, 1))
                act.activation(gates[:, ds(g.times(4 * NKEYS), 4 * NKEYS)], bank(2 + n % 2),
                               ACT.Copy).then_inc(gate_taken, 1)

            def hidden_steps(j, t, first, unit=None, group=None):
                for n in range(4):
                    hi(t + 2 * n, T_U + 2 * n)
                    if n > 0 or not first:
                        gelu(j + (n - 1), t + (2 * n - 2), (n - 1) % 4)
                    if group is not None and (n > 0 or not first):
                        take_gates(group + (n - 1), (n - 1) % 4)
                    hi(t + 2 * n + 1, T_U + 2 * n + 1)
                    if unit is not None and n == 3:
                        gate_exp(unit)

            hidden_steps(Pos(0), Pos(T_U), True, unit=Pos(0))
            hidden_steps(Pos(4), Pos(T_U + 8), False, unit=Pos(1))
            with act.Fori(0, 14) as i:
                hidden_steps(Pos(8, 4, i), Pos(T_U + 16, 8, i), False, unit=Pos(2, 1, i))
            hi(Pos(T_U + 128), T_U)
            gelu(Pos(63), Pos(T_U + 126), 3)
            act.wait_ge(ex_t_done, 1)
            for k, dst in enumerate((idx0_t, idx1_t, gate_t)):
                act.activation(dst[:], bank(2 + k // 2, k % 2 * T, (k % 2 + 1) * T),
                               ACT.Copy).then_inc(ex_t_taken, 1)
            hi(Pos(T_U + 129), T_U + 1)
            for n in range(1, 4):
                hi(Pos(T_U + 128 + 2 * n), T_U + 2 * n)
                gelu(Pos(63 + n), Pos(T_U + 126 + 2 * n), n - 1)
                if n == 1:
                    act.wait_ge(res_spilled, 16)
                take_gates(Pos(n - 1), n - 1)
                hi(Pos(T_U + 129 + 2 * n), T_U + 2 * n + 1)
            with act.Fori(0, 15) as i:
                hidden_steps(Pos(68, 4, i), Pos(T_U + 136, 8, i), False, group=Pos(4, 4, i))
            hi(Pos(T_V), T_V)
            gelu(Pos(127), Pos(T_U + 254), 3)
            take_gates(Pos(63), 3)
            hi(Pos(T_V + 1), T_V + 1)

            def weight_hi(j, parity):
                act.wait_ge(w_ready, j.times(1, 1))
                if j.i is not None or j.const >= 2:
                    act.wait_ge(tile_used, j.times(2, T_V - 2))
                act.activation(ys[:, parity * 2 * T:parity * 2 * T + T],
                               wexp[:, parity * T:(parity + 1) * T], ACT.Copy).then_inc(w_hi, 1)

            weight_hi(Pos(0), 0)
            weight_hi(Pos(1), 1)
            for k in range(2 + AHEAD, 4):
                upper(Pos(T_V + k), T_V + k)
            with act.Fori(0, NKEYS // 2 - 1) as i:
                for k in range(2):
                    upper(Pos(T_V + 4 + 2 * k, 4, i), T_V + 2 * k)
                    weight_hi(Pos(2 + k, 2, i), k)
                    upper(Pos(T_V + 5 + 2 * k, 4, i), T_V + 2 * k + 1)
            norm_act(2, fin, fin_sq, False)

        @block.vector
        def _(dve):
            def lower(t, slot):
                dve.wait_ge(hi_ready, t.times(1, 1))
                s = slice(slot % RING * TILE, (slot % RING + 1) * TILE)
                dve.tensor_tensor(w_low[:, s], w_in[:, s], w_up[:, s].bitcast(F32),
                                  ALU.subtract).then_inc(split_ready, 1)

            def lo(t, slot):
                if t.i is not None or t.const + AHEAD < T_END:
                    lower(t + AHEAD, slot + AHEAD)

            def over_chunks(row, n):
                return row.unsqueeze(1).to_broadcast([P, n, T])

            ln_c = Chain(dve, ln_chain, 5)

            def norm_dve(n, r, sq, gain, split):
                ln_c.begin(Pos(n))
                dve.wait_ge(ln_sum, n + 1)
                for g in range(4):
                    v = r[:, g * 4 * T:(g + 1) * 4 * T].rearrange("p (c t) -> p c t", c=4)
                    dve.tensor_tensor(v, v, over_chunks(bank(0, 0, T), 4), ALU.subtract).then_inc(ln_centered, 1)
                dve.wait_ge(ln_std, n + 1)
                ln_c.step(dve.reciprocal(sq[:, T:2 * T], sq[:, 0:T]))
                dve.wait_ge(ln_centered, 4 * n + 4)
                for g in range(4):
                    v = r[:, g * 4 * T:(g + 1) * 4 * T].rearrange("p (c t) -> p c t", c=4)
                    ln_c.step(dve.tensor_tensor(v, v, over_chunks(sq[:, T:2 * T], 4), ALU.mult))
                    for c in range(4 * g, 4 * g + 4):
                        v1 = r[:, c * T:(c + 1) * T]
                        ins = dve.tensor_scalar(v1, v1, vec[:, gain + c:gain + c + 1],
                                                vec[:, gain + KC + c:gain + KC + c + 1], ALU.mult, ALU.add)
                    ins.then_inc(ln_normed if split else out_ready, 1)
                ln_c.end()
                if split:
                    for g in range(4):
                        dve.wait_ge(ln_hi, 4 * n + g + 1)
                        dve.wait_ge(ln_normed, 4 * n + g + 1)
                        d = xs[:, g * 8 * T:(g + 1) * 8 * T].rearrange("p (c s t) -> p c s t", c=4, s=2)
                        v = r[:, g * 4 * T:(g + 1) * 4 * T].rearrange("p (c t) -> p c t", c=4)
                        dve.tensor_tensor(d[:, :, 1, :], v, d[:, :, 0, :].bitcast(F32),
                                          ALU.subtract).then_inc(ln_lo, 1)

            dve.wait_ge(consts_ready, 1)
            dve.wait_ge(x_landed, 16)
            dve.wait_ge(vec_landed, 16)
            for k in range(AHEAD):
                lower(Pos(k), k)
            lo(Pos(0), 0)
            lo(Pos(1), 1)
            norm_dve(0, x_in, sq_in, V_LN, True)

            na_c = Chain(dve, na_chain, 1)

            def na_softmax(s, parity):
                na_c.begin(s)
                dve.wait_ge(na_qk, s.times(1, 1))
                dve.wait_ge(bias_landed[parity], s.over(2).times(16, 16) if s.i is not None
                            else 16 * (s.const // 2 + 1))
                wait(dve, na_pt_done, s.times(1))
                for e in range(2):
                    a, b = e * 2 * T, (e + 1) * 2 * T
                    ins = dve.scalar_tensor_tensor(out=na_s[:, a:b], in0=bank(2 + e), scalar=NA_DIM ** -0.5,
                                                   in1=na_bias[:, parity * 4 * T + a:parity * 4 * T + b],
                                                   op0=ALU.mult, op1=ALU.add)
                ins.then_inc(na_s_read, 1)
                dve.wait_ge(na_s_read, s.times(1, 1))
                na_c.step(dve.tensor_reduce(na_small[:, 0:4], na_s[:].rearrange("p (k t) -> p k t", k=4),
                                            AX.X, ALU.max))
                dve.tensor_scalar(na_small[:, 4:8], na_small[:, 0:4], -1.0, None, ALU.mult).then_inc(na_negmax, 1)
                na_c.end()

            def na_recip(s):
                dve.wait_ge(na_exp, s.times(4, 4))
                dve.reciprocal(na_small[:, 12:16], na_small[:, 8:12]).then_inc(na_rinv, 1)

            def na_take_turned(s):
                dve.wait_ge(na_pt_done, s.times(1, 1))
                wait(dve, na_pv, s.times(1))
                for e in range(2):
                    dve.tensor_copy(na_pt[:, e * 2 * T:(e + 1) * 2 * T], bank(4 + e)).then_inc(na_pt_copied, 1)

            def na_out_lo(s):
                dve.wait_ge(na_hi, s.times(1, 1))
                dve.tensor_tensor(nas[:, ds(s.times(2 * T, T), T)], bank(7, 0, T),
                                  nas[:, ds(s.times(2 * T), T)].bitcast(F32), ALU.subtract).then_inc(na_lo, 1)

            def na_step(s, slot, parity, prev2):
                t = Pos(s.const * 6, s.per * 6, s.i)
                lo(t, slot)
                if prev2:
                    na_out_lo(s + -2)
                na_softmax(s + -1, 1 - parity)
                lo(t + 1, slot + 1)
                lo(t + 2, slot + 2)
                na_recip(s + -1)
                lo(t + 3, slot + 3)
                lo(t + 4, slot + 4)
                lo(t + 5, slot + 5)
                na_take_turned(s + -1)

            for k in range(2, 6):
                lo(Pos(k), k)
            na_step(Pos(1), 6, 1, False)
            with dve.Fori(0, (NA_PAIRS - 2) // 2) as i:
                na_step(Pos(2, 2, i), 0, 0, True)
                na_step(Pos(3, 2, i), 2, 1, True)
            NL = NA_PAIRS - 1
            lo(Pos(T_RANK), T_RANK)
            na_out_lo(Pos(NL - 1))
            na_softmax(Pos(NL), NL % 2)
            lo(Pos(T_RANK + 1), T_RANK + 1)
            lo(Pos(T_RANK + 2), T_RANK + 2)
            na_recip(Pos(NL))
            lo(Pos(T_RANK + 3), T_RANK + 3)
            na_take_turned(Pos(NL))
            lo(Pos(T_RANK + 4), T_RANK + 4)
            lo(Pos(T_RANK + 5), T_RANK + 5)
            lo(Pos(T_RANK + 6), T_RANK + 6)
            na_out_lo(Pos(NL))
            for k in range(7, 10):
                lo(Pos(T_RANK + k), T_RANK + k)

            gc = Chain(dve, gla_dve, 4)
            gd = {}

            def cumulate(h):
                gc.begin(h)
                dve.wait_ge(z_done, h.times(1, 1))
                dve.wait_ge(consts_ready, 2)
                gc.step(dve.scalar_tensor_tensor(out=g_z[:], in0=g_z[:], scalar=0.0, in1=g_a[:],
                                                 op0=ALU.min, op1=ALU.subtract))
                gc.step(dve.tensor_tensor_scan(g_c[:, 0:2 * T], g_reset[:], g_z[:, 0:2 * T], 0.0,
                                               ALU.mult, ALU.add))
                back = g_c[:, 2 * T:4 * T]
                gc.step(dve.tensor_tensor_scan(back[:, ::-1], g_reset[:], g_z[:, 2 * T:4 * T][:, ::-1], 0.0,
                                               ALU.mult, ALU.add))
                for d in range(2):
                    c = g_c[:, d * 2 * T:(d + 1) * 2 * T].rearrange("p (k c) -> p k c", c=CHUNK)
                    a = g_a[:, d * 2 * T:(d + 1) * 2 * T].rearrange("p (k c) -> p k c", c=CHUNK)
                    whole = c[:, :, CHUNK - 1:CHUNK] if d == 0 else c[:, :, 0:1]
                    ins = dve.tensor_tensor(a, whole.to_broadcast([P, 2 * N_CHUNKS, CHUNK]), c, ALU.subtract)
                    if d == 0:
                        gc.step(ins)
                ins.then_inc(gap_done, 1)
                gc.end()

            def decay(h):
                dve.wait_ge(exp_done, h.times(1, 1))
                def both(x):
                    return x[:].unsqueeze(1).to_broadcast([P, 2, 2 * T])

                def dirs(x):
                    return x[:].rearrange("p (d k) -> p d k", d=2)

                dve.scalar_tensor_tensor(out=dirs(g_qd), in0=both(g_q), scalar=DK ** -0.5, in1=dirs(g_qd),
                                         op0=ALU.mult, op1=ALU.mult)
                dve.tensor_tensor(dirs(g_ki), both(g_k), dirs(g_ki), ALU.mult)
                dve.tensor_tensor(dirs(g_ks), both(g_k), dirs(g_ks), ALU.mult).then_inc(decayed, 1)

            at = Chain(dve, sem("gla_mask_chain"), 1, nop=True)

            def mask_att(h):
                at.begin(h)
                dve.wait_ge(att_done, h.times(1, 1))
                at.step(dve.tensor_copy(g_att[:], bank(4, 2 * CHUNK, 4 * CHUNK)))
                dve.copy_predicated(g_att[:], g_mask[:], bank(4, 0, 2 * CHUNK)).then_inc(att_masked, 1)
                at.end()

            def update_states(h, m):
                dve.wait_ge(gain_done, h.times(3, m + 1))
                if m > 0:
                    dve.wait_ge(state_done, h.times(3, m))
                for d in range(2):
                    n = m if d == 0 else N_CHUNKS - 1 - m
                    for kb in range(NKB):
                        q = d * NKB + kb
                        st = g_state[:, q * DV:(q + 1) * DV]
                        if m == 0:
                            ins = dve.tensor_copy(st, bank(2 + q))
                        else:
                            k = q * N_CHUNKS + n
                            ins = dve.scalar_tensor_tensor(out=st, in0=st, scalar=g_dec[:, k:k + 1],
                                                           in1=bank(2 + q), op0=ALU.mult, op1=ALU.add)
                ins.then_inc(state_done, 1)

            nc_ = Chain(dve, sem("gla_norm_chain"), 1)

            def norm_out(h):
                nc_.begin(h)
                dve.wait_ge(rms_done, h.times(2, 2))
                nc_.step(dve.reciprocal(g_small[:, 4:6], g_small[:, 2:4]))
                for tt in range(2):
                    ins = dve.tensor_scalar(g_on[:, tt * DV:(tt + 1) * DV], bank(6 + tt),
                                            g_small[:, 4 + tt:5 + tt], None, ALU.mult)
                ins.then_inc(on_done, 1)
                nc_.end()

            def gate_silu(h):
                gs.begin(h)
                dve.wait_ge(proj_taken, gd["taken"](h))
                gs.step(dve.tensor_tensor(g_x[:], g_x[:], g_sg[:], ALU.mult))
                gs.end()

            gs = Chain(dve, sem("gla_silu_chain"), 1)

            def gate_out(h):
                dve.wait_ge(ot_done, h.times(1, 1))
                for vb in range(NVB):
                    a, b = vb * T, (vb + 1) * T
                    ins = dve.scalar_tensor_tensor(
                        out=g_ot[:, a:b], in0=bank(2 + vb // 2, vb % 2 * T, (vb % 2 + 1) * T),
                        scalar=vec[:, V_NORM + vb:V_NORM + vb + 1], in1=g_x[:, a:b],
                        op0=ALU.mult, op1=ALU.mult)
                ins.then_inc(gated, 1)

            def out_lo(h):
                dve.wait_ge(o_hi, h.times(1, 1))
                dve.wait_ge(gated, h.times(1, 1))
                d = gls[:, ds(h.times(NVB * 2 * T), NVB * 2 * T)].rearrange("p (c s t) -> p c s t", c=NVB, s=2)
                dve.tensor_tensor(d[:, :, 1, :], g_ot[:].rearrange("p (c t) -> p c t", c=NVB),
                                  d[:, :, 0, :].bitcast(F32), ALU.subtract).then_inc(o_lo, 1)

            B1 = 3 * NA_PAIRS + 5
            gd["taken"] = lambda h: h.times(12, B1 + 8)

            def gla_head(h, t, last, first):
                s0 = T_GLA + QK_TILES
                for k in range(8 if last else 12):
                    lo(t + 2 * k, s0 + 2 * k)
                    if k == 1 and not first:
                        norm_out(h + -1)
                    if k == 3 and not first:
                        out_lo(h + -1)
                    if k == 9:
                        gate_silu(h)
                    lo(t + 2 * k + 1, s0 + 2 * k + 1)
                    if k == 1:
                        cumulate(h)
                    if k == 2 and not first:
                        gate_out(h + -1)
                    if k == 3:
                        decay(h)
                    if k == 4:
                        mask_att(h)
                    if k == 7:
                        update_states(h, 0)
                    if k == 9:
                        update_states(h, 1)
                    if k == 10:
                        update_states(h, 2)

            s_h = T_GLA + QK_TILES
            gla_head(Pos(0), Pos(s_h), False, True)
            with dve.Fori(0, GLA_HEADS - 2) as i:
                gla_head(Pos(1, 1, i), Pos(s_h + HEAD_TILES, HEAD_TILES, i), False, False)
            H = GLA_HEADS - 1
            gla_head(Pos(H), Pos(s_h + H * HEAD_TILES), True, False)
            update_states(Pos(H), 1)
            update_states(Pos(H), 2)
            lo(Pos(T_MERGE), T_MERGE)
            lo(Pos(T_MERGE + 1), T_MERGE + 1)
            gate_silu(Pos(H))
            norm_out(Pos(H))
            gate_out(Pos(H))
            out_lo(Pos(H))

            mc = Chain(dve, m_chain, 1)

            def gate_a(c, t, parity):
                dve.wait_ge(sig_a, c.times(1, 1))
                dve.wait_ge(tile_used, t.times(1, 3))
                a, b = parity * T, (parity + 1) * T
                dve.tensor_tensor(m_a[:, a:b], bank(4 * parity + 1, 0, T), m_sa[:, a:b],
                                  ALU.mult).then_inc(a_gated, 1)

            def gate_b(c, t, parity):
                mc.begin(c)
                dve.wait_ge(sig_b, c.times(1, 1))
                dve.wait_ge(tile_used, t.times(1, 7))
                dve.wait_ge(a_gated, c.times(1, 1))
                wait(dve, m_lo, c.times(1, -1))
                a, b = parity * T, (parity + 1) * T
                mc.step(dve.tensor_tensor(m_m[:, a:b], bank(4 * parity + 3, 0, T), m_sb[:, a:b], ALU.mult))
                dve.tensor_tensor(m_m[:, a:b], m_m[:, a:b], m_a[:, a:b], ALU.add).then_inc(merged, 1)
                mc.end()

            def merged_lo(c, parity):
                dve.wait_ge(m_hi, c.times(1, 1))
                dve.wait_ge(merged, c.times(1, 1))
                dve.tensor_tensor(ms[:, ds(c.times(2 * T, T), T)], m_m[:, parity * T:(parity + 1) * T],
                                  ms[:, ds(c.times(2 * T), T)].bitcast(F32), ALU.subtract).then_inc(m_lo, 1)

            def merge_step(c, t, slot, parity, prev, ahead=0):
                for k in range(ahead, MERGE_TILES):
                    lo(t + k, slot + k)
                    if k == 1 and prev:
                        gate_b(c + -1, t + -7, 1 - parity)
                    if k == 4:
                        if prev:
                            merged_lo(c + -1, 1 - parity)
                        gate_a(c, t, parity)

            for k in range(4):
                merge_step(Pos(k), Pos(T_MERGE + 7 * k), T_MERGE + 7 * k, k % 2, k > 0, 0 if k else 2)
            with dve.Fori(0, KC // 4 - 1) as i:
                for k in range(4):
                    merge_step(Pos(4 + k, 4, i), Pos(T_MERGE + 28 + 7 * k, 28, i), T_MERGE + 7 * k,
                               k % 2, True)
            lo(Pos(T_OUT), T_OUT)
            lo(Pos(T_OUT + 1), T_OUT + 1)
            gate_b(Pos(KC - 1), Pos(T_OUT - 7), 1)
            merged_lo(Pos(KC - 1), 1)

            rc = Chain(dve, res_chain, 1)

            def add_out(c, t, parity):
                rc.begin(c)
                dve.wait_ge(tile_used, t.times(1, 2))
                r = res[:, ds(c.times(T), T)]
                rc.step(dve.scalar_tensor_tensor(out=r, in0=xs[:, ds(c.times(2 * T), T)].bitcast(F32),
                                                 scalar=ALPHA, in1=bank(parity, 0, T),
                                                 op0=ALU.mult, op1=ALU.add))
                dve.scalar_tensor_tensor(out=r, in0=xs[:, ds(c.times(2 * T, T), T)].bitcast(F32),
                                         scalar=ALPHA, in1=r, op0=ALU.mult, op1=ALU.add).then_inc(res_done, 1)
                rc.end()

            lo(Pos(T_OUT + 2), T_OUT + 2)
            add_out(Pos(0), Pos(T_OUT), 0)
            lo(Pos(T_OUT + 3), T_OUT + 3)
            with dve.Fori(0, KC // 2 - 1) as i:
                lo(Pos(T_OUT + 4, 4, i), T_OUT)
                add_out(Pos(1, 2, i), Pos(T_OUT + 2, 4, i), 1)
                lo(Pos(T_OUT + 5, 4, i), T_OUT + 1)
                lo(Pos(T_OUT + 6, 4, i), T_OUT + 2)
                add_out(Pos(2, 2, i), Pos(T_OUT + 4, 4, i), 0)
                lo(Pos(T_OUT + 7, 4, i), T_OUT + 3)
            lo(Pos(T_PQ), T_PQ)
            add_out(Pos(KC - 1), Pos(T_OUT + 30), 1)
            lo(Pos(T_PQ + 1), T_PQ + 1)
            norm_dve(1, res, sq_a, V_LN + 2 * KC, True)

            lo(Pos(T_PQ + 2), T_PQ + 2)
            lo(Pos(T_PQ + 3), T_PQ + 3)
            with dve.Fori(0, KC // 2 - 1) as i:
                for k in range(4):
                    lo(Pos(T_PQ + 4 + k, 4, i), T_PQ + k)
            lo(Pos(T_PLE), T_PLE)
            dve.wait_ge(p_hi, 1)
            p_dst = ys[:].rearrange("p (c s t) -> p c s t", c=2, s=2)
            dve.tensor_tensor(p_dst[:, :, 1, :], p_in[:].rearrange("p (c t) -> p c t", c=2),
                              p_dst[:, :, 0, :].bitcast(F32), ALU.subtract).then_inc(p_lo, 1)
            for k in range(1, 4):
                lo(Pos(T_PLE + k), T_PLE + k)
            lo(Pos(T_PGATE), T_PGATE)
            lo(Pos(T_PGATE + 1), T_PGATE + 1)

            r2 = Chain(dve, res2_chain, 1)

            def add_ple(c, parity):
                r2.begin(c)
                dve.wait_ge(gsig, c.times(1, 1))
                a, b = parity * T, (parity + 1) * T
                r = res[:, ds(c.times(T), T)]
                r2.step(dve.tensor_tensor(ple_g[:, a:b], ple[:, ds(c.times(T), T)], sgm[:, a:b], ALU.mult))
                dve.scalar_tensor_tensor(out=r, in0=r, scalar=ALPHA, in1=ple_g[:, a:b],
                                         op0=ALU.mult, op1=ALU.add).then_inc(res2_done, 1)
                r2.end()

            dve.wait_ge(ln_normed, 8)
            lo(Pos(T_PGATE + 2), T_PGATE + 2)
            add_ple(Pos(0), 0)
            lo(Pos(T_PGATE + 3), T_PGATE + 3)
            with dve.Fori(0, KC // 2 - 1) as i:
                lo(Pos(T_PGATE + 4, 4, i), T_PGATE)
                add_ple(Pos(1, 2, i), 1)
                lo(Pos(T_PGATE + 5, 4, i), T_PGATE + 1)
                lo(Pos(T_PGATE + 6, 4, i), T_PGATE + 2)
                add_ple(Pos(2, 2, i), 0)
                lo(Pos(T_PGATE + 7, 4, i), T_PGATE + 3)
            add_ple(Pos(KC - 1), 1)

            tk = Chain(dve, tk_chain, 25, nop=True)

            def best8(scores, values, index):
                tk.step(dve.max(values, scores))
                tk.step(dve.max_index(index, values, scores))

            def next8(scores, rest, values, index):
                tk.step(dve.match_replace(rest, values[:, 0:8], scores, LOWEST))
                best8(rest, values[:, 8:16], index[:, 8:16])

            def key_columns(half):
                return slice(half * NKEYS, (half + 1) * NKEYS), slice(half * TOPK, (half + 1) * TOPK)

            def best_keys(u, half):
                a, b = key_columns(half)
                tk.step(dve.tensor_copy(tk_in[:, a], sc[:, ds(u.times(2 * NKEYS, half * NKEYS), NKEYS)]))
                best8(tk_in[:, a], tk_v[:, b][:, 0:8], tk_i[:, b][:, 0:8])

            def next_keys(half):
                a, b = key_columns(half)
                next8(tk_in[:, a], tk_w[:, a], tk_v[:, b], tk_i[:, b])

            def grid(x):
                return x.rearrange("p (a b) -> p a b", a=TOPK)

            def best_pairs():
                a = tk_v[:, 0:TOPK].unsqueeze(2).to_broadcast([P, TOPK, TOPK])
                b = tk_v[:, TOPK:2 * TOPK].unsqueeze(1).to_broadcast([P, TOPK, TOPK])
                tk.step(dve.tensor_tensor(grid(tk_c[:]), a, b, ALU.add))
                best8(tk_c[:], tk_cv[:, 0:8], tk_cp[:, 0:8])
                tk.step(dve.tensor_scalar(tk_s[:, 0:1], tk_cv[:, 0:1], -1.0, None, ALU.mult))

            def pair_ranks():
                dve.tensor_scalar(tk_ab[:, 0:TOPK], tk_cp[:], 4, None, ALU.logical_shift_right)
                tk.step(dve.tensor_scalar(tk_ab[:, TOPK:2 * TOPK], tk_cp[:], 15, None, ALU.bitwise_and))
                dve.tensor_copy(tk_if[:], tk_i[:])
                tk.step(dve.tensor_copy(tk_abf[:], tk_ab[:]))

            halves = tk_eq[:].rearrange("p (h a b) -> p h a b", h=2, a=TOPK)

            def match_ranks():
                r = tk_abf[:].rearrange("p (h a) -> p h a", h=2).unsqueeze(3).to_broadcast([P, 2, TOPK, TOPK])
                ranks = iota_top[:].unsqueeze(1).unsqueeze(1).to_broadcast([P, 2, TOPK, TOPK])
                tk.step(dve.tensor_tensor(halves, r, ranks, ALU.is_equal))

            def look_up(u):
                index = tk_if[:].rearrange("p (h b) -> p h b", h=2).unsqueeze(2).to_broadcast([P, 2, TOPK, TOPK])
                tk.step(dve.tensor_tensor(halves, halves, index, ALU.mult))
                dst = ex[:].rearrange("p (h c) -> p h c", h=2)[:, :, ds(u.times(TOPK), TOPK)]
                tk.step(dve.tensor_reduce(dst, halves, AX.X, ALU.add))

            def expert_gates(u):
                dve.wait_ge(tk_exp, u.times(1, 1))
                tk.step(dve.reciprocal(tk_s[:, 2:3], tk_s[:, 1:2]))
                dve.tensor_scalar(exg[:, ds(u.times(TOPK), TOPK)], tk_g[:], tk_s[:, 2:3], None,
                                  ALU.mult).then_inc(ex_done, 1)

            def top_unit(u, t):
                tk.begin(u)
                for k in range(8):
                    lo(t + k, T_U + k)
                    if k in (0, 2):
                        best_keys(u, k // 2)
                    if k in (1, 3):
                        next_keys(k // 2)
                    if k == 4:
                        best_pairs()
                    if k == 5:
                        next8(tk_c[:], tk_cw[:], tk_cv, tk_cp)
                        dve.engine_nop().then_inc(tk_neg, 1)
                        pair_ranks()
                    if k == 6:
                        match_ranks()
                    if k == 7:
                        look_up(u)
                        expert_gates(u)
                tk.end()

            dve.wait_ge(sc_taken, HP)
            with dve.Fori(0, 16) as i:
                top_unit(Pos(0, 1, i), Pos(T_U, 8, i))

            def hot(g, n):
                wait(dve, gate_mm, g.times(1))
                for q in range(4):
                    a, b = q * NKEYS, (q + 1) * NKEYS
                    col = ds(g.times(4, q), 1)
                    dve.tensor_scalar(hot0[:, a:b], iota_key[:], idx0_t[:, col], gate_t[:, col],
                                      ALU.is_equal, ALU.mult).then_inc(hot_ready, 1)
                    dve.tensor_scalar(hot1[:, a:b], iota_key[:], idx1_t[:, col], None,
                                      ALU.is_equal).then_inc(hot_ready, 1)

            lo(Pos(T_U + 128), T_U)
            dve.wait_ge(ex_t_taken, 3)
            lo(Pos(T_U + 129), T_U + 1)
            hot(Pos(0), 0)
            for n in range(1, 4):
                lo(Pos(T_U + 128 + 2 * n), T_U + 2 * n)
                lo(Pos(T_U + 129 + 2 * n), T_U + 2 * n + 1)
                hot(Pos(n), n)
            with dve.Fori(0, 15) as i:
                for n in range(4):
                    lo(Pos(T_U + 136 + 2 * n, 8, i), T_U + 2 * n)
                    lo(Pos(T_U + 137 + 2 * n, 8, i), T_U + 2 * n + 1)
                    hot(Pos(4 + n, 4, i), n)

            by_column = gates[:].rearrange("p (t j) -> p t j", j=NKEYS)

            def weigh(j, slot):
                dve.wait_ge(gelu_landed[slot], j.over(4).times(16, 16) if j.i is not None
                            else 16 * (j.const // 4 + 1))
                parity = slot % 2
                wait(dve, w_lo, j.times(1, -1))
                dve.tensor_tensor(wexp[:, parity * T:(parity + 1) * T].unsqueeze(2),
                                  gst[:, slot * T:(slot + 1) * T].unsqueeze(2),
                                  by_column[:, :, ds(j.times(1), 1)], ALU.mult).then_inc(w_ready, 1)

            def weight_lo(j, parity):
                dve.wait_ge(w_hi, j.times(1, 1))
                dve.wait_ge(w_ready, j.times(1, 1))
                a = parity * 2 * T
                dve.tensor_tensor(ys[:, a + T:a + 2 * T], wexp[:, parity * T:(parity + 1) * T],
                                  ys[:, a:a + T].bitcast(F32), ALU.subtract).then_inc(w_lo, 1)

            dve.wait_ge(gate_taken, T // 4)
            lo(Pos(T_V), T_V)
            lo(Pos(T_V + 1), T_V + 1)
            weigh(Pos(0), 0)
            weigh(Pos(1), 1)
            weight_lo(Pos(0), 0)
            weight_lo(Pos(1), 1)
            weigh(Pos(2), 2)
            for k in range(2 + AHEAD, 4):
                lower(Pos(T_V + k), T_V + k)
            with dve.Fori(0, NKEYS // 4 - 1) as i:
                for k in range(4):
                    lower(Pos(T_V + 4 + 2 * k, 8, i), T_V + 2 * k)
                    weight_lo(Pos(2 + k, 4, i), k % 2)
                    lower(Pos(T_V + 5 + 2 * k, 8, i), T_V + 2 * k + 1)
                    weigh(Pos(3 + k, 4, i), (3 + k) % 4)
            for k in range(2):
                lower(Pos(T_END - 4 + 2 * k), T_END + 2 * k)
                weight_lo(Pos(NKEYS - 2 + k), k)
                if k == 0:
                    weigh(Pos(NKEYS - 1), 3)
                lower(Pos(T_END - 3 + 2 * k), T_END + 2 * k + 1)

            dve.wait_ge(tile_used, T_END)
            dve.wait_ge(res_back, 16)
            for n in range(8):
                a, b = n * 512, (n + 1) * 512
                dve.tensor_tensor(fin[:, a:b], fin[:, a:b], bank(n), ALU.add).then_inc(fin_added, 1)
            dve.wait_ge(fin_added, 8)
            norm_dve(2, fin, fin_sq, V_LN + 4 * KC, False)


def _block(w):
    return w.reshape(2, 8, P, P).transpose(0, 2, 1, 3).reshape(2, P, TILE)


def _half(w):
    return w.reshape(8, P, P).transpose(1, 0, 2).reshape(1, P, TILE)


def _layout(a):
    import numpy as np

    w, b = a["w_in"][0], a["b_in"][0]
    naq, nak, nav = 0, 1024, 2048
    gq, gk, gv, gg = 3072, 4096, 5120, 7168
    lrf, lrb, ga, gb = 9216, 9232, 9248, 11296
    cols = []
    for s in range(NA_PAIRS):
        cols += [naq + s * P, nak + s * P, nav + s * P]
    w_rank = np.zeros((D, P), w.dtype)
    b_rank = np.zeros(P, b.dtype)
    for k, at in enumerate((lrf, lrb)):
        w_rank[:, 32 * k:32 * k + RANK] = w[:, at:at + RANK]
        b_rank[32 * k:32 * k + RANK] = b[at:at + RANK]
    qk = [[gq + h * DK + k * P for k in range(2)] + [gk + h * DK + k * P for k in range(2)]
          for h in range(GLA_HEADS)]
    vg = [[gv + h * DV + k * P for k in range(4)] + [gg + h * DV + k * P for k in range(4)]
          for h in range(GLA_HEADS)]
    stream = np.empty((T_END, P, TILE), w.dtype)
    at = 0

    def put(tiles):
        nonlocal at
        stream[at:at + len(tiles)] = tiles
        at += len(tiles)

    for c in cols:
        put(_block(w[:, c:c + P]))
    put(_block(w_rank))
    for c in qk[0]:
        put(_block(w[:, c:c + P]))
    for h in range(GLA_HEADS):
        for c in vg[h] + (qk[h + 1] if h + 1 < GLA_HEADS else []):
            put(_block(w[:, c:c + P]))
    assert at == T_MERGE - 0
    for c in range(KC):
        s = slice(c * P, (c + 1) * P)
        put(_block(w[:, ga + c * P:ga + (c + 1) * P]))
        put(_half(a["w_proj_a"][0][:, s]))
        put(_block(w[:, gb + c * P:gb + (c + 1) * P]))
        put(_block(a["w_proj_b"][0][:, s]))
    for m in (a["w_out"][0], a["peer_wq"][0]):
        for c in range(KC):
            put(_block(m[:, c * P:(c + 1) * P]))
    put(a["w_ple"][0].reshape(2, P, 4, 4, P).transpose(2, 1, 3, 0, 4).reshape(4, P, TILE))
    for c in range(KC):
        put(_block(a["w_ple_gate"][0][:, c * P:(c + 1) * P]))
    assert at == T_U
    u = a["peer_u"][0].reshape(NKEYS, NKEYS, 2, 8, P)
    stream[T_U:T_V] = u.transpose(1, 2, 4, 3, 0).reshape(2 * NKEYS, P, TILE)
    v = a["peer_v"][0].reshape(NKEYS, NKEYS, 2, TILE)
    stream[T_V:T_END] = v.transpose(1, 2, 0, 3).reshape(2 * NKEYS, P, TILE)

    vectors = np.zeros((P, V_COLS), b.dtype)
    for k, name in enumerate(("ln_emb_g", "ln_emb_b", "ln_a_g", "ln_a_b", "ln_b_g", "ln_b_b")):
        vectors[:, V_LN + k * KC:V_LN + (k + 1) * KC] = a[name].reshape(KC, P).T
    for k, c in enumerate(cols):
        vectors[:, V_NA + k] = b[c:c + P]
    vectors[:, V_RANK] = b_rank
    for h in range(GLA_HEADS):
        for k, c in enumerate(qk[h] + vg[h]):
            vectors[:, V_GLA + h * GLA_BLOCKS + k] = b[c:c + P]
        for k, name in enumerate(("gla_gk_bias_f", "gla_gk_bias_b")):
            part = a[name][0].reshape(GLA_HEADS, NKB, P)[h]
            vectors[:, V_DECAY + 4 * h + 2 * k:V_DECAY + 4 * h + 2 * k + 2] = part.T
    for c in range(KC):
        for k, base in enumerate((ga, gb)):
            vectors[:, V_GATES + 2 * c + k] = b[base + c * P:base + (c + 1) * P]
    vectors[:, V_NORM:V_NORM + NVB] = a["gla_norm_g"][0].reshape(NVB, P).T

    rows = T // GRID_W
    q, k = np.arange(T), np.arange(T)
    qr, qc, kr, kc = q // GRID_W, q % GRID_W, k // GRID_W, k % GRID_W
    start = np.clip(qc - WIN_C // 2, 0, GRID_W - WIN_C)
    seen = (kc[None] >= start[:, None]) & (kc[None] < start[:, None] + WIN_C)
    assert rows <= WIN_R
    dr = kr[None] - qr[:, None] + WIN_R - 1
    dc = np.where(seen, kc[None] - qc[:, None] + WIN_C - 1, 0)
    table = a["na_rpb"][0][:, dr, dc]
    table = np.where(seen[None], table, np.float32(MASKED)).astype(b.dtype)
    rpb = table.reshape(NA_PAIRS, 2, 2, P, T).transpose(0, 3, 1, 2, 4).reshape(NA_PAIRS, P, 4 * T)

    up = np.zeros((GLA_HEADS, 64, DK), w.dtype)
    for k, name in enumerate(("gla_gk_up_f", "gla_gk_up_b")):
        up[:, 32 * k:32 * k + RANK] = a[name][0].reshape(RANK, GLA_HEADS, DK).transpose(1, 0, 2)
    keys = a["peer_sub_keys"][0].reshape(HP, NKEYS, P).transpose(2, 0, 1).reshape(P, HP * NKEYS)
    x_t = a["x"][0].T.reshape(KC, P, T).transpose(1, 0, 2).reshape(P, KC * T)
    p_t = a["p"][0, 0].T.reshape(2, P, T).transpose(1, 0, 2).reshape(P, 2 * T)
    return {"stream": stream, "vectors": vectors, "x_t": x_t, "p_t": p_t, "rpb": rpb,
            "decay_up": up, "keys": keys}


def kernel(**inputs):
    import numpy as np
    import concourse.bacc as bacc
    from concourse.bass_utils import run_bass_kernel_spmd

    laid = {n: np.ascontiguousarray(v) for n, v in
            _layout({n: np.asarray(v) for n, v in inputs.items()}).items()}
    nc = bacc.Bacc("TRN2", target_bir_lowering=False, num_devices=1)
    args = {n: nc.dram_tensor(n, v.shape, mybir.dt.from_np(v.dtype), kind="ExternalInput").ap()
            for n, v in laid.items()}
    out = nc.dram_tensor("out_t", (P, KC * T), mybir.dt.float32, kind="ExternalOutput").ap()
    encoder_layer(nc, out=out, **args)
    r = run_bass_kernel_spmd(nc, [laid], core_ids=[0])
    y = np.asarray(r.results[0]["out_t"]).reshape(P, KC, T)
    return np.ascontiguousarray(y.transpose(2, 1, 0).reshape(1, T, D))
```

```python
from contextlib import ExitStack

import concourse.bass as bass
from concourse import mybir

P = 128
D = 2048
T = 256
KC = D // P
NA_HEADS, NA_DIM, GRID_W, WIN_R, WIN_C = 16, 64, 64, 8, 16
NA_PAIRS = NA_HEADS // 2
GLA_HEADS, DK, DV, CHUNK, RANK = 4, 256, 512, 64, 16
NKB, NVB = DK // P, DV // P
N_CHUNKS = T // CHUNK
PEER_HEADS, NKEYS, TOPK = 8, 128, 16
HP = 2 * PEER_HEADS
PLE = 256
EPS = 1e-5
ALPHA = 2.0 ** 0.25
LOWEST = -3.0e38
MASKED = -1.0e30

TILE = 8 * P
RING = 4
AHEAD = 1
NA_TILES = NA_PAIRS * 6
RANK_TILES = 2
QK_TILES = 8
VG_TILES = 16
HEAD_TILES = VG_TILES + QK_TILES
MERGE_TILES = 7
T_NA = 0
T_RANK = T_NA + NA_TILES
T_GLA = T_RANK + RANK_TILES
T_MERGE = T_GLA + GLA_HEADS * HEAD_TILES
T_OUT = T_MERGE + KC * MERGE_TILES
T_PLE = T_OUT + 2 * KC
T_PQ = T_PLE + 4
T_PGATE = T_PQ + 2 * KC
T_U = T_PGATE + 2 * KC
T_V = T_U + 2 * NKEYS
T_END = T_V + 2 * NKEYS

V_LN = 0
V_NA = V_LN + 4 * KC
V_RANK = V_NA + 3 * NA_PAIRS
V_GLA = V_RANK + 1
GLA_BLOCKS = 2 * NKB + 2 * NVB
V_GATES = V_GLA + GLA_HEADS * GLA_BLOCKS
V_NORM = V_GATES + 2 * KC
V_DECAY = V_NORM + NVB
V_COLS = V_DECAY + 4 * GLA_HEADS


class Pos:

    def __init__(self, const, per=0, i=None):
        self.const, self.per, self.i = const, per, i

    def __add__(self, n):
        return Pos(self.const + n, self.per, self.i)

    def times(self, each, plus=0):
        fixed = self.const * each + plus
        return fixed if self.i is None else self.i * (self.per * each) + fixed

    def over(self, n):
        assert self.per % n == 0
        return Pos(self.const // n, self.per // n, self.i)


def wait(eng, sem, value):
    if isinstance(value, int) and value <= 0:
        return
    eng.wait_ge(sem, value)


class Line:

    def __init__(self, eng, sem):
        self.eng, self.sem, self.n = eng, sem, 0

    def step(self, ins):
        self.n += 1
        ins.then_inc(self.sem, 1)
        self.eng.wait_ge(self.sem, self.n)


class Chain:

    def __init__(self, eng, sem, per, nop=False):
        self.eng, self.sem, self.per, self.turn, self.n = eng, sem, per, None, 0
        self.nop = nop

    def begin(self, turn):
        self.turn, self.n = turn, 0

    def step(self, ins):
        self.n += 1
        ins.then_inc(self.sem, 1)
        self.eng.wait_ge(self.sem, self.turn.times(self.per, self.n))
        if self.nop:
            self.eng.nop(nofuse=True)

    def end(self):
        assert self.n == self.per


def encoder_layer(nc, stream, vectors, gains, x_in, p_t, rpb, decay_up, keys, out):
    F32, F32R, BF16, U32, U8 = (mybir.dt.float32, mybir.dt.float32r, mybir.dt.bfloat16,
                                mybir.dt.uint32, mybir.dt.uint8)
    ALU, ACT, AX = mybir.AluOpType, mybir.ActivationFunctionType, mybir.AxisListType
    ds = bass.ds

    h_dram = nc.dram_tensor("h_spill", (2, P, D), F32, kind="Internal").ap()
    residual_dram = nc.dram_tensor("residual_spill", (2, P, D), F32, kind="Internal").ap()
    gelu_dram = nc.dram_tensor("gelu_spill", (NKEYS, P, T), F32, kind="Internal").ap()

    with ExitStack() as ctx:
        def sb(name, cols, dt=F32, group=ctx):
            return group.enter_context(nc.sbuf_tensor(name, [P, cols], dt))

        def sem(name):
            return ctx.enter_context(nc.semaphore(name))

        with ExitStack() as g:
            fin = sb("final", 2 * D, group=g)
            fin_tab = sb("final_gain_shift", 2 * D, group=g)
        xs = sb("act_split", KC * 2 * T, F32R)
        with ExitStack() as g:
            w_in = sb("weights_in", RING * TILE, group=g)
        w_low = sb("weights_lower", RING * TILE, F32R)
        w_up = sb("weights_upper", RING * TILE, F32R)
        vec = sb("vec_table", V_COLS)
        ident = sb("identity", P)
        iota_key = sb("iota_key", NKEYS)
        iota_top = sb("iota_top", TOPK)
        eps_t = sb("eps", 1)
        ln_st = sb("norm_stats", 2 * 4 * 6)
        ln_mv = sb("norm_mean_var", 2 * 2)
        ln_sd = sb("norm_std", 2 * 2)
        zeros = sb("zeros", P, BF16)
        gst = sb("gelu_ring", 4 * T)

        with ExitStack() as g:
            idx0_t = sb("expert_row_t", T, group=g)
            idx1_t = sb("expert_col_t", T, group=g)
            gate_t = sb("expert_gate_t", T, group=g)
            hot0 = sb("hot_rows", 4 * NKEYS, group=g)
            hot1 = sb("hot_cols", 4 * NKEYS, group=g)
        with ExitStack() as g:
            ys = sb("last_split", 2 * 2 * T, F32R, group=g)
            wexp = sb("expert_weight", 2 * T, group=g)
        sb("shared_small", 3 * T + 8 * NKEYS)

        region = ExitStack()
        with region as g:
            nas = sb("na_split", NA_PAIRS * 2 * T, F32R, group=g)
            gls = sb("gla_split", KC * 2 * T, F32R, group=g)
            with ExitStack() as h:
                na_qkv = sb("na_qkv", 2 * 3 * T, group=h)
                na_bias = sb("na_bias", 2 * 4 * T, group=h)
                na_s = sb("na_scores", 4 * T, group=h)
                na_pt = sb("na_probs_t", 4 * T, group=h)
                na_v = sb("na_v", 2 * P, group=h)
                na_small = sb("na_small", 16, group=h)
                x_tok = sb("x_tokens", 2 * D, group=h)
                x_tab = sb("x_gain_shift", 2 * D, group=h)
                x_feat = sb("x_features", KC * T, group=h)
            with ExitStack() as h:
                g_z = sb("gla_z", 4 * T, group=h)
                g_a = sb("gla_a", 4 * T, group=h)
                g_c = sb("gla_cum", 4 * T, group=h)
                g_qd = sb("gla_q_decayed", 4 * T, group=h)
                g_ki = sb("gla_k_intra", 4 * T, group=h)
                g_ks = sb("gla_k_state", 4 * T, group=h)
                g_kt = sb("gla_k_state_t", 4 * T, group=h)
                g_q = sb("gla_q", NKB * T, group=h)
                g_k = sb("gla_k", NKB * T, group=h)
                g_vt = sb("gla_v_t", NVB * T, group=h)
                g_rank = sb("gla_rank", T, group=h)
                g_up = sb("gla_up", DK, group=h)
                g_v = sb("gla_v", 2 * DV, group=h)
                g_att = sb("gla_att", 2 * CHUNK, group=h)
                g_state = sb("gla_state", 4 * DV, group=h)
                g_dec = sb("gla_chunk_decay", 16, group=h)
                g_x = sb("gla_gate_in", NVB * T, group=h)
                g_sg = sb("gla_gate_sig", NVB * T, group=h)
                g_on = sb("gla_out_normed", 2 * DV, group=h)
                g_ot = sb("gla_out_t", NVB * T, group=h)
                g_small = sb("gla_small", 8, group=h)
                g_reset = sb("gla_reset", 2 * T, group=h)
                g_mask = sb("gla_mask", 2 * CHUNK, U8, group=h)
                g_maskf = sb("gla_mask_f", 2 * CHUNK, group=h)
            with ExitStack() as h:
                ms = sb("merged_split", KC * 2 * T, F32R, group=h)
                m_sa = sb("merge_sig_a", 2 * T, group=h)
                m_sb = sb("merge_sig_b", 2 * T, group=h)
                m_a = sb("merge_a", 2 * T, group=h)
                m_m = sb("merge_sum", 2 * T, group=h)
                tok = sb("residual", 2 * D, group=h)
                tok_tab = sb("residual_gain_shift", 2 * D, group=h)
        with ExitStack() as g:
            sc = sb("key_scores", 2 * HP * NKEYS, group=g)
            key_t = sb("keys_t", HP * NKEYS, group=g)
            pq = sb("peer_q", 2 * T, group=g)
            ple = sb("ple", 2 * D, group=g)
            p_in = sb("p_in", 2 * T, group=g)
            sgm = sb("ple_sig", 2 * 512, group=g)
            ple_g = sb("ple_gated", 2 * 512, group=g)
            tk_in = sb("top_scores", 2 * NKEYS, group=g)
            tk_w = sb("top_rest", 2 * NKEYS, group=g)
            tk_v = sb("top_values", 2 * TOPK, group=g)
            tk_i = sb("top_index", 2 * TOPK, U32, group=g)
            tk_if = sb("top_index_f", 2 * TOPK, group=g)
            tk_c = sb("pair_sums", TOPK * TOPK, group=g)
            tk_cw = sb("pair_rest", TOPK * TOPK, group=g)
            tk_cv = sb("pair_values", TOPK, group=g)
            tk_cp = sb("pair_pos", TOPK, U32, group=g)
            tk_ab = sb("pair_ranks", 2 * TOPK, U32, group=g)
            tk_abf = sb("pair_ranks_f", 2 * TOPK, group=g)
            tk_eq = sb("pair_match", 2 * TOPK * TOPK, group=g)
            tk_g = sb("pair_gate", TOPK, group=g)
            tk_s = sb("pair_small", 4, group=g)
            ex = sb("expert_row_col", 4 * P, group=g)
            exg = sb("expert_gate", 2 * P, group=g)
            h_feat = sb("h_features", KC * T, group=g)
        gates = sb("expert_gates", T * NKEYS)
        ps = ctx.enter_context(nc.psum_tensor("psum", [P, 8 * 512], F32))

        def bank(n, a=0, b=512, p0=0, p1=P):
            return ps[p0:p1, n * 512 + a:n * 512 + b]

        landed = [sem(f"tile_landed_{i}") for i in range(4)]
        hi_ready, split_ready, tile_used = sem("hi_ready"), sem("split_ready"), sem("tile_used")
        consts_ready, pool_chain = sem("consts_ready"), sem("pool_chain")
        vec_landed, up_landed = sem("vec_landed"), sem("up_landed")
        x_landed = [sem("x_landed_0"), sem("x_landed_1")]
        bias_landed = [sem("na_bias_landed_0"), sem("na_bias_landed_1")]
        ln_var, ln_std, ln_normed, ln_turned, ln_part_a, ln_part_d, ln_hi, ln_lo, ln_chain = (
            sem(n) for n in ("ln_var", "ln_std", "ln_normed", "ln_turned", "ln_features_act",
                             "ln_features_dve", "ln_hi", "ln_lo", "ln_chain"))
        x_tab_landed, h_ready, h_spilled, h_back, tok_tab_landed, h2_ready = (sem(n) for n in (
            "x_gain_shift_landed", "h_ready", "h_spilled", "h_back", "gain_shift_landed", "h2_ready"))
        proj_taken = sem("proj_taken")
        na_qk, na_s_read, na_negmax, na_exp, na_rinv, na_probs = (sem(n) for n in (
            "na_qk", "na_scores_read", "na_negmax", "na_exp", "na_rinv", "na_probs"))
        na_pt_done, na_pt_copied, na_vt_done, na_v_copied, na_pv, na_hi, na_lo, na_chain = (
            sem(n) for n in ("na_pt_done", "na_pt_copied", "na_vt_done", "na_v_copied", "na_pv",
                             "na_hi", "na_lo", "na_chain"))
        la_done, z_done, gap_done, exp_done, decayed, kt_done, kt_copied = (sem(n) for n in (
            "gla_la_done", "gla_z_done", "gla_gap_done", "gla_exp_done", "gla_decayed",
            "gla_kt_done", "gla_kt_copied"))
        att_done, att_masked, vt_done, v_copied, gain_done, state_done, o_done = (sem(n) for n in (
            "gla_att_done", "gla_att_masked", "gla_vt_done", "gla_v_copied", "gla_gain_done",
            "gla_state_done", "gla_o_done"))
        rms_done, on_done, ot_done, gated, o_hi, o_lo, gla_act, gla_dve, sig_ready = (
            sem(n) for n in ("gla_rms_done", "gla_on_done", "gla_ot_done", "gla_gated", "gla_o_hi",
                             "gla_o_lo", "gla_act_chain", "gla_dve_chain", "gla_sig_ready"))
        sig_a, sig_b, a_gated, merged, m_hi, m_lo, m_chain = (sem(n) for n in (
            "merge_sig_a", "merge_sig_b", "merge_a_gated", "merge_sum_ready", "merge_hi", "merge_lo",
            "merge_chain"))
        res_done = sem("residual_done")
        keys_landed, pq_taken, sc_done, sc_taken = (sem(n) for n in (
            "keys_landed", "peer_q_taken", "scores_done", "scores_taken"))
        p_landed, p_hi, p_lo, ple_taken, gsig, res2_done, res2_chain, res_spilled = (
            sem(n) for n in ("p_landed", "p_hi", "p_lo", "ple_taken", "ple_sig_ready",
                             "residual2_done", "residual2_chain", "residual_spilled"))
        tk_chain, tk_neg, tk_exp, ex_done, ex_t_done, ex_t_taken = (sem(n) for n in (
            "topk_chain", "topk_negmax", "topk_exp", "experts_done", "experts_turned",
            "experts_taken"))
        gelu_done = sem("gelu_done")
        gelu_stored = [sem(f"gelu_stored_{i}") for i in range(4)]
        hot_ready, gate_mm, gate_taken = sem("hot_ready"), sem("gate_spread"), sem("gate_taken")
        gelu_landed = [sem(f"gelu_landed_{i}") for i in range(4)]
        w_ready, w_hi, w_lo, y_used, y_done = (sem(n) for n in (
            "expert_weight_ready", "expert_weight_hi", "expert_weight_lo", "expert_weight_used",
            "y_done"))
        fin_landed, fin_added, out_ready, out_stored = (sem(n) for n in (
            "final_landed", "final_added", "out_ready", "out_stored"))

        block = ctx.enter_context(nc.Block())

        @block.sync
        def _(sp):
            def load(t, slot):
                wait(sp, tile_used, t.times(1, 1 - RING))
                src = stream[ds(t.times(1), 1)].rearrange("n p f -> (n p) f")
                sp.dma_start(w_in[:, slot * TILE:(slot + 1) * TILE], src).then_inc(landed[slot], 16)

            for tt in range(2):
                sp.dma_start(x_tok[:, tt * D:(tt + 1) * D], x_in[tt]).then_inc(x_landed[tt], 16)
            for s in range(4):
                load(Pos(s), s)
            with sp.Fori(0, T_END // 4 - 1) as i:
                for s in range(4):
                    load(Pos(4 + s, 4, i), s)
            for t in range(T_END // 4 * 4, T_END):
                load(Pos(t), t % 4)
            for tt in range(2):
                sp.wait_ge(out_ready, tt + 1)
                sp.dma_start(out[tt], fin[:, tt * D:(tt + 1) * D]).then_inc(out_stored, 16)
            sp.wait_ge(out_stored, 32)

        @block.gpsimd
        def _(pool):
            def load_table(dst, norm, done):
                for k in range(2):
                    src = gains[2 * norm + k:2 * norm + k + 1].to_broadcast([P, D])
                    pool.dma_start(dst[:, k * D:(k + 1) * D], src).then_inc(done, 16)

            pool.dma_start(vec[:], vectors).then_inc(vec_landed, 16)
            n = [0]

            def const(ins):
                n[0] += 1
                ins.then_inc(pool_chain, 1)
                pool.wait_ge(pool_chain, n[0])

            const(pool.memset(eps_t[:], EPS))
            const(pool.memset(zeros[:], 0.0))
            const(pool.memset(ident[:], 0.0))
            const(pool.affine_select(out=ident[:], in_=ident[:], compare_op=ALU.not_equal, fill=1.0,
                                     base=0, pattern=[[-1, P]], channel_multiplier=1))
            const(pool.iota(iota_key[:], [[1, NKEYS]], base=0, channel_multiplier=0,
                            allow_small_or_imprecise_dtypes=True))
            const(pool.iota(iota_top[:], [[1, TOPK]], base=0, channel_multiplier=0,
                            allow_small_or_imprecise_dtypes=True))
            pool.engine_nop().then_inc(consts_ready, 1)

            def load_bias(s, slot):
                wait(pool, na_s_read, s.times(1, -1))
                src = rpb[ds(s.times(1), 1)].rearrange("n p f -> (n p) f")
                pool.dma_start(na_bias[:, slot * 4 * T:(slot + 1) * 4 * T], src).then_inc(
                    bias_landed[slot], 16)

            load_table(x_tab, 0, x_tab_landed)
            load_bias(Pos(0), 0)
            load_bias(Pos(1), 1)

            def scale_shift(x, table, tt, done):
                v = x[:, tt * D:(tt + 1) * D]
                const(pool.tensor_tensor(v, v, table[:, 0:D], ALU.mult))
                pool.tensor_tensor(v, v, table[:, D:2 * D], ALU.add).then_inc(done, 1)

            pool.wait_ge(x_tab_landed, 32)
            for tt in range(2):
                pool.wait_ge(ln_turned, tt + 1)
                scale_shift(x_tok, x_tab, tt, h_ready)
                pool.wait_ge(h_ready, tt + 1)
                pool.dma_start(h_dram[tt], x_tok[:, tt * D:(tt + 1) * D]).then_inc(h_spilled, 16)
            with pool.Fori(0, NA_PAIRS // 2 - 1) as i:
                load_bias(Pos(2, 2, i), 0)
                load_bias(Pos(3, 2, i), 1)

            pool.wait_ge(na_lo, NA_PAIRS)
            pool.wait_ge(h_spilled, 32)
            const(pool.memset(g_reset[:], 1.0))
            reset0 = g_reset[:].rearrange("p (n c) -> p n c", c=CHUNK)[:, :, 0:1]
            const(pool.memset(reset0, 0.0))
            const(pool.memset(g_maskf[:], 1.0))
            for half in range(2):
                m = g_maskf[64 * half:64 * half + 64, :].rearrange("p (a c) -> p a c", a=2)
                const(pool.affine_select(out=m, in_=m, compare_op=ALU.is_ge, fill=0.0, base=0,
                                         pattern=[[0, 2], [1, CHUNK]], channel_multiplier=-1))
            const(pool.tensor_copy(g_mask[:], g_maskf[:]))
            pool.engine_nop().then_inc(consts_ready, 1)

            def load_up(h):
                wait(pool, la_done, h.times(1))
                src = decay_up[ds(h.times(1), 1)].rearrange("n p f -> (n p) f")
                pool.dma_start(g_up[0:64, :], src).then_inc(up_landed, 16)

            load_up(Pos(0))
            with pool.Fori(0, GLA_HEADS - 1) as i:
                load_up(Pos(1, 1, i))

            pool.wait_ge(o_lo, GLA_HEADS)
            for tt in range(2):
                pool.dma_start(tok[:, tt * D:(tt + 1) * D], h_dram[tt]).then_inc(h_back, 16)
            load_table(tok_tab, 1, tok_tab_landed)
            pool.wait_ge(tile_used, T_OUT)
            pool.dma_start(p_in[:], p_t).then_inc(p_landed, 16)
            pool.dma_start(key_t[:], keys).then_inc(keys_landed, 16)
            pool.wait_ge(tok_tab_landed, 32)
            for tt in range(2):
                pool.wait_ge(ln_turned, 2 + tt + 1)
                scale_shift(tok, tok_tab, tt, h2_ready)
            pool.wait_ge(res2_done, 8)
            for tt in range(2):
                pool.dma_start(residual_dram[tt], tok[:, tt * D:(tt + 1) * D]).then_inc(res_spilled, 16)

            def store_gelu(j, slot):
                pool.wait_ge(gelu_done, j.times(1, 1))
                dst = gelu_dram[ds(j.times(1), 1)].rearrange("n p f -> (n p) f")
                pool.dma_start(dst, gst[:, slot * T:(slot + 1) * T]).then_inc(gelu_stored[slot], 16)

            with pool.Fori(0, NKEYS // 4) as i:
                for s in range(4):
                    store_gelu(Pos(s, 4, i), s)
            for s in range(4):
                pool.wait_ge(gelu_stored[s], 16 * (NKEYS // 4))

            def load_gelu(j, slot):
                wait(pool, w_ready, j.times(1, -3))
                src = gelu_dram[ds(j.times(1), 1)].rearrange("n p f -> (n p) f")
                pool.dma_start(gst[:, slot * T:(slot + 1) * T], src).then_inc(gelu_landed[slot], 16)

            for s in range(4):
                load_gelu(Pos(s), s)
            pool.wait_ge(tile_used, T_V)
            pool.wait_ge(res_spilled, 32)
            for tt in range(2):
                pool.dma_start(fin[:, tt * D:(tt + 1) * D], residual_dram[tt]).then_inc(fin_landed, 16)
            load_table(fin_tab, 2, fin_landed)
            with pool.Fori(0, NKEYS // 4 - 1) as i:
                for s in range(4):
                    load_gelu(Pos(4 + s, 4, i), s)

        @block.tensor
        def _(pe):
            def turn_normed(n, x):
                for tt in range(2):
                    pe.wait_ge(ln_normed, 2 * n + tt + 1)
                    for c in range(KC):
                        a = tt * D + c * P
                        mm = pe.transpose(bank(c // 2, c % 2 * T + tt * P, c % 2 * T + (tt + 1) * P),
                                          x[:, a:a + P], ident[:])
                    mm.then_inc(ln_turned, 1)

            def products(t, slot, pieces, last_of=None):
                pe.wait_ge(split_ready, t.times(1, 1))
                base = slot % RING * TILE
                for dst, col, act, start, stop in pieces:
                    w_h = w_up[:, base + col * P:base + (col + 1) * P]
                    w_l = w_low[:, base + col * P:base + (col + 1) * P]
                    pe.matmul(dst, w_h, act[:, 0:T], start=start, stop=False, skip_group_check=True)
                    pe.matmul(dst, w_h, act[:, T:2 * T], start=False, stop=False,
                              skip_group_check=True)
                    mm = pe.matmul(dst, w_l, act[:, 0:T], start=False, stop=stop,
                                   skip_group_check=True)
                mm.then_inc(tile_used, 1)

            def products_by_token(t, slot, act, out_bank, start, stop):
                pe.wait_ge(split_ready, t.times(1, 1))
                base = slot % RING * TILE
                for tt in range(2):
                    for k, (part, w) in enumerate(((0, w_up), (0, w_low), (1, w_up))):
                        for n in range(2):
                            mm = pe.matmul(out_bank(tt, n), act[:, part * T + tt * P:part * T + (tt + 1) * P],
                                           w[:, base + n * 512:base + (n + 1) * 512],
                                           start=start and k == 0, stop=stop and k == 2,
                                           skip_group_check=True)
                mm.then_inc(tile_used, 1)

            def by_token(t, acts):
                with pe.Fori(0, 2) as half:
                    for c in range(KC):
                        products_by_token(Pos(t + c, KC, half), t + c, chunk(acts, c),
                                          lambda tt, n: ps[:, ds(half * 1024 + (tt * D + n * 512), 512)],
                                          c == 0, c == KC - 1)

            def chunk(acts, c):
                return acts[:, c * 2 * T:(c + 1) * 2 * T]

            def half_block(t, slot, dst, acts, first, last, k0=0):
                products(t, slot, [(dst, c, chunk(acts, k0 + c), first and c == 0, last and c == 7)
                                   for c in range(8)])

            def two_tiles(t, slot, dst, acts):
                half_block(t, slot, dst, acts, True, False)
                half_block(t + 1, slot + 1, dst, acts, False, True, k0=8)

            pe.wait_ge(consts_ready, 1)
            turn_normed(0, x_tok)
            pe.wait_ge(ln_lo, 4)

            def na_block(s, k, t, slot, parity):
                wait(pe, proj_taken, s.times(3, k - 1))
                two_tiles(t, slot, bank((3 * parity + k) % 2, 0, T), xs)

            def qkv(parity, k):
                a = (parity * 3 + k) * T
                return na_qkv[:, a:a + T]

            def na_scores(s, parity):
                pe.wait_ge(proj_taken, s.times(3, 3))
                wait(pe, na_s_read, s.times(1))
                for e in range(2):
                    rows = slice(64 * e, 64 * e + 64)
                    for tq in range(2):
                        mm = pe.matmul(bank(2 + e, tq * T, (tq + 1) * T),
                                       qkv(parity, 0)[rows, tq * P:(tq + 1) * P],
                                       qkv(parity, 1)[rows, :], start=True, stop=True)
                mm.then_inc(na_qk, 1)
                wait(pe, na_v_copied, s.times(1))
                for tk in range(2):
                    mm = pe.transpose(bank(6, tk * P, (tk + 1) * P),
                                      qkv(parity, 2)[:, tk * P:(tk + 1) * P], ident[:])
                mm.then_inc(na_vt_done, 1)

            def na_turn(s):
                pe.wait_ge(na_probs, s.times(1, 1))
                wait(pe, na_pt_copied, s.times(2))
                for e in range(2):
                    for tk in range(2):
                        for tq in range(2):
                            a = (2 * e + tq) * T + tk * P
                            mm = pe.transpose(bank(4 + e, tk * T + tq * P, tk * T + (tq + 1) * P),
                                              na_s[:, a:a + P], ident[:])
                mm.then_inc(na_pt_done, 1)

            def na_values(s):
                pe.wait_ge(na_pt_copied, s.times(2, 2))
                pe.wait_ge(na_v_copied, s.times(1, 1))
                wait(pe, na_lo, s.times(1))
                for e in range(2):
                    for tk in range(2):
                        mm = pe.matmul(bank(7, 0, T, 64 * e, 64 * e + 64),
                                       na_v[:, tk * P + 64 * e:tk * P + 64 * e + 64],
                                       na_pt[:, (2 * e + tk) * T:(2 * e + tk + 1) * T],
                                       start=tk == 0, stop=tk == 1, skip_group_check=True)
                mm.then_inc(na_pv, 1)

            def na_step(s, slot, parity, prev2):
                t = Pos(s.const * 6, s.per * 6, s.i)
                if prev2:
                    na_values(s + -2)
                na_scores(s + -1, 1 - parity)
                na_block(s, 0, t, slot, parity)
                na_block(s, 1, t + 2, slot + 2, parity)
                na_turn(s + -1)
                na_block(s, 2, t + 4, slot + 4, parity)

            for k in range(3):
                na_block(Pos(0), k, Pos(2 * k), 2 * k, 0)
            na_step(Pos(1), 6, 1, False)
            na_step(Pos(2), 0, 0, True)
            na_step(Pos(3), 2, 1, True)
            with pe.Fori(0, (NA_PAIRS - 4) // 2) as i:
                na_step(Pos(4, 2, i), 0, 0, True)
                na_step(Pos(5, 2, i), 2, 1, True)

            def gla_block(b, t, slot, n):
                wait(pe, proj_taken, b.times(1, -1))
                two_tiles(t, slot, bank(n % 2, 0, T), xs)

            B0 = 3 * NA_PAIRS
            na_values(Pos(NA_PAIRS - 2))
            na_scores(Pos(NA_PAIRS - 1), 1)
            gla_block(Pos(B0), Pos(T_RANK), T_RANK, B0)
            gla_block(Pos(B0 + 1), Pos(T_GLA), T_GLA, B0 + 1)
            na_turn(Pos(NA_PAIRS - 1))
            gla_block(Pos(B0 + 2), Pos(T_GLA + 2), T_GLA + 2, B0 + 2)
            na_values(Pos(NA_PAIRS - 1))
            gla_block(Pos(B0 + 3), Pos(T_GLA + 4), T_GLA + 4, B0 + 3)
            gla_block(Pos(B0 + 4), Pos(T_GLA + 6), T_GLA + 6, B0 + 4)
            B1 = B0 + 5

            def decay_inputs(h):
                pe.wait_ge(up_landed, h.times(16, 16))
                pe.wait_ge(consts_ready, 2)
                pe.wait_ge(proj_taken, B0 + 1)
                for d in range(2):
                    for kb in range(NKB):
                        mm = pe.matmul(bank(2 + d, kb * T, (kb + 1) * T),
                                       g_up[32 * d:32 * d + 32, kb * P:(kb + 1) * P],
                                       g_rank[32 * d:32 * d + 32, :], start=True, stop=True)
                mm.then_inc(la_done, 1)

            def turn_outputs(h):
                pe.wait_ge(on_done, h.times(1, 1))
                if h.i is not None or h.const < GLA_HEADS - 1:
                    pe.wait_ge(z_done, h.times(1, 2))
                for vb in range(NVB):
                    for tt in range(2):
                        mm = pe.transpose(bank(2 + vb // 2, vb % 2 * T + tt * P, vb % 2 * T + (tt + 1) * P),
                                          g_on[:, tt * DV + vb * P:tt * DV + (vb + 1) * P], ident[:])
                mm.then_inc(ot_done, 1)

            def intra(h):
                pe.wait_ge(decayed, h.times(1, 1))
                wait(pe, gated, h.times(1))
                pe.wait_ge(z_done, h.times(1, 1))
                for d in range(2):
                    for tt in range(2):
                        for kb in range(NKB):
                            a = (d * NKB + kb) * T + tt * P
                            mm = pe.transpose(bank(2 + d, tt * DK + kb * P, tt * DK + (kb + 1) * P),
                                              g_ks[:, a:a + P], ident[:])
                mm.then_inc(kt_done, 1)
                for d in range(2):
                    for n in range(N_CHUNKS):
                        rows, tt = 64 * (n % 2), n // 2
                        dst = bank(4, (d * 2 + tt) * CHUNK, (d * 2 + tt + 1) * CHUNK, rows, rows + 64)
                        for kb in range(NKB):
                            a = (d * NKB + kb) * T + n * CHUNK
                            mm = pe.matmul(dst, g_ki[:, a:a + CHUNK], g_qd[:, a:a + CHUNK],
                                           start=kb == 0, stop=kb == NKB - 1, skip_group_check=True)
                mm.then_inc(att_done, 1)

            def turn_values(h, b):
                pe.wait_ge(proj_taken, b)
                pe.wait_ge(kt_copied, h.times(2, 2))
                for tt in range(2):
                    for vb in range(NVB):
                        mm = pe.transpose(bank(2 + tt, vb * P, (vb + 1) * P),
                                          g_vt[:, vb * T + tt * P:vb * T + (tt + 1) * P], ident[:])
                mm.then_inc(vt_done, 1)

            def recur(h, m):
                if m == 0:
                    pe.wait_ge(v_copied, h.times(2, 2))
                    pe.wait_ge(att_masked, h.times(1, 1))
                    wait(pe, on_done, h.times(1))
                    for tt in range(2):
                        pe.matmul(bank(6 + tt), zeros[:], zeros[:].unsqueeze(1).to_broadcast([P, 4, P]),
                                  start=True, stop=False, skip_group_check=True)
                    for n in range(N_CHUNKS):
                        r0, tt = 64 * (n % 2), n // 2
                        pe.matmul(bank(6 + tt, 0, DV, r0, r0 + 64),
                                  g_att[r0:r0 + 64, tt * CHUNK:(tt + 1) * CHUNK],
                                  g_v[r0:r0 + 64, tt * DV:(tt + 1) * DV],
                                  start=False, stop=False, skip_group_check=True)
                else:
                    pe.wait_ge(state_done, h.times(3, m))
                for d in range(2):
                    n = m if d == 0 else N_CHUNKS - 1 - m
                    r0, tt = 64 * (n % 2), n // 2
                    if m > 0:
                        for kb in range(NKB):
                            a = (d * NKB + kb) * T + n * CHUNK
                            mm = pe.matmul(bank(6 + tt, 0, DV, r0, r0 + 64), g_qd[:, a:a + CHUNK],
                                           g_state[:, (d * NKB + kb) * DV:(d * NKB + kb + 1) * DV],
                                           start=False, stop=False, skip_group_check=True)
                if m < N_CHUNKS - 1:
                    for d in range(2):
                        n = m if d == 0 else N_CHUNKS - 1 - m
                        r0, tt = 64 * (n % 2), n // 2
                        for kb in range(NKB):
                            a = (d * 2 + tt) * DK + kb * P
                            mm = pe.matmul(bank(2 + d * NKB + kb), g_kt[r0:r0 + 64, a:a + P],
                                           g_v[r0:r0 + 64, tt * DV:(tt + 1) * DV],
                                           start=True, stop=True, skip_group_check=True)
                    mm.then_inc(gain_done, 1)
                else:
                    mm.then_inc(o_done, 1)

            def gla_head(h, t, b, last, first):
                decay_inputs(h)
                for k in range(8 if last else 12):
                    if k == 2 and not first:
                        turn_outputs(h + -1)
                    if k == 4:
                        intra(h)
                    if k == 5:
                        turn_values(h, b.times(1, 4))
                    if k == 7:
                        recur(h, 0)
                    if k == 9:
                        recur(h, 1)
                    if k == 10:
                        recur(h, 2)
                    gla_block(b + k, t + 2 * k, T_GLA + QK_TILES + 2 * k, B1 + k)
                for m in ((1, 2, 3) if last else (3,)):
                    recur(h, m)

            gla_head(Pos(0), Pos(T_GLA + QK_TILES), Pos(B1), False, True)
            with pe.Fori(0, GLA_HEADS - 2) as i:
                gla_head(Pos(1, 1, i), Pos(T_GLA + QK_TILES + HEAD_TILES, HEAD_TILES, i),
                         Pos(B1 + 12, 12, i), False, False)
            H = GLA_HEADS - 1
            gla_head(Pos(H), Pos(T_GLA + QK_TILES + H * HEAD_TILES), Pos(B1 + 12 * H), True, False)
            turn_outputs(Pos(H))

            def merge_step(c, t, slot, parity):
                wait(pe, merged, c.times(1, -1))
                b = 4 * parity
                two_tiles(t, slot, bank(b, 0, T), xs)
                half_block(t + 2, slot + 2, bank(b + 1, 0, T), nas, True, True)
                two_tiles(t + 3, slot + 3, bank(b + 2, 0, T), xs)
                two_tiles(t + 5, slot + 5, bank(b + 3, 0, T), gls)

            pe.wait_ge(proj_taken, B1 + 12 * GLA_HEADS - 4)
            pe.wait_ge(o_lo, GLA_HEADS)
            for k in range(4):
                merge_step(Pos(k), Pos(T_MERGE + 7 * k), T_MERGE + 7 * k, k % 2)
            with pe.Fori(0, KC // 4 - 1) as i:
                for k in range(4):
                    merge_step(Pos(4 + k, 4, i), Pos(T_MERGE + 28 + 7 * k, 28, i), T_MERGE + 7 * k, k % 2)

            pe.wait_ge(m_lo, KC)

            by_token(T_OUT, ms)

            pe.wait_ge(p_lo, 1)
            for half in range(2):
                pe.wait_ge(res_done, 4 * (half + 1))
                for k in range(2):
                    products_by_token(Pos(T_PLE + 2 * half + k), T_PLE + 2 * half + k,
                                      ys[:, k * 2 * T:(k + 1) * 2 * T],
                                      lambda tt, n: bank(4 * tt + 2 * half + n), k == 0, k == 1)
            pe.wait_ge(ple_taken, 8)
            turn_normed(1, tok)
            pe.wait_ge(ln_lo, 8)

            pe.wait_ge(keys_landed, 16)

            def query_block(c, t, slot, parity):
                wait(pe, pq_taken, c.times(1, -1))
                two_tiles(t, slot, bank(parity, 0, T), xs)

            def key_scores(c, parity):
                pe.wait_ge(pq_taken, c.times(1, 1))
                wait(pe, sc_taken, c.times(1, -1))
                for tt in range(2):
                    a = parity * T + tt * P
                    mm = pe.matmul(bank(2 + parity, tt * NKEYS, (tt + 1) * NKEYS), pq[:, a:a + P],
                                   key_t[:, ds(c.times(NKEYS), NKEYS)], start=True, stop=True)
                mm.then_inc(sc_done, 1)

            query_block(Pos(0), Pos(T_PQ), T_PQ, 0)
            query_block(Pos(1), Pos(T_PQ + 2), T_PQ + 2, 1)
            key_scores(Pos(0), 0)

            def two_queries(c, t):
                query_block(c, t, T_PQ, 0)
                key_scores(c + -1, 1)
                query_block(c + 1, t + 2, T_PQ + 2, 1)
                key_scores(c, 0)

            two_queries(Pos(2), Pos(T_PQ + 4))
            with pe.Fori(0, KC // 2 - 2) as i:
                two_queries(Pos(4, 2, i), Pos(T_PQ + 8, 4, i))
            key_scores(Pos(KC - 1), 1)

            pe.wait_ge(sc_taken, HP)
            by_token(T_PGATE, xs)

            pe.wait_ge(gsig, 4)

            def hidden(j, t, slot, n):
                wait(pe, gelu_done, j.times(1, -1))
                two_tiles(t, slot, bank(n % 2, 0, T), xs)

            for n in range(4):
                hidden(Pos(n), Pos(T_U + 2 * n), T_U + 2 * n, n)
            with pe.Fori(0, 15) as i:
                for n in range(4):
                    hidden(Pos(4 + n, 4, i), Pos(T_U + 8 + 2 * n, 8, i), T_U + 2 * n, n)
            pe.wait_ge(ex_done, 16)
            pe.wait_ge(gsig, 8)
            for tt in range(2):
                for k, src in enumerate((ex[:, 0:2 * P], ex[:, 2 * P:4 * P], exg)):
                    mm = pe.transpose(bank(2 + k // 2, k % 2 * T + tt * P, k % 2 * T + (tt + 1) * P),
                                      src[:, tt * P:(tt + 1) * P], ident[:])
            mm.then_inc(ex_t_done, 1)

            def spread_gates(g, n):
                pe.wait_ge(hot_ready, g.times(8, 8))
                wait(pe, gate_taken, g.times(1, -1))
                for q in range(4):
                    mm = pe.matmul(bank(2 + n % 2, q * NKEYS, (q + 1) * NKEYS),
                                   hot0[:, q * NKEYS:(q + 1) * NKEYS], hot1[:, q * NKEYS:(q + 1) * NKEYS],
                                   start=True, stop=True)
                mm.then_inc(gate_mm, 1)

            pe.wait_ge(ex_t_taken, 3)
            for n in range(4):
                hidden(Pos(64 + n), Pos(T_U + 128 + 2 * n), T_U + 2 * n, n)
                spread_gates(Pos(n), n)
            with pe.Fori(0, 15) as i:
                for n in range(4):
                    hidden(Pos(68 + n, 4, i), Pos(T_U + 136 + 2 * n, 8, i), T_U + 2 * n, n)
                    spread_gates(Pos(4 + n, 4, i), n)

            pe.wait_ge(gelu_done, NKEYS)
            pe.wait_ge(gate_taken, T // 4)
            for n in range(8):
                pe.matmul(bank(n), zeros[:], zeros[:].unsqueeze(1).to_broadcast([P, 4, P]),
                          start=True, stop=False, skip_group_check=True)

            def expert_out(j, t, slot, parity):
                pe.wait_ge(w_lo, j.times(1, 1))
                for half in range(2):
                    products_by_token(t + half, slot + half, ys[:, parity * 2 * T:(parity + 1) * 2 * T],
                                      lambda tt, n: bank(4 * tt + 2 * half + n), False, False)

            with pe.Fori(0, NKEYS // 2) as i:
                expert_out(Pos(0, 2, i), Pos(T_V, 4, i), T_V, 0)
                expert_out(Pos(1, 2, i), Pos(T_V + 2, 4, i), T_V + 2, 1)


        @block.scalar
        def _(act):
            def upper(t, slot):
                act.wait_ge(landed[slot % RING], t.over(RING).times(16, 16))
                s = slice(slot % RING * TILE, (slot % RING + 1) * TILE)
                act.activation(w_up[:, s], w_in[:, s], ACT.Copy).then_inc(hi_ready, 1)

            def hi(t, slot):
                if t.i is not None or t.const + AHEAD < T_END:
                    upper(t + AHEAD, slot + AHEAD)

            def std(n, tt):
                act.wait_ge(ln_var, 2 * n + tt + 1)
                act.activation(ln_sd[:, 2 * tt:2 * tt + 1], ln_mv[:, 2 * tt + 1:2 * tt + 2], ACT.Sqrt,
                               bias=eps_t[:]).then_inc(ln_std, 1)

            def features(n, dst):
                act.wait_ge(ln_turned, 2 * n + 2)
                for g in range(5):
                    if g < 4:
                        for c in range(4 * g, 4 * g + 2):
                            ins = act.activation(dst[:, c * T:(c + 1) * T], bank(c // 2, c % 2 * T, (c % 2 + 1) * T),
                                                 ACT.Identity, scale=vec[:, V_LN + 2 * n * KC + c:V_LN + 2 * n * KC + c + 1],
                                                 bias=vec[:, V_LN + (2 * n + 1) * KC + c:V_LN + (2 * n + 1) * KC + c + 1])
                        ins.then_inc(ln_part_a, 1)
                    if g > 0:
                        act.wait_ge(ln_part_a, 4 * n + g)
                        act.wait_ge(ln_part_d, 4 * n + g)
                        up = xs[:, (g - 1) * 8 * T:g * 8 * T].rearrange("p (c s t) -> p c s t", c=4, s=2)[:, :, 0, :]
                        src = dst[:, (g - 1) * 4 * T:g * 4 * T].rearrange("p (c t) -> p c t", c=4)
                        act.activation(up, src, ACT.Copy).then_inc(ln_hi, 1)

            act.wait_ge(consts_ready, 1)
            std(0, 0)
            for k in range(AHEAD):
                upper(Pos(k), k)
            std(0, 1)
            hi(Pos(0), 0)
            hi(Pos(1), 1)

            act.wait_ge(vec_landed, 16)
            features(0, x_feat)

            def na_take(s, k, t, parity):
                act.wait_ge(tile_used, t.times(1, 2))
                if k == 0:
                    wait(act, na_pv, s.times(1, -1))
                    if s.i is None and s.const < 2:
                        act.wait_ge(ln_lo, 4)
                a = (parity * 3 + k) * T
                act.activation(na_qkv[:, a:a + T], bank((3 * parity + k) % 2, 0, T), ACT.Identity,
                               bias=vec[:, ds(s.times(3, V_NA + k), 1)]).then_inc(proj_taken, 1)

            def na_exps(s):
                act.wait_ge(na_negmax, s.times(1, 1))
                for k in range(4):
                    act.activation(na_s[:, k * T:(k + 1) * T], na_s[:, k * T:(k + 1) * T], ACT.Exp,
                                   bias=na_small[:, 4 + k:5 + k],
                                   accum_out=na_small[:, 8 + k:9 + k]).then_inc(na_exp, 1)
                act.wait_ge(na_vt_done, s.times(1, 1))
                wait(act, na_pv, s.times(1))
                act.activation(na_v[:], bank(6, 0, 2 * P), ACT.Copy).then_inc(na_v_copied, 1)

            def na_norm(s):
                act.wait_ge(na_rinv, s.times(1, 1))
                act.wait_ge(na_exp, s.times(4, 4))
                for k in range(4):
                    ins = act.activation(na_s[:, k * T:(k + 1) * T], na_s[:, k * T:(k + 1) * T],
                                         ACT.Copy, scale=na_small[:, 12 + k:13 + k])
                ins.then_inc(na_probs, 1)

            def na_out(s):
                act.wait_ge(na_pv, s.times(1, 1))
                act.activation(nas[:, ds(s.times(2 * T), T)], bank(7, 0, T), ACT.Copy).then_inc(na_hi, 1)

            def na_step(s, slot, parity, prev2):
                t = Pos(s.const * 6, s.per * 6, s.i)
                hi(t, slot)
                na_take(s + -1, 2, t + -2, 1 - parity)
                if prev2:
                    na_out(s + -2)
                hi(t + 1, slot + 1)
                na_exps(s + -1)
                hi(t + 2, slot + 2)
                na_take(s, 0, t, parity)
                hi(t + 3, slot + 3)
                na_norm(s + -1)
                hi(t + 4, slot + 4)
                na_take(s, 1, t + 2, parity)
                hi(t + 5, slot + 5)

            hi(Pos(2), 2)
            na_take(Pos(0), 0, Pos(0), 0)
            hi(Pos(3), 3)
            hi(Pos(4), 4)
            na_take(Pos(0), 1, Pos(2), 0)
            hi(Pos(5), 5)
            na_step(Pos(1), 6, 1, False)
            with act.Fori(0, (NA_PAIRS - 2) // 2) as i:
                na_step(Pos(2, 2, i), 0, 0, True)
                na_step(Pos(3, 2, i), 2, 1, True)

            B0 = 3 * NA_PAIRS
            B1 = B0 + 5
            chain = Chain(act, gla_act, 6)

            def take(dst, n, t, col):
                act.wait_ge(tile_used, t.times(1, 2))
                act.activation(dst, bank(n % 2, 0, T), ACT.Identity,
                               bias=vec[:, ds(col.times(1), 1)]).then_inc(proj_taken, 1)

            def take_gate(vb, n, t, col):
                act.wait_ge(tile_used, t.times(1, 2))
                a, b = vb * T, (vb + 1) * T
                act.activation(g_x[:, a:b], bank(n % 2, 0, T), ACT.Identity,
                               bias=vec[:, ds(col.times(1), 1)])
                act.activation(g_sg[:, a:b], bank(n % 2, 0, T), ACT.Sigmoid,
                               bias=vec[:, ds(col.times(1), 1)]).then_inc(proj_taken, 1)

            def decay_logs(h):
                chain.begin(h)
                act.wait_ge(la_done, h.times(1, 1))
                for k in range(4):
                    chain.step(act.activation(g_z[:, k * T:(k + 1) * T],
                                              bank(2 + k // 2, k % 2 * T, (k % 2 + 1) * T), ACT.Identity,
                                              bias=vec[:, ds(h.times(4, V_DECAY + k), 1)]))
                chain.step(act.activation(g_a[:], g_z[:], ACT.Abs))
                chain.step(act.activation(g_a[:], g_a[:], ACT.Exp, scale=-1.0))
                act.activation(g_a[:], g_a[:], ACT.Ln, bias=1.0).then_inc(z_done, 1)
                chain.end()

            def decay_exps(h):
                act.wait_ge(gap_done, h.times(1, 1))
                wait(act, o_done, h.times(1))
                act.activation(g_qd[:], g_c[:], ACT.Exp, scale=1.0 / 16)
                act.activation(g_ki[:], g_c[:], ACT.Exp, scale=-1.0 / 16)
                act.activation(g_ks[:], g_a[:], ACT.Exp, scale=1.0 / 16)
                c = g_c[:].rearrange("p (d k c) -> p d k c", d=2, c=CHUNK)
                dec = g_dec[:].rearrange("p (d k c) -> p d k c", d=2, c=1)
                act.activation(dec[:, 0], c[:, 0, :, CHUNK - 1:CHUNK], ACT.Exp, scale=1.0 / 16)
                act.activation(dec[:, 1], c[:, 1, :, 0:1], ACT.Exp, scale=1.0 / 16).then_inc(exp_done, 1)

            def keys_taken(h):
                act.wait_ge(kt_done, h.times(1, 1))
                for d in range(2):
                    act.activation(g_kt[:, d * 2 * DK:(d + 1) * 2 * DK], bank(2 + d),
                                   ACT.Copy).then_inc(kt_copied, 1)

            def values_taken(h):
                act.wait_ge(vt_done, h.times(1, 1))
                for tt in range(2):
                    act.activation(g_v[:, tt * DV:(tt + 1) * DV], bank(2 + tt), ACT.Copy).then_inc(v_copied, 1)

            def out_rms(h):
                act.wait_ge(o_done, h.times(1, 1))
                for tt in range(2):
                    ins = act.activation(g_on[:, tt * DV:(tt + 1) * DV], bank(6 + tt), ACT.Square,
                                         accum_out=g_small[:, tt:tt + 1])
                ins.then_inc(rms_done, 1)
                act.wait_ge(rms_done, h.times(2, 1))
                act.activation(g_small[:, 2:4], g_small[:, 0:2], ACT.Sqrt, bias=eps_t[:],
                               scale=1.0 / DV).then_inc(rms_done, 1)

            def out_hi(h):
                act.wait_ge(gated, h.times(1, 1))
                dst = gls[:, ds(h.times(NVB * 2 * T), NVB * 2 * T)].rearrange(
                    "p (c s t) -> p c s t", c=NVB, s=2)[:, :, 0, :]
                act.activation(dst, g_ot[:].rearrange("p (c t) -> p c t", c=NVB), ACT.Copy).then_inc(o_hi, 1)

            NL = NA_PAIRS - 1
            hi(Pos(T_RANK), T_RANK)
            na_take(Pos(NL), 2, Pos(T_RANK - 2), NL % 2)
            na_out(Pos(NL - 1))
            hi(Pos(T_RANK + 1), T_RANK + 1)
            na_exps(Pos(NL))
            hi(Pos(T_RANK + 2), T_RANK + 2)
            na_norm(Pos(NL))
            hi(Pos(T_RANK + 3), T_RANK + 3)

            def gla_take(h, k, n, t):
                col = Pos(V_GLA + k + GLA_BLOCKS * h.const, GLA_BLOCKS * h.per, h.i)
                if k < 2:
                    take(g_q[:, k * T:(k + 1) * T], n, t, col)
                elif k < 4:
                    take(g_k[:, (k - 2) * T:(k - 1) * T], n, t, col)
                elif k < 8:
                    take(g_vt[:, (k - 4) * T:(k - 3) * T], n, t, col)
                else:
                    take_gate(k - 8, n, t, col)

            act.wait_ge(h_spilled, 32)
            take(g_rank[:], B0, Pos(T_RANK), Pos(V_RANK))
            hi(Pos(T_GLA + 2), T_GLA + 2)
            gla_take(Pos(0), 0, B0 + 1, Pos(T_GLA))
            hi(Pos(T_GLA + 3), T_GLA + 3)
            hi(Pos(T_GLA + 4), T_GLA + 4)
            gla_take(Pos(0), 1, B0 + 2, Pos(T_GLA + 2))
            na_out(Pos(NL))
            hi(Pos(T_GLA + 5), T_GLA + 5)
            hi(Pos(T_GLA + 6), T_GLA + 6)
            gla_take(Pos(0), 2, B0 + 3, Pos(T_GLA + 4))
            hi(Pos(T_GLA + 7), T_GLA + 7)

            def gla_head(h, t, last, first):
                s0 = T_GLA + QK_TILES
                for k in range(8 if last else 12):
                    if k == 6:
                        values_taken(h)
                    hi(t + 2 * k, s0 + 2 * k)
                    if k == 0:
                        gla_take(h, 3, B1 - 1, t + -2)
                    elif k <= 8:
                        gla_take(h, 3 + k, B1 + k - 1, t + 2 * (k - 1))
                    else:
                        gla_take(h + 1, k - 9, B1 + k - 1, t + 2 * (k - 1))
                    hi(t + 2 * k + 1, s0 + 2 * k + 1)
                    if k == 0:
                        if not first:
                            out_rms(h + -1)
                        decay_logs(h)
                    if k == 2:
                        decay_exps(h)
                    if k == 3 and not first:
                        out_hi(h + -1)
                    if k == 4:
                        keys_taken(h)

            s_h = T_GLA + QK_TILES
            gla_head(Pos(0), Pos(s_h), False, True)
            with act.Fori(0, GLA_HEADS - 2) as i:
                gla_head(Pos(1, 1, i), Pos(s_h + HEAD_TILES, HEAD_TILES, i), False, False)
            H = GLA_HEADS - 1
            gla_head(Pos(H), Pos(s_h + H * HEAD_TILES), True, False)
            hi(Pos(T_MERGE), T_MERGE)
            gla_take(Pos(H), 11, B1 + 7, Pos(T_MERGE - 2))
            hi(Pos(T_MERGE + 1), T_MERGE + 1)
            out_rms(Pos(H))
            out_hi(Pos(H))

            def sigmoid(dst, parity, n, t, col, done, c, freed):
                act.wait_ge(tile_used, t.times(1, 2))
                wait(act, freed, c.times(1, -1))
                act.activation(dst[:, parity * T:(parity + 1) * T], bank(4 * parity + n, 0, T),
                               ACT.Sigmoid, bias=vec[:, ds(col.times(1), 1)]).then_inc(done, 1)

            def merged_hi(c, parity):
                act.wait_ge(merged, c.times(1, 1))
                act.activation(ms[:, ds(c.times(2 * T), T)], m_m[:, parity * T:(parity + 1) * T],
                               ACT.Copy).then_inc(m_hi, 1)

            def merge_step(c, t, slot, parity, prev, ahead=0):
                for k in range(ahead, MERGE_TILES):
                    hi(t + k, slot + k)
                    if k == 3:
                        sigmoid(m_sa, parity, 0, t, Pos(V_GATES + 2 * c.const, 2 * c.per, c.i),
                                sig_a, c, a_gated)
                        if prev:
                            merged_hi(c + -1, 1 - parity)
                    if k == 6:
                        sigmoid(m_sb, parity, 2, t + 3, Pos(V_GATES + 1 + 2 * c.const, 2 * c.per, c.i),
                                sig_b, c, merged)

            for k in range(4):
                merge_step(Pos(k), Pos(T_MERGE + 7 * k), T_MERGE + 7 * k, k % 2, k > 0, 0 if k else 2)
            with act.Fori(0, KC // 4 - 1) as i:
                for k in range(4):
                    merge_step(Pos(4 + k, 4, i), Pos(T_MERGE + 28 + 7 * k, 28, i), T_MERGE + 7 * k,
                               k % 2, True)
            hi(Pos(T_OUT), T_OUT)
            hi(Pos(T_OUT + 1), T_OUT + 1)
            merged_hi(Pos(KC - 1), 1)

            for k in range(2, 4):
                hi(Pos(T_OUT + k), T_OUT + k)
            act.wait_ge(p_landed, 16)
            p_dst = ys[:].rearrange("p (c s t) -> p c s t", c=2, s=2)[:, :, 0, :]
            act.activation(p_dst, p_in[:].rearrange("p (c t) -> p c t", c=2), ACT.Copy).then_inc(p_hi, 1)
            with act.Fori(0, 7) as i:
                for k in range(4):
                    hi(Pos(T_OUT + 4 + k, 4, i), T_OUT + k)

            def take_ple(half):
                act.wait_ge(tile_used, T_PLE + 2 * (half + 1))
                for tt in range(2):
                    for n in range(2):
                        a = tt * D + half * 1024 + n * 512
                        act.activation(ple[:, a:a + 512], bank(4 * tt + 2 * half + n),
                                       ACT.Copy).then_inc(ple_taken, 1)

            for k in range(3):
                hi(Pos(T_PLE + k), T_PLE + k)
            std(1, 0)
            take_ple(0)
            std(1, 1)
            hi(Pos(T_PLE + 3), T_PLE + 3)
            take_ple(1)
            hi(Pos(T_PQ), T_PQ)
            hi(Pos(T_PQ + 1), T_PQ + 1)
            features(1, h_feat)

            def take_query(c, t, parity):
                act.wait_ge(tile_used, t.times(1, 2))
                wait(act, sc_done, c.times(1, -1))
                act.activation(pq[:, parity * T:(parity + 1) * T], bank(parity, 0, T),
                               ACT.Copy).then_inc(pq_taken, 1)

            def take_scores(c, parity):
                act.wait_ge(sc_done, c.times(1, 1))
                for tt in range(2):
                    ins = act.activation(sc[:, ds(c.times(NKEYS, tt * HP * NKEYS), NKEYS)],
                                         bank(2 + parity, tt * NKEYS, (tt + 1) * NKEYS), ACT.Copy)
                ins.then_inc(sc_taken, 1)

            hi(Pos(T_PQ + 2), T_PQ + 2)
            take_query(Pos(0), Pos(T_PQ), 0)
            hi(Pos(T_PQ + 3), T_PQ + 3)

            def two_queries(c, t):
                hi(t + 2, T_PQ)
                take_query(c, t, 1)
                take_scores(c + -1, 0)
                hi(t + 3, T_PQ + 1)
                hi(t + 4, T_PQ + 2)
                take_query(c + 1, t + 2, 0)
                take_scores(c, 1)
                hi(t + 5, T_PQ + 3)

            two_queries(Pos(1), Pos(T_PQ + 2))
            with act.Fori(0, KC // 2 - 2) as i:
                two_queries(Pos(3, 2, i), Pos(T_PQ + 6, 4, i))
            hi(Pos(T_PGATE), T_PGATE)
            take_query(Pos(KC - 1), Pos(T_PQ + 30), 1)
            take_scores(Pos(KC - 2), 0)
            take_scores(Pos(KC - 1), 1)

            def take_ple_gate(half, n):
                act.wait_ge(tile_used, T_PGATE + KC * (half + 1))
                q = 4 * half + n
                wait(act, res2_done, q - 1)
                act.activation(sgm[:, q % 2 * 512:(q % 2 + 1) * 512], bank(4 * (n // 2) + 2 * half + n % 2),
                               ACT.Sigmoid).then_inc(gsig, 1)

            for k in range(1, 4):
                hi(Pos(T_PGATE + k), T_PGATE + k)
            with act.Fori(0, 3) as i:
                for k in range(4):
                    hi(Pos(T_PGATE + 4 + k, 4, i), T_PGATE + k)
            for k in range(16, 32):
                hi(Pos(T_PGATE + k), T_PGATE + k)
                if 17 <= k < 21:
                    take_ple_gate(0, k - 17)

            def gelu(j, t, n):
                act.wait_ge(tile_used, t.times(1, 2))
                wait(act, gelu_stored[n], j.over(4).times(16))
                act.activation(gst[:, n * T:(n + 1) * T], bank(n % 2, 0, T), ACT.Gelu).then_inc(gelu_done, 1)

            def gate_exp(u):
                act.wait_ge(tk_neg, u.times(1, 1))
                act.activation(tk_g[:], tk_cv[:], ACT.Exp, bias=tk_s[:, 0:1],
                               accum_out=tk_s[:, 1:2]).then_inc(tk_exp, 1)

            def take_gates(g, n):
                act.wait_ge(gate_mm, g.times(1, 1))
                act.activation(gates[:, ds(g.times(4 * NKEYS), 4 * NKEYS)], bank(2 + n % 2),
                               ACT.Copy).then_inc(gate_taken, 1)

            def hidden_steps(j, t, first, unit=None, group=None):
                for n in range(4):
                    hi(t + 2 * n, T_U + 2 * n)
                    if first:
                        take_ple_gate(1, n)
                    if n > 0 or not first:
                        gelu(j + (n - 1), t + (2 * n - 2), (n - 1) % 4)
                    if group is not None and (n > 0 or not first):
                        take_gates(group + (n - 1), (n - 1) % 4)
                    hi(t + 2 * n + 1, T_U + 2 * n + 1)
                    if unit is not None and n == 3:
                        gate_exp(unit)

            hidden_steps(Pos(0), Pos(T_U), True, unit=Pos(0))
            hidden_steps(Pos(4), Pos(T_U + 8), False, unit=Pos(1))
            with act.Fori(0, 14) as i:
                hidden_steps(Pos(8, 4, i), Pos(T_U + 16, 8, i), False, unit=Pos(2, 1, i))
            hi(Pos(T_U + 128), T_U)
            gelu(Pos(63), Pos(T_U + 126), 3)
            act.wait_ge(ex_t_done, 1)
            for k, dst in enumerate((idx0_t, idx1_t, gate_t)):
                act.activation(dst[:], bank(2 + k // 2, k % 2 * T, (k % 2 + 1) * T),
                               ACT.Copy).then_inc(ex_t_taken, 1)
            hi(Pos(T_U + 129), T_U + 1)
            for n in range(1, 4):
                hi(Pos(T_U + 128 + 2 * n), T_U + 2 * n)
                gelu(Pos(63 + n), Pos(T_U + 126 + 2 * n), n - 1)
                if n == 1:
                    act.wait_ge(res_spilled, 32)
                take_gates(Pos(n - 1), n - 1)
                hi(Pos(T_U + 129 + 2 * n), T_U + 2 * n + 1)
            with act.Fori(0, 15) as i:
                hidden_steps(Pos(68, 4, i), Pos(T_U + 136, 8, i), False, group=Pos(4, 4, i))
            hi(Pos(T_V), T_V)
            gelu(Pos(127), Pos(T_U + 254), 3)
            take_gates(Pos(63), 3)
            hi(Pos(T_V + 1), T_V + 1)

            def weight_hi(j, parity):
                act.wait_ge(w_ready, j.times(1, 1))
                if j.i is not None or j.const >= 2:
                    act.wait_ge(tile_used, j.times(2, T_V - 2))
                act.activation(ys[:, parity * 2 * T:parity * 2 * T + T],
                               wexp[:, parity * T:(parity + 1) * T], ACT.Copy).then_inc(w_hi, 1)

            weight_hi(Pos(0), 0)
            weight_hi(Pos(1), 1)
            for k in range(2 + AHEAD, 4):
                upper(Pos(T_V + k), T_V + k)
            with act.Fori(0, NKEYS // 2 - 1) as i:
                for k in range(2):
                    upper(Pos(T_V + 4 + 2 * k, 4, i), T_V + 2 * k)
                    weight_hi(Pos(2 + k, 2, i), k)
                    upper(Pos(T_V + 5 + 2 * k, 4, i), T_V + 2 * k + 1)
            for tt in range(2):
                std(2, tt)

        @block.vector
        def _(dve):
            def lower(t, slot):
                dve.wait_ge(hi_ready, t.times(1, 1))
                s = slice(slot % RING * TILE, (slot % RING + 1) * TILE)
                dve.tensor_tensor(w_low[:, s], w_in[:, s], w_up[:, s].bitcast(F32),
                                  ALU.subtract).then_inc(split_ready, 1)

            def lo(t, slot):
                if t.i is not None or t.const + AHEAD < T_END:
                    lower(t + AHEAD, slot + AHEAD)

            ln_c = Line(dve, ln_chain)

            def stats(x, tt, q):
                return dve.bn_stats(ln_st[:, (tt * 4 + q) * 6:(tt * 4 + q + 1) * 6],
                                    x[:, tt * D + q * 512:tt * D + (q + 1) * 512])

            def mean_var(tt):
                dve.bn_aggr(ln_mv[:, 2 * tt:2 * tt + 2], ln_st[:, tt * 24:(tt + 1) * 24]).then_inc(ln_var, 1)

            def inverse_std(n, tt):
                dve.wait_ge(ln_std, 2 * n + tt + 1)
                dve.wait_ge(ln_var, 2 * n + tt + 1)
                ln_c.step(dve.reciprocal(ln_sd[:, 2 * tt + 1:2 * tt + 2], ln_sd[:, 2 * tt:2 * tt + 1]))

            def normalize(n, x, tt):
                inverse_std(n, tt)
                v = x[:, tt * D:(tt + 1) * D]
                dve.tensor_scalar(v, v, ln_mv[:, 2 * tt:2 * tt + 1], ln_sd[:, 2 * tt + 1:2 * tt + 2],
                                  ALU.subtract, ALU.mult).then_inc(ln_normed, 1)

            def features(n, dst):
                dve.wait_ge(ln_turned, 2 * n + 2)
                for g in range(5):
                    if g < 4:
                        for c in range(4 * g + 2, 4 * g + 4):
                            ins = dve.tensor_scalar(dst[:, c * T:(c + 1) * T], bank(c // 2, c % 2 * T, (c % 2 + 1) * T),
                                                    vec[:, V_LN + 2 * n * KC + c:V_LN + 2 * n * KC + c + 1],
                                                    vec[:, V_LN + (2 * n + 1) * KC + c:V_LN + (2 * n + 1) * KC + c + 1],
                                                    ALU.mult, ALU.add)
                        ins.then_inc(ln_part_d, 1)
                    if g > 0:
                        dve.wait_ge(ln_hi, 4 * n + g)
                        dve.wait_ge(ln_part_d, 4 * n + g)
                        d = xs[:, (g - 1) * 8 * T:g * 8 * T].rearrange("p (c s t) -> p c s t", c=4, s=2)
                        v = dst[:, (g - 1) * 4 * T:g * 4 * T].rearrange("p (c t) -> p c t", c=4)
                        dve.tensor_tensor(d[:, :, 1, :], v, d[:, :, 0, :].bitcast(F32),
                                          ALU.subtract).then_inc(ln_lo, 1)

            for tt in range(2):
                dve.wait_ge(x_landed[tt], 16)
                for q in range(4):
                    ins = stats(x_tok, tt, q)
                ln_c.step(ins)
                mean_var(tt)
                normalize(0, x_tok, tt)
            for k in range(AHEAD):
                lower(Pos(k), k)
            dve.wait_ge(vec_landed, 16)
            features(0, x_feat)
            lo(Pos(0), 0)
            lo(Pos(1), 1)

            na_c = Chain(dve, na_chain, 1)

            def na_softmax(s, parity):
                na_c.begin(s)
                dve.wait_ge(na_qk, s.times(1, 1))
                dve.wait_ge(bias_landed[parity], s.over(2).times(16, 16) if s.i is not None
                            else 16 * (s.const // 2 + 1))
                wait(dve, na_pt_done, s.times(1))
                for e in range(2):
                    a, b = e * 2 * T, (e + 1) * 2 * T
                    ins = dve.scalar_tensor_tensor(out=na_s[:, a:b], in0=bank(2 + e), scalar=NA_DIM ** -0.5,
                                                   in1=na_bias[:, parity * 4 * T + a:parity * 4 * T + b],
                                                   op0=ALU.mult, op1=ALU.add)
                ins.then_inc(na_s_read, 1)
                dve.wait_ge(na_s_read, s.times(1, 1))
                na_c.step(dve.tensor_reduce(na_small[:, 0:4], na_s[:].rearrange("p (k t) -> p k t", k=4),
                                            AX.X, ALU.max))
                dve.tensor_scalar(na_small[:, 4:8], na_small[:, 0:4], -1.0, None, ALU.mult).then_inc(na_negmax, 1)
                na_c.end()

            def na_recip(s):
                dve.wait_ge(na_exp, s.times(4, 4))
                dve.reciprocal(na_small[:, 12:16], na_small[:, 8:12]).then_inc(na_rinv, 1)

            def na_take_turned(s):
                dve.wait_ge(na_pt_done, s.times(1, 1))
                wait(dve, na_pv, s.times(1))
                for e in range(2):
                    dve.tensor_copy(na_pt[:, e * 2 * T:(e + 1) * 2 * T], bank(4 + e)).then_inc(na_pt_copied, 1)

            def na_out_lo(s):
                dve.wait_ge(na_hi, s.times(1, 1))
                dve.tensor_tensor(nas[:, ds(s.times(2 * T, T), T)], bank(7, 0, T),
                                  nas[:, ds(s.times(2 * T), T)].bitcast(F32), ALU.subtract).then_inc(na_lo, 1)

            def na_step(s, slot, parity, prev2):
                t = Pos(s.const * 6, s.per * 6, s.i)
                lo(t, slot)
                if prev2:
                    na_out_lo(s + -2)
                na_softmax(s + -1, 1 - parity)
                lo(t + 1, slot + 1)
                lo(t + 2, slot + 2)
                na_recip(s + -1)
                lo(t + 3, slot + 3)
                lo(t + 4, slot + 4)
                lo(t + 5, slot + 5)
                na_take_turned(s + -1)

            for k in range(2, 6):
                lo(Pos(k), k)
            na_step(Pos(1), 6, 1, False)
            with dve.Fori(0, (NA_PAIRS - 2) // 2) as i:
                na_step(Pos(2, 2, i), 0, 0, True)
                na_step(Pos(3, 2, i), 2, 1, True)
            NL = NA_PAIRS - 1
            lo(Pos(T_RANK), T_RANK)
            na_out_lo(Pos(NL - 1))
            na_softmax(Pos(NL), NL % 2)
            lo(Pos(T_RANK + 1), T_RANK + 1)
            lo(Pos(T_RANK + 2), T_RANK + 2)
            na_recip(Pos(NL))
            lo(Pos(T_RANK + 3), T_RANK + 3)
            na_take_turned(Pos(NL))
            lo(Pos(T_RANK + 4), T_RANK + 4)
            lo(Pos(T_RANK + 5), T_RANK + 5)
            lo(Pos(T_RANK + 6), T_RANK + 6)
            na_out_lo(Pos(NL))
            for k in range(7, 10):
                lo(Pos(T_RANK + k), T_RANK + k)

            gc = Chain(dve, gla_dve, 4)
            gd = {}

            def cumulate(h):
                gc.begin(h)
                dve.wait_ge(z_done, h.times(1, 1))
                dve.wait_ge(consts_ready, 2)
                gc.step(dve.scalar_tensor_tensor(out=g_z[:], in0=g_z[:], scalar=0.0, in1=g_a[:],
                                                 op0=ALU.min, op1=ALU.subtract))
                gc.step(dve.tensor_tensor_scan(g_c[:, 0:2 * T], g_reset[:], g_z[:, 0:2 * T], 0.0,
                                               ALU.mult, ALU.add))
                back = g_c[:, 2 * T:4 * T]
                gc.step(dve.tensor_tensor_scan(back[:, ::-1], g_reset[:], g_z[:, 2 * T:4 * T][:, ::-1], 0.0,
                                               ALU.mult, ALU.add))
                for d in range(2):
                    c = g_c[:, d * 2 * T:(d + 1) * 2 * T].rearrange("p (k c) -> p k c", c=CHUNK)
                    a = g_a[:, d * 2 * T:(d + 1) * 2 * T].rearrange("p (k c) -> p k c", c=CHUNK)
                    whole = c[:, :, CHUNK - 1:CHUNK] if d == 0 else c[:, :, 0:1]
                    ins = dve.tensor_tensor(a, whole.to_broadcast([P, 2 * N_CHUNKS, CHUNK]), c, ALU.subtract)
                    if d == 0:
                        gc.step(ins)
                ins.then_inc(gap_done, 1)
                gc.end()

            def decay(h):
                dve.wait_ge(exp_done, h.times(1, 1))
                def both(x):
                    return x[:].unsqueeze(1).to_broadcast([P, 2, 2 * T])

                def dirs(x):
                    return x[:].rearrange("p (d k) -> p d k", d=2)

                dve.scalar_tensor_tensor(out=dirs(g_qd), in0=both(g_q), scalar=DK ** -0.5, in1=dirs(g_qd),
                                         op0=ALU.mult, op1=ALU.mult)
                dve.tensor_tensor(dirs(g_ki), both(g_k), dirs(g_ki), ALU.mult)
                dve.tensor_tensor(dirs(g_ks), both(g_k), dirs(g_ks), ALU.mult).then_inc(decayed, 1)

            at = Chain(dve, sem("gla_mask_chain"), 1, nop=True)

            def mask_att(h):
                at.begin(h)
                dve.wait_ge(att_done, h.times(1, 1))
                at.step(dve.tensor_copy(g_att[:], bank(4, 2 * CHUNK, 4 * CHUNK)))
                dve.copy_predicated(g_att[:], g_mask[:], bank(4, 0, 2 * CHUNK)).then_inc(att_masked, 1)
                at.end()

            def update_states(h, m):
                dve.wait_ge(gain_done, h.times(3, m + 1))
                if m > 0:
                    dve.wait_ge(state_done, h.times(3, m))
                for d in range(2):
                    n = m if d == 0 else N_CHUNKS - 1 - m
                    for kb in range(NKB):
                        q = d * NKB + kb
                        st = g_state[:, q * DV:(q + 1) * DV]
                        if m == 0:
                            ins = dve.tensor_copy(st, bank(2 + q))
                        else:
                            k = q * N_CHUNKS + n
                            ins = dve.scalar_tensor_tensor(out=st, in0=st, scalar=g_dec[:, k:k + 1],
                                                           in1=bank(2 + q), op0=ALU.mult, op1=ALU.add)
                ins.then_inc(state_done, 1)

            nc_ = Chain(dve, sem("gla_norm_chain"), 1)

            def norm_out(h):
                nc_.begin(h)
                dve.wait_ge(rms_done, h.times(2, 2))
                nc_.step(dve.reciprocal(g_small[:, 4:6], g_small[:, 2:4]))
                for tt in range(2):
                    ins = dve.tensor_scalar(g_on[:, tt * DV:(tt + 1) * DV], bank(6 + tt),
                                            g_small[:, 4 + tt:5 + tt], None, ALU.mult)
                ins.then_inc(on_done, 1)
                nc_.end()

            def gate_silu(h):
                gs.begin(h)
                dve.wait_ge(proj_taken, gd["taken"](h))
                gs.step(dve.tensor_tensor(g_x[:], g_x[:], g_sg[:], ALU.mult))
                gs.end()

            gs = Chain(dve, sem("gla_silu_chain"), 1)

            def gate_out(h):
                dve.wait_ge(ot_done, h.times(1, 1))
                for vb in range(NVB):
                    a, b = vb * T, (vb + 1) * T
                    ins = dve.scalar_tensor_tensor(
                        out=g_ot[:, a:b], in0=bank(2 + vb // 2, vb % 2 * T, (vb % 2 + 1) * T),
                        scalar=vec[:, V_NORM + vb:V_NORM + vb + 1], in1=g_x[:, a:b],
                        op0=ALU.mult, op1=ALU.mult)
                ins.then_inc(gated, 1)

            def out_lo(h):
                dve.wait_ge(o_hi, h.times(1, 1))
                dve.wait_ge(gated, h.times(1, 1))
                d = gls[:, ds(h.times(NVB * 2 * T), NVB * 2 * T)].rearrange("p (c s t) -> p c s t", c=NVB, s=2)
                dve.tensor_tensor(d[:, :, 1, :], g_ot[:].rearrange("p (c t) -> p c t", c=NVB),
                                  d[:, :, 0, :].bitcast(F32), ALU.subtract).then_inc(o_lo, 1)

            B1 = 3 * NA_PAIRS + 5
            gd["taken"] = lambda h: h.times(12, B1 + 8)

            def gla_head(h, t, last, first):
                s0 = T_GLA + QK_TILES
                for k in range(8 if last else 12):
                    lo(t + 2 * k, s0 + 2 * k)
                    if k == 1 and not first:
                        norm_out(h + -1)
                    if k == 3 and not first:
                        out_lo(h + -1)
                    if k == 9:
                        gate_silu(h)
                    lo(t + 2 * k + 1, s0 + 2 * k + 1)
                    if k == 1:
                        cumulate(h)
                    if k == 2 and not first:
                        gate_out(h + -1)
                    if k == 3:
                        decay(h)
                    if k == 4:
                        mask_att(h)
                    if k == 7:
                        update_states(h, 0)
                    if k == 9:
                        update_states(h, 1)
                    if k == 10:
                        update_states(h, 2)

            s_h = T_GLA + QK_TILES
            gla_head(Pos(0), Pos(s_h), False, True)
            with dve.Fori(0, GLA_HEADS - 2) as i:
                gla_head(Pos(1, 1, i), Pos(s_h + HEAD_TILES, HEAD_TILES, i), False, False)
            H = GLA_HEADS - 1
            gla_head(Pos(H), Pos(s_h + H * HEAD_TILES), True, False)
            update_states(Pos(H), 1)
            update_states(Pos(H), 2)
            lo(Pos(T_MERGE), T_MERGE)
            lo(Pos(T_MERGE + 1), T_MERGE + 1)
            gate_silu(Pos(H))
            norm_out(Pos(H))
            gate_out(Pos(H))
            out_lo(Pos(H))

            mc = Chain(dve, m_chain, 1)

            def gate_a(c, t, parity):
                dve.wait_ge(sig_a, c.times(1, 1))
                dve.wait_ge(tile_used, t.times(1, 3))
                a, b = parity * T, (parity + 1) * T
                dve.tensor_tensor(m_a[:, a:b], bank(4 * parity + 1, 0, T), m_sa[:, a:b],
                                  ALU.mult).then_inc(a_gated, 1)

            def gate_b(c, t, parity):
                mc.begin(c)
                dve.wait_ge(sig_b, c.times(1, 1))
                dve.wait_ge(tile_used, t.times(1, 7))
                dve.wait_ge(a_gated, c.times(1, 1))
                wait(dve, m_lo, c.times(1, -1))
                a, b = parity * T, (parity + 1) * T
                mc.step(dve.tensor_tensor(m_m[:, a:b], bank(4 * parity + 3, 0, T), m_sb[:, a:b], ALU.mult))
                dve.tensor_tensor(m_m[:, a:b], m_m[:, a:b], m_a[:, a:b], ALU.add).then_inc(merged, 1)
                mc.end()

            def merged_lo(c, parity):
                dve.wait_ge(m_hi, c.times(1, 1))
                dve.wait_ge(merged, c.times(1, 1))
                dve.tensor_tensor(ms[:, ds(c.times(2 * T, T), T)], m_m[:, parity * T:(parity + 1) * T],
                                  ms[:, ds(c.times(2 * T), T)].bitcast(F32), ALU.subtract).then_inc(m_lo, 1)

            def merge_step(c, t, slot, parity, prev, ahead=0):
                for k in range(ahead, MERGE_TILES):
                    lo(t + k, slot + k)
                    if k == 1 and prev:
                        gate_b(c + -1, t + -7, 1 - parity)
                    if k == 4:
                        if prev:
                            merged_lo(c + -1, 1 - parity)
                        gate_a(c, t, parity)

            for k in range(4):
                merge_step(Pos(k), Pos(T_MERGE + 7 * k), T_MERGE + 7 * k, k % 2, k > 0, 0 if k else 2)
            with dve.Fori(0, KC // 4 - 1) as i:
                for k in range(4):
                    merge_step(Pos(4 + k, 4, i), Pos(T_MERGE + 28 + 7 * k, 28, i), T_MERGE + 7 * k,
                               k % 2, True)
            lo(Pos(T_OUT), T_OUT)
            lo(Pos(T_OUT + 1), T_OUT + 1)
            gate_b(Pos(KC - 1), Pos(T_OUT - 7), 1)
            merged_lo(Pos(KC - 1), 1)

            def add_out(half, tt, n):
                dve.wait_ge(tile_used, T_OUT + KC * (half + 1))
                v = tok[:, tt * D + (2 * half + n) * 512:tt * D + (2 * half + n + 1) * 512]
                dve.scalar_tensor_tensor(out=v, in0=v, scalar=ALPHA, in1=bank(4 * tt + 2 * half + n),
                                         op0=ALU.mult, op1=ALU.add).then_inc(res_done, 1)

            def out_stats(half, tt):
                dve.wait_ge(res_done, 4 * half + 2 * tt + 2)
                for n in range(2):
                    ins = stats(tok, tt, 2 * half + n)
                ln_c.step(ins)

            for k in range(2, 4):
                lo(Pos(T_OUT + k), T_OUT + k)
            dve.wait_ge(p_hi, 1)
            p_dst = ys[:].rearrange("p (c s t) -> p c s t", c=2, s=2)
            dve.tensor_tensor(p_dst[:, :, 1, :], p_in[:].rearrange("p (c t) -> p c t", c=2),
                              p_dst[:, :, 0, :].bitcast(F32), ALU.subtract).then_inc(p_lo, 1)
            with dve.Fori(0, 3) as i:
                for k in range(4):
                    lo(Pos(T_OUT + 4 + k, 4, i), T_OUT + k)
            dve.wait_ge(h_back, 32)
            for k in range(16, 32):
                lo(Pos(T_OUT + k), T_OUT + k)
                if 17 <= k < 21:
                    add_out(0, (k - 17) // 2, (k - 17) % 2)
                if k in (21, 22):
                    out_stats(0, k - 21)
            lo(Pos(T_PLE), T_PLE)
            lo(Pos(T_PLE + 1), T_PLE + 1)
            for n in range(2):
                add_out(1, 0, n)
            lo(Pos(T_PLE + 2), T_PLE + 2)
            out_stats(1, 0)
            mean_var(0)
            for n in range(2):
                add_out(1, 1, n)
            out_stats(1, 1)
            mean_var(1)
            normalize(1, tok, 0)
            normalize(1, tok, 1)
            lo(Pos(T_PLE + 3), T_PLE + 3)
            lo(Pos(T_PQ), T_PQ)
            lo(Pos(T_PQ + 1), T_PQ + 1)
            features(1, h_feat)

            lo(Pos(T_PQ + 2), T_PQ + 2)
            lo(Pos(T_PQ + 3), T_PQ + 3)
            with dve.Fori(0, KC // 2 - 1) as i:
                for k in range(4):
                    lo(Pos(T_PQ + 4 + k, 4, i), T_PQ + k)
            r2 = Line(dve, res2_chain)

            def add_ple(half, n):
                q = 4 * half + n
                dve.wait_ge(gsig, q + 1)
                dve.wait_ge(h2_ready, n // 2 + 1)
                a, b = q % 2 * 512, (q % 2 + 1) * 512
                v = slice(n // 2 * D + (2 * half + n % 2) * 512, n // 2 * D + (2 * half + n % 2 + 1) * 512)
                r2.step(dve.tensor_tensor(ple_g[:, a:b], ple[:, v], sgm[:, a:b], ALU.mult))
                dve.scalar_tensor_tensor(out=tok[:, v], in0=tok[:, v], scalar=ALPHA, in1=ple_g[:, a:b],
                                         op0=ALU.mult, op1=ALU.add).then_inc(res2_done, 1)

            with dve.Fori(0, 4) as i:
                for k in range(4):
                    lo(Pos(T_PGATE + k, 4, i), T_PGATE + k)
            for k in range(16, 32):
                lo(Pos(T_PGATE + k), T_PGATE + k)
                if 17 <= k < 21:
                    add_ple(0, k - 17)

            tk = Chain(dve, tk_chain, 25, nop=True)

            def best8(scores, values, index):
                tk.step(dve.max(values, scores))
                tk.step(dve.max_index(index, values, scores))

            def next8(scores, rest, values, index):
                tk.step(dve.match_replace(rest, values[:, 0:8], scores, LOWEST))
                best8(rest, values[:, 8:16], index[:, 8:16])

            def key_columns(half):
                return slice(half * NKEYS, (half + 1) * NKEYS), slice(half * TOPK, (half + 1) * TOPK)

            def best_keys(u, half):
                a, b = key_columns(half)
                tk.step(dve.tensor_copy(tk_in[:, a], sc[:, ds(u.times(2 * NKEYS, half * NKEYS), NKEYS)]))
                best8(tk_in[:, a], tk_v[:, b][:, 0:8], tk_i[:, b][:, 0:8])

            def next_keys(half):
                a, b = key_columns(half)
                next8(tk_in[:, a], tk_w[:, a], tk_v[:, b], tk_i[:, b])

            def grid(x):
                return x.rearrange("p (a b) -> p a b", a=TOPK)

            def best_pairs():
                a = tk_v[:, 0:TOPK].unsqueeze(2).to_broadcast([P, TOPK, TOPK])
                b = tk_v[:, TOPK:2 * TOPK].unsqueeze(1).to_broadcast([P, TOPK, TOPK])
                tk.step(dve.tensor_tensor(grid(tk_c[:]), a, b, ALU.add))
                best8(tk_c[:], tk_cv[:, 0:8], tk_cp[:, 0:8])
                tk.step(dve.tensor_scalar(tk_s[:, 0:1], tk_cv[:, 0:1], -1.0, None, ALU.mult))

            def pair_ranks():
                dve.tensor_scalar(tk_ab[:, 0:TOPK], tk_cp[:], 4, None, ALU.logical_shift_right)
                tk.step(dve.tensor_scalar(tk_ab[:, TOPK:2 * TOPK], tk_cp[:], 15, None, ALU.bitwise_and))
                dve.tensor_copy(tk_if[:], tk_i[:])
                tk.step(dve.tensor_copy(tk_abf[:], tk_ab[:]))

            halves = tk_eq[:].rearrange("p (h a b) -> p h a b", h=2, a=TOPK)

            def match_ranks():
                r = tk_abf[:].rearrange("p (h a) -> p h a", h=2).unsqueeze(3).to_broadcast([P, 2, TOPK, TOPK])
                ranks = iota_top[:].unsqueeze(1).unsqueeze(1).to_broadcast([P, 2, TOPK, TOPK])
                tk.step(dve.tensor_tensor(halves, r, ranks, ALU.is_equal))

            def look_up(u):
                index = tk_if[:].rearrange("p (h b) -> p h b", h=2).unsqueeze(2).to_broadcast([P, 2, TOPK, TOPK])
                tk.step(dve.tensor_tensor(halves, halves, index, ALU.mult))
                dst = ex[:].rearrange("p (h c) -> p h c", h=2)[:, :, ds(u.times(TOPK), TOPK)]
                tk.step(dve.tensor_reduce(dst, halves, AX.X, ALU.add))

            def expert_gates(u):
                dve.wait_ge(tk_exp, u.times(1, 1))
                tk.step(dve.reciprocal(tk_s[:, 2:3], tk_s[:, 1:2]))
                dve.tensor_scalar(exg[:, ds(u.times(TOPK), TOPK)], tk_g[:], tk_s[:, 2:3], None,
                                  ALU.mult).then_inc(ex_done, 1)

            def top_unit(u, t, first=False):
                tk.begin(u)
                for k in range(8):
                    lo(t + k, T_U + k)
                    if first and k % 2 == 0:
                        add_ple(1, k // 2)
                    if k in (0, 2):
                        best_keys(u, k // 2)
                    if k in (1, 3):
                        next_keys(k // 2)
                    if k == 4:
                        best_pairs()
                    if k == 5:
                        next8(tk_c[:], tk_cw[:], tk_cv, tk_cp)
                        dve.engine_nop().then_inc(tk_neg, 1)
                        pair_ranks()
                    if k == 6:
                        match_ranks()
                    if k == 7:
                        look_up(u)
                        expert_gates(u)
                tk.end()

            dve.wait_ge(sc_taken, HP)
            top_unit(Pos(0), Pos(T_U), True)
            with dve.Fori(0, 15) as i:
                top_unit(Pos(1, 1, i), Pos(T_U + 8, 8, i))

            def hot(g, n):
                wait(dve, gate_mm, g.times(1))
                for q in range(4):
                    a, b = q * NKEYS, (q + 1) * NKEYS
                    col = ds(g.times(4, q), 1)
                    dve.tensor_scalar(hot0[:, a:b], iota_key[:], idx0_t[:, col], gate_t[:, col],
                                      ALU.is_equal, ALU.mult).then_inc(hot_ready, 1)
                    dve.tensor_scalar(hot1[:, a:b], iota_key[:], idx1_t[:, col], None,
                                      ALU.is_equal).then_inc(hot_ready, 1)

            lo(Pos(T_U + 128), T_U)
            dve.wait_ge(ex_t_taken, 3)
            lo(Pos(T_U + 129), T_U + 1)
            hot(Pos(0), 0)
            for n in range(1, 4):
                lo(Pos(T_U + 128 + 2 * n), T_U + 2 * n)
                lo(Pos(T_U + 129 + 2 * n), T_U + 2 * n + 1)
                hot(Pos(n), n)
            with dve.Fori(0, 15) as i:
                for n in range(4):
                    lo(Pos(T_U + 136 + 2 * n, 8, i), T_U + 2 * n)
                    lo(Pos(T_U + 137 + 2 * n, 8, i), T_U + 2 * n + 1)
                    hot(Pos(4 + n, 4, i), n)

            by_column = gates[:].rearrange("p (t j) -> p t j", j=NKEYS)

            def weigh(j, slot):
                dve.wait_ge(gelu_landed[slot], j.over(4).times(16, 16) if j.i is not None
                            else 16 * (j.const // 4 + 1))
                parity = slot % 2
                wait(dve, w_lo, j.times(1, -1))
                dve.tensor_tensor(wexp[:, parity * T:(parity + 1) * T].unsqueeze(2),
                                  gst[:, slot * T:(slot + 1) * T].unsqueeze(2),
                                  by_column[:, :, ds(j.times(1), 1)], ALU.mult).then_inc(w_ready, 1)

            def weight_lo(j, parity):
                dve.wait_ge(w_hi, j.times(1, 1))
                dve.wait_ge(w_ready, j.times(1, 1))
                a = parity * 2 * T
                dve.tensor_tensor(ys[:, a + T:a + 2 * T], wexp[:, parity * T:(parity + 1) * T],
                                  ys[:, a:a + T].bitcast(F32), ALU.subtract).then_inc(w_lo, 1)

            dve.wait_ge(gate_taken, T // 4)
            lo(Pos(T_V), T_V)
            lo(Pos(T_V + 1), T_V + 1)
            weigh(Pos(0), 0)
            weigh(Pos(1), 1)
            weight_lo(Pos(0), 0)
            weight_lo(Pos(1), 1)
            weigh(Pos(2), 2)
            for k in range(2 + AHEAD, 4):
                lower(Pos(T_V + k), T_V + k)
            with dve.Fori(0, NKEYS // 4 - 1) as i:
                for k in range(4):
                    lower(Pos(T_V + 4 + 2 * k, 8, i), T_V + 2 * k)
                    weight_lo(Pos(2 + k, 4, i), k % 2)
                    lower(Pos(T_V + 5 + 2 * k, 8, i), T_V + 2 * k + 1)
                    weigh(Pos(3 + k, 4, i), (3 + k) % 4)
            for k in range(2):
                lower(Pos(T_END - 4 + 2 * k), T_END + 2 * k)
                weight_lo(Pos(NKEYS - 2 + k), k)
                if k == 0:
                    weigh(Pos(NKEYS - 1), 3)
                lower(Pos(T_END - 3 + 2 * k), T_END + 2 * k + 1)

            dve.wait_ge(fin_landed, 64)
            for half in range(2):
                dve.wait_ge(tile_used, T_END - 1 + half)
                for tt in range(2):
                    for n in range(2):
                        v = fin[:, tt * D + (2 * half + n) * 512:tt * D + (2 * half + n + 1) * 512]
                        dve.tensor_tensor(v, v, bank(4 * tt + 2 * half + n), ALU.add).then_inc(fin_added, 1)
                    dve.wait_ge(fin_added, 4 * half + 2 * tt + 2)
                    for n in range(2):
                        ins = stats(fin, tt, 2 * half + n)
                    ln_c.step(ins)
                    if half == 1:
                        mean_var(tt)
            for tt in range(2):
                inverse_std(2, tt)
                v = fin[:, tt * D:(tt + 1) * D]
                ln_c.step(dve.scalar_tensor_tensor(out=v, in0=v, scalar=ln_mv[:, 2 * tt:2 * tt + 1],
                                                   in1=fin_tab[:, 0:D], op0=ALU.subtract, op1=ALU.mult))
                dve.scalar_tensor_tensor(out=v, in0=v, scalar=ln_sd[:, 2 * tt + 1:2 * tt + 2],
                                         in1=fin_tab[:, D:2 * D], op0=ALU.mult, op1=ALU.add).then_inc(out_ready, 1)


def _block(w):
    return w.reshape(2, 8, P, P).transpose(0, 2, 1, 3).reshape(2, P, TILE)


def _half(w):
    return w.reshape(8, P, P).transpose(1, 0, 2).reshape(1, P, TILE)


def _by_token(w):
    return w.reshape(-1, P, 2, TILE).transpose(2, 0, 1, 3).reshape(-1, P, TILE)


def _layout(a):
    import numpy as np

    w, b = a["w_in"][0], a["b_in"][0]
    naq, nak, nav = 0, 1024, 2048
    gq, gk, gv, gg = 3072, 4096, 5120, 7168
    lrf, lrb, ga, gb = 9216, 9232, 9248, 11296
    cols = []
    for s in range(NA_PAIRS):
        cols += [naq + s * P, nak + s * P, nav + s * P]
    w_rank = np.zeros((D, P), w.dtype)
    b_rank = np.zeros(P, b.dtype)
    for k, at in enumerate((lrf, lrb)):
        w_rank[:, 32 * k:32 * k + RANK] = w[:, at:at + RANK]
        b_rank[32 * k:32 * k + RANK] = b[at:at + RANK]
    qk = [[gq + h * DK + k * P for k in range(2)] + [gk + h * DK + k * P for k in range(2)]
          for h in range(GLA_HEADS)]
    vg = [[gv + h * DV + k * P for k in range(4)] + [gg + h * DV + k * P for k in range(4)]
          for h in range(GLA_HEADS)]
    stream = np.empty((T_END, P, TILE), w.dtype)
    at = 0

    def put(tiles):
        nonlocal at
        stream[at:at + len(tiles)] = tiles
        at += len(tiles)

    for c in cols:
        put(_block(w[:, c:c + P]))
    put(_block(w_rank))
    for c in qk[0]:
        put(_block(w[:, c:c + P]))
    for h in range(GLA_HEADS):
        for c in vg[h] + (qk[h + 1] if h + 1 < GLA_HEADS else []):
            put(_block(w[:, c:c + P]))
    assert at == T_MERGE - 0
    for c in range(KC):
        s = slice(c * P, (c + 1) * P)
        put(_block(w[:, ga + c * P:ga + (c + 1) * P]))
        put(_half(a["w_proj_a"][0][:, s]))
        put(_block(w[:, gb + c * P:gb + (c + 1) * P]))
        put(_block(a["w_proj_b"][0][:, s]))
    put(_by_token(a["w_out"][0]))
    put(_by_token(a["w_ple"][0]))
    for c in range(KC):
        put(_block(a["peer_wq"][0][:, c * P:(c + 1) * P]))
    put(_by_token(a["w_ple_gate"][0]))
    assert at == T_U
    u = a["peer_u"][0].reshape(NKEYS, NKEYS, 2, 8, P)
    stream[T_U:T_V] = u.transpose(1, 2, 4, 3, 0).reshape(2 * NKEYS, P, TILE)
    v = a["peer_v"][0].reshape(NKEYS, NKEYS, 2, TILE)
    stream[T_V:T_END] = v.transpose(1, 2, 0, 3).reshape(2 * NKEYS, P, TILE)

    vectors = np.zeros((P, V_COLS), b.dtype)
    for k, name in enumerate(("ln_emb_g", "ln_emb_b", "ln_a_g", "ln_a_b")):
        vectors[:, V_LN + k * KC:V_LN + (k + 1) * KC] = a[name].reshape(KC, P).T
    for k, c in enumerate(cols):
        vectors[:, V_NA + k] = b[c:c + P]
    vectors[:, V_RANK] = b_rank
    for h in range(GLA_HEADS):
        for k, c in enumerate(qk[h] + vg[h]):
            vectors[:, V_GLA + h * GLA_BLOCKS + k] = b[c:c + P]
        for k, name in enumerate(("gla_gk_bias_f", "gla_gk_bias_b")):
            part = a[name][0].reshape(GLA_HEADS, NKB, P)[h]
            vectors[:, V_DECAY + 4 * h + 2 * k:V_DECAY + 4 * h + 2 * k + 2] = part.T
    for c in range(KC):
        for k, base in enumerate((ga, gb)):
            vectors[:, V_GATES + 2 * c + k] = b[base + c * P:base + (c + 1) * P]
    vectors[:, V_NORM:V_NORM + NVB] = a["gla_norm_g"][0].reshape(NVB, P).T

    rows = T // GRID_W
    q, k = np.arange(T), np.arange(T)
    qr, qc, kr, kc = q // GRID_W, q % GRID_W, k // GRID_W, k % GRID_W
    start = np.clip(qc - WIN_C // 2, 0, GRID_W - WIN_C)
    seen = (kc[None] >= start[:, None]) & (kc[None] < start[:, None] + WIN_C)
    assert rows <= WIN_R
    dr = kr[None] - qr[:, None] + WIN_R - 1
    dc = np.where(seen, kc[None] - qc[:, None] + WIN_C - 1, 0)
    table = a["na_rpb"][0][:, dr, dc]
    table = np.where(seen[None], table, np.float32(MASKED)).astype(b.dtype)
    rpb = table.reshape(NA_PAIRS, 2, 2, P, T).transpose(0, 3, 1, 2, 4).reshape(NA_PAIRS, P, 4 * T)

    up = np.zeros((GLA_HEADS, 64, DK), w.dtype)
    for k, name in enumerate(("gla_gk_up_f", "gla_gk_up_b")):
        up[:, 32 * k:32 * k + RANK] = a[name][0].reshape(RANK, GLA_HEADS, DK).transpose(1, 0, 2)
    keys = a["peer_sub_keys"][0].reshape(HP, NKEYS, P).transpose(2, 0, 1).reshape(P, HP * NKEYS)
    gains = np.stack([a[n].reshape(D) for n in ("ln_emb_g", "ln_emb_b", "ln_a_g", "ln_a_b", "ln_b_g", "ln_b_b")])
    p_t = a["p"][0, 0].T.reshape(2, P, T).transpose(1, 0, 2).reshape(P, 2 * T)
    return {"stream": stream, "vectors": vectors, "gains": gains, "x_in": a["x"].reshape(2, P, D), "p_t": p_t, "rpb": rpb,
            "decay_up": up, "keys": keys}


def kernel(**inputs):
    import numpy as np
    import concourse.bacc as bacc
    from concourse.bass_utils import run_bass_kernel_spmd

    laid = {n: np.ascontiguousarray(v) for n, v in
            _layout({n: np.asarray(v) for n, v in inputs.items()}).items()}
    nc = bacc.Bacc("TRN2", target_bir_lowering=False, num_devices=1)
    args = {n: nc.dram_tensor(n, v.shape, mybir.dt.from_np(v.dtype), kind="ExternalInput").ap()
            for n, v in laid.items()}
    out = nc.dram_tensor("out", (2, P, D), mybir.dt.float32, kind="ExternalOutput").ap()
    encoder_layer(nc, out=out, **args)
    r = run_bass_kernel_spmd(nc, [laid], core_ids=[0])
    return np.asarray(r.results[0]["out"]).reshape(1, T, D)
```

```python
from contextlib import ExitStack

import concourse.bass as bass
from concourse import mybir

P = 128
D = 2048
T = 256
KC = D // P
NA_HEADS, NA_DIM, GRID_W, WIN_R, WIN_C = 16, 64, 64, 8, 16
NA_PAIRS = NA_HEADS // 2
GLA_HEADS, DK, DV, CHUNK, RANK = 4, 256, 512, 64, 16
NKB, NVB = DK // P, DV // P
N_CHUNKS = T // CHUNK
PEER_HEADS, NKEYS, TOPK = 8, 128, 16
HP = 2 * PEER_HEADS
PLE = 256
EPS = 1e-5
ALPHA = 2.0 ** 0.25
LOWEST = -3.0e38
MASKED = -1.0e30

TOP_STEPS, TOP_KEY_STEPS = 22, 8

TILE = 8 * P
RING = 4
AHEAD = 1
NA_TILES = NA_PAIRS * 6
RANK_TILES = 2
QK_TILES = 8
VG_TILES = 16
HEAD_TILES = VG_TILES + QK_TILES
MERGE_TILES = 7
T_NA = 0
T_RANK = T_NA + NA_TILES
T_GLA = T_RANK + RANK_TILES
T_MERGE = T_GLA + GLA_HEADS * HEAD_TILES
T_FIRST = T_MERGE + 8
T_OUT = T_MERGE + KC * MERGE_TILES
T_PLE = T_OUT + 2 * KC
T_PQ = T_PLE + 4
T_PGATE = T_PQ + 2 * KC
T_U = T_PGATE + 2 * KC
T_V = T_U + 2 * NKEYS
T_END = T_V + 2 * NKEYS

V_LN = 0
V_NA = V_LN + 4 * KC
V_RANK = V_NA + 3 * NA_PAIRS
V_GLA = V_RANK + 1
GLA_BLOCKS = 2 * NKB + 2 * NVB
V_GATES = V_GLA + GLA_HEADS * GLA_BLOCKS
V_NORM = V_GATES + 2 * KC
V_DECAY = V_NORM + NVB
V_COLS = V_DECAY + 4 * GLA_HEADS


class Pos:

    def __init__(self, const, per=0, i=None):
        self.const, self.per, self.i = const, per, i

    def __add__(self, n):
        return Pos(self.const + n, self.per, self.i)

    def times(self, each, plus=0):
        fixed = self.const * each + plus
        return fixed if self.i is None else self.i * (self.per * each) + fixed

    def over(self, n):
        assert self.per % n == 0
        return Pos(self.const // n, self.per // n, self.i)


def wait(eng, sem, value):
    if isinstance(value, int) and value <= 0:
        return
    eng.wait_ge(sem, value)


class Line:

    def __init__(self, eng, sem):
        self.eng, self.sem, self.n = eng, sem, 0

    def step(self, ins):
        self.n += 1
        ins.then_inc(self.sem, 1)
        self.eng.wait_ge(self.sem, self.n)


class Chain:

    def __init__(self, eng, sem, per, nop=False):
        self.eng, self.sem, self.per, self.turn, self.n = eng, sem, per, None, 0
        self.nop = nop

    def begin(self, turn):
        self.turn, self.n = turn, 0

    def step(self, ins):
        self.n += 1
        ins.then_inc(self.sem, 1)
        self.eng.wait_ge(self.sem, self.turn.times(self.per, self.n))
        if self.nop:
            self.eng.nop(nofuse=True)

    def end(self):
        assert self.n == self.per


def encoder_layer(nc, stream, vectors, gains, x_in, p_t, rpb, decay_up, keys, out):
    F32, F32R, BF16, U32, U8 = (mybir.dt.float32, mybir.dt.float32r, mybir.dt.bfloat16,
                                mybir.dt.uint32, mybir.dt.uint8)
    ALU, ACT, AX = mybir.AluOpType, mybir.ActivationFunctionType, mybir.AxisListType
    ds = bass.ds

    h_dram = nc.dram_tensor("h_spill", (P, 2 * D), F32, kind="Internal").ap()
    residual_dram = nc.dram_tensor("residual_spill", (P, 2 * D), F32, kind="Internal").ap()
    gelu_dram = nc.dram_tensor("gelu_spill", (NKEYS, P, T), F32, kind="Internal").ap()

    with ExitStack() as ctx:
        def sb(name, cols, dt=F32, group=ctx):
            return group.enter_context(nc.sbuf_tensor(name, [P, cols], dt))

        def sem(name):
            return ctx.enter_context(nc.semaphore(name))

        with ExitStack() as g:
            fin = sb("final", 2 * D, group=g)
            fin_tab = sb("final_gain_shift", 2 * D, group=g)
        xs = sb("act_split", KC * 2 * T, F32R)
        with ExitStack() as g:
            w_in = sb("weights_in", RING * TILE, group=g)
        w_low = sb("weights_lower", RING * TILE, F32R)
        w_up = sb("weights_upper", RING * TILE, F32R)
        vec = sb("vec_table", V_COLS)
        ident = sb("identity", P)
        iota_key = sb("iota_key", NKEYS)
        iota_top = sb("iota_top", TOPK)
        eps_t = sb("eps", 1)
        ln_st = sb("norm_stats", 2 * 4 * 6)
        ln_mv = sb("norm_mean_var", 2 * 2)
        ln_shift = sb("norm_shift", 1)
        ln_sd = sb("norm_std", 2 * 2)
        zeros = sb("zeros", P, BF16)
        gst = sb("gelu_ring", 4 * T)

        with ExitStack() as g:
            idx0_t = sb("expert_row_t", T, group=g)
            idx1_t = sb("expert_col_t", T, group=g)
            gate_t = sb("expert_gate_t", T, group=g)
            hot0 = sb("hot_rows", 4 * NKEYS, group=g)
            hot1 = sb("hot_cols", 4 * NKEYS, group=g)
        with ExitStack() as g:
            ys = sb("last_split", 2 * 2 * T, F32R, group=g)
            wexp = sb("expert_weight", 2 * T, group=g)
        sb("shared_small", 3 * T + 8 * NKEYS)

        region = ExitStack()
        with region as g:
            nas = sb("na_split", NA_PAIRS * 2 * T, F32R, group=g)
            gls = sb("gla_split", KC * 2 * T, F32R, group=g)
            with ExitStack() as h:
                na_qkv = sb("na_qkv", 2 * 3 * T, group=h)
                na_bias = sb("na_bias", 2 * 4 * T, group=h)
                na_s = sb("na_scores", 4 * T, group=h)
                na_pt = sb("na_probs_t", 4 * T, group=h)
                na_v = sb("na_v", 2 * P, group=h)
                na_small = sb("na_small", 16, group=h)
                x_tok = sb("x_tokens", 2 * D, group=h)
                x_tab = sb("x_gain_shift", 2 * D, group=h)
                x_feat = sb("x_features", KC * T, group=h)
            with ExitStack() as h:
                g_z = sb("gla_z", 4 * T, group=h)
                g_a = sb("gla_a", 4 * T, group=h)
                g_c = sb("gla_cum", 4 * T, group=h)
                g_qd = sb("gla_q_decayed", 4 * T, group=h)
                g_ki = sb("gla_k_intra", 4 * T, group=h)
                g_ks = sb("gla_k_state", 4 * T, group=h)
                g_kt = sb("gla_k_state_t", 4 * T, group=h)
                g_q = sb("gla_q", NKB * T, group=h)
                g_k = sb("gla_k", NKB * T, group=h)
                g_vt = sb("gla_v_t", NVB * T, group=h)
                g_rank = sb("gla_rank", T, group=h)
                g_up = sb("gla_up", DK, group=h)
                g_v = sb("gla_v", 2 * DV, group=h)
                g_att = sb("gla_att", 2 * CHUNK, group=h)
                g_state = sb("gla_state", 4 * DV, group=h)
                g_dec = sb("gla_chunk_decay", 16, group=h)
                g_x = sb("gla_gate_in", NVB * T, group=h)
                g_sg = sb("gla_gate_sig", NVB * T, group=h)
                g_on = sb("gla_out_normed", 2 * DV, group=h)
                g_ot = sb("gla_out_t", NVB * T, group=h)
                g_small = sb("gla_small", 8, group=h)
                g_reset = sb("gla_reset", 2 * T, group=h)
                g_early = sb("early_gate_sig", 4 * T, group=h)
                g_mask = sb("gla_mask", 2 * CHUNK, U8, group=h)
                g_maskf = sb("gla_mask_f", 2 * CHUNK, group=h)
            with ExitStack() as h:
                ms = sb("merged_split", KC * 2 * T, F32R, group=h)
                m_sa = sb("merge_sig_a", 2 * T, group=h)
                m_sb = sb("merge_sig_b", 2 * T, group=h)
                m_a = sb("merge_a", 2 * T, group=h)
                m_m = sb("merge_sum", 2 * T, group=h)
                tok = sb("residual", 2 * D, group=h)
                tok_tab = sb("residual_gain_shift", 2 * D, group=h)
        with ExitStack() as g:
            sc = sb("key_scores", 2 * HP * NKEYS, group=g)
            key_t = sb("keys_t", HP * NKEYS, group=g)
            pq = sb("peer_q", 2 * T, group=g)
            ple = sb("ple", 2 * D, group=g)
            p_in = sb("p_in", 2 * T, group=g)
            sgm = sb("ple_sig", 2 * 512, group=g)
            ple_g = sb("ple_gated", 2 * 512, group=g)
            tk_in = sb("top_scores", 2 * NKEYS, group=g)
            tk_w = sb("top_rest", 2 * NKEYS, group=g)
            tk_v = sb("top_values", 2 * TOPK, group=g)
            tk_i = sb("top_index", 2 * TOPK, U32, group=g)
            tk_if = sb("top_index_f", 2 * TOPK, group=g)
            tk_c = sb("pair_sums", TOPK * TOPK, group=g)
            tk_cw = sb("pair_rest", TOPK * TOPK, group=g)
            tk_cv = sb("pair_values", TOPK, group=g)
            tk_cp = sb("pair_pos", TOPK, U32, group=g)
            tk_ab = sb("pair_ranks", 2 * TOPK, U32, group=g)
            tk_abf = sb("pair_ranks_f", 2 * TOPK, group=g)
            tk_eq = sb("pair_match", 2 * TOPK * TOPK, group=g)
            tk_sum = sb("gate_sums", 2 * HP, group=g)
            ex = sb("expert_row_col", 4 * P, group=g)
            exg = sb("expert_gate", 2 * P, group=g)
            h_feat = sb("h_features", KC * T, group=g)
        gates = sb("expert_gates", T * NKEYS)
        ps = ctx.enter_context(nc.psum_tensor("psum", [P, 8 * 512], F32))

        def bank(n, a=0, b=512, p0=0, p1=P):
            return ps[p0:p1, n * 512 + a:n * 512 + b]

        def feature_bank(c, a, b):
            return bank((0, 1, 4, 5, 2, 3, 6, 7)[c // 2], c % 2 * T + a, c % 2 * T + b)

        def norm_gain(n, c):
            return vec[:, V_LN + 2 * n * KC + c:V_LN + 2 * n * KC + c + 1]

        def norm_shift(n, c):
            return vec[:, V_LN + (2 * n + 1) * KC + c:V_LN + (2 * n + 1) * KC + c + 1]

        landed = [sem(f"tile_landed_{i}") for i in range(4)]
        hi_ready, split_ready, tile_used = sem("hi_ready"), sem("split_ready"), sem("tile_used")
        consts_ready, pool_chain = sem("consts_ready"), sem("pool_chain")
        vec_landed, up_landed = sem("vec_landed"), sem("up_landed")
        x_landed = [sem(f"x_landed_{i}") for i in range(8)]
        bias_landed = [sem("na_bias_landed_0"), sem("na_bias_landed_1")]
        ln_var, ln_std, ln_turned, ln_part_a, ln_part_d, ln_hi, ln_lo, ln_chain = (
            sem(n) for n in ("ln_var", "ln_std", "ln_turned", "ln_features_act",
                             "ln_features_dve", "ln_hi", "ln_lo", "ln_chain"))
        ln_shift_ready = sem("ln_shift_ready")
        ln_normed = [sem("ln_normed_0"), sem("ln_normed_1")]
        x_tab_landed, h_ready, h_spilled, h_back, tok_tab_landed, h2_ready = (sem(n) for n in (
            "x_gain_shift_landed", "h_ready", "h_spilled", "h_back", "gain_shift_landed", "h2_ready"))
        proj_taken = sem("proj_taken")
        na_qk, na_s_read, na_negmax, na_exp, na_rinv, na_probs = (sem(n) for n in (
            "na_qk", "na_scores_read", "na_negmax", "na_exp", "na_rinv", "na_probs"))
        na_pt_done, na_pt_copied, na_vt_done, na_v_copied, na_pv, na_hi, na_lo, na_chain = (
            sem(n) for n in ("na_pt_done", "na_pt_copied", "na_vt_done", "na_v_copied", "na_pv",
                             "na_hi", "na_lo", "na_chain"))
        la_done, z_done, gap_done, exp_done, decayed, kt_done, kt_copied = (sem(n) for n in (
            "gla_la_done", "gla_z_done", "gla_gap_done", "gla_exp_done", "gla_decayed",
            "gla_kt_done", "gla_kt_copied"))
        att_done, att_masked, vt_done, v_copied, gain_done, state_done, o_done = (sem(n) for n in (
            "gla_att_done", "gla_att_masked", "gla_vt_done", "gla_v_copied", "gla_gain_done",
            "gla_state_done", "gla_o_done"))
        rms_done, on_done, ot_done, gated, o_hi, o_lo, gla_act, gla_dve = (
            sem(n) for n in ("gla_rms_done", "gla_on_done", "gla_ot_done", "gla_gated", "gla_o_hi",
                             "gla_o_lo", "gla_act_chain", "gla_dve_chain"))
        sig_a, sig_b, a_gated, merged, m_hi, m_lo, m_chain = (sem(n) for n in (
            "merge_sig_a", "merge_sig_b", "merge_a_gated", "merge_sum_ready", "merge_hi", "merge_lo",
            "merge_chain"))
        res_done = sem("residual_done")
        keys_landed, pq_taken, sc_done, sc_taken = (sem(n) for n in (
            "keys_landed", "peer_q_taken", "scores_done", "scores_taken"))
        p_landed, p_hi, p_lo, ple_taken, gsig, res2_done, res2_chain, res_spilled = (
            sem(n) for n in ("p_landed", "p_hi", "p_lo", "ple_taken", "ple_sig_ready",
                             "residual2_done", "residual2_chain", "residual_spilled"))
        tk_loaded = sem("unit_scores_ready")
        tk_chain, tk_exp, ex_done, ex_t_done, ex_t_taken = (sem(n) for n in (
            "topk_chain", "gates_exp", "experts_done", "experts_turned",
            "experts_taken"))
        gelu_done = sem("gelu_done")
        gelu_stored = [sem(f"gelu_stored_{i}") for i in range(4)]
        hot_ready, gate_mm, gate_taken = sem("hot_ready"), sem("gate_spread"), sem("gate_taken")
        gelu_landed = [sem(f"gelu_landed_{i}") for i in range(4)]
        w_ready, w_hi, w_lo = (sem(n) for n in (
            "expert_weight_ready", "expert_weight_hi", "expert_weight_lo"))
        fin_landed, fin_added, out_ready, out_stored = (sem(n) for n in (
            "final_landed", "final_added", "out_ready", "out_stored"))

        block = ctx.enter_context(nc.Block())

        @block.sync
        def _(sp):
            def load(t, slot):
                wait(sp, tile_used, t.times(1, 1 - RING))
                src = stream[ds(t.times(1), 1)].rearrange("n p f -> (n p) f")
                sp.dma_start(w_in[:, slot * TILE:(slot + 1) * TILE], src).then_inc(landed[slot], 16)

            for tt in range(2):
                for q in range(4):
                    sp.dma_start(x_tok[:, tt * D + q * 512:tt * D + (q + 1) * 512],
                                 x_in[tt][:, q * 512:(q + 1) * 512]).then_inc(x_landed[4 * tt + q], 16)
            for s in range(4):
                load(Pos(s), s)
            with sp.Fori(0, T_END // 4 - 1) as i:
                for s in range(4):
                    load(Pos(4 + s, 4, i), s)
            for t in range(T_END // 4 * 4, T_END):
                load(Pos(t), t % 4)
            for tt in range(2):
                for half in range(2):
                    a, b = half * 1024, (half + 1) * 1024
                    sp.wait_ge(out_ready, 2 * tt + half + 1)
                    sp.dma_start(out[tt][:, a:b], fin[:, tt * D + a:tt * D + b]).then_inc(out_stored, 16)
            sp.wait_ge(out_stored, 64)

        @block.gpsimd
        def _(pool):
            pool.dma_start(vec[:], vectors).then_inc(vec_landed, 16)
            n = [0]

            def const(ins):
                n[0] += 1
                ins.then_inc(pool_chain, 1)
                pool.wait_ge(pool_chain, n[0])

            const(pool.memset(eps_t[:], EPS))
            const(pool.memset(zeros[:], 0.0))
            const(pool.memset(ident[:], 0.0))
            const(pool.affine_select(out=ident[:], in_=ident[:], compare_op=ALU.not_equal, fill=1.0,
                                     base=0, pattern=[[-1, P]], channel_multiplier=1))
            const(pool.iota(iota_key[:], [[1, NKEYS]], base=0, channel_multiplier=0,
                            allow_small_or_imprecise_dtypes=True))
            const(pool.iota(iota_top[:], [[1, TOPK]], base=0, channel_multiplier=0,
                            allow_small_or_imprecise_dtypes=True))
            pool.engine_nop().then_inc(consts_ready, 1)

            def load_bias(s, slot):
                wait(pool, na_s_read, s.times(1, -1))
                src = rpb[ds(s.times(1), 1)].rearrange("n p f -> (n p) f")
                pool.dma_start(na_bias[:, slot * 4 * T:(slot + 1) * 4 * T], src).then_inc(
                    bias_landed[slot], 16)

            pool.wait_ge(landed[3], 16)
            load_bias(Pos(0), 0)
            load_bias(Pos(1), 1)
            with pool.Fori(0, 8) as i:
                pool.wait_ge(tile_used, i + 3)
                pool.dma_start(x_tab[:, ds(i * 512, 512)],
                               gains[0:1][:, ds(i * 512, 512)].to_broadcast([P, 512])).then_inc(x_tab_landed, 16)

            def scale_shift(x, table, tt, done):
                v = x[:, tt * D:(tt + 1) * D]
                const(pool.tensor_tensor(v, v, table[:, 0:D], ALU.mult))
                pool.tensor_tensor(v, v, table[:, D:2 * D], ALU.add).then_inc(done, 1)

            pool.wait_ge(x_tab_landed, 128)
            pool.wait_ge(ln_turned, 2)
            for tt in range(2):
                scale_shift(x_tok, x_tab, tt, h_ready)
                pool.wait_ge(h_ready, tt + 1)
                pool.dma_start(h_dram[:, tt * D:(tt + 1) * D], x_tok[:, tt * D:(tt + 1) * D]).then_inc(h_spilled, 16)
                load_bias(Pos(2 + tt), tt)
            with pool.Fori(0, NA_PAIRS // 2 - 2) as i:
                load_bias(Pos(4, 2, i), 0)
                load_bias(Pos(5, 2, i), 1)

            pool.wait_ge(na_lo, NA_PAIRS)
            pool.wait_ge(h_spilled, 32)
            const(pool.memset(g_reset[:], 1.0))
            reset0 = g_reset[:].rearrange("p (n c) -> p n c", c=CHUNK)[:, :, 0:1]
            const(pool.memset(reset0, 0.0))
            const(pool.memset(g_maskf[:], 1.0))
            for half in range(2):
                m = g_maskf[64 * half:64 * half + 64, :].rearrange("p (a c) -> p a c", a=2)
                const(pool.affine_select(out=m, in_=m, compare_op=ALU.is_ge, fill=0.0, base=0,
                                         pattern=[[0, 2], [1, CHUNK]], channel_multiplier=-1))
            const(pool.tensor_copy(g_mask[:], g_maskf[:]))
            pool.engine_nop().then_inc(consts_ready, 1)

            def load_up(h):
                wait(pool, la_done, h.times(1))
                src = decay_up[ds(h.times(1), 1)].rearrange("n p f -> (n p) f")
                pool.dma_start(g_up[0:64, :], src).then_inc(up_landed, 16)

            load_up(Pos(0))
            with pool.Fori(0, GLA_HEADS - 1) as i:
                load_up(Pos(1, 1, i))

            pool.wait_ge(o_lo, GLA_HEADS)
            pool.wait_ge(merged, 2)
            with pool.Fori(0, 8) as i:
                pool.wait_ge(tile_used, i * 8 + (T_MERGE + 14))
                pool.dma_start(tok[:, ds(i * 512, 512)], h_dram[:, ds(i * 512, 512)]).then_inc(h_back, 16)
                pool.dma_start(tok_tab[:, ds(i * 512, 512)],
                               gains[1:2][:, ds(i * 512, 512)].to_broadcast([P, 512])).then_inc(tok_tab_landed, 16)
            pool.wait_ge(tile_used, T_OUT)
            pool.dma_start(p_in[:], p_t).then_inc(p_landed, 16)
            pool.dma_start(key_t[:], keys).then_inc(keys_landed, 16)
            pool.wait_ge(tok_tab_landed, 128)
            pool.wait_ge(ln_turned, 4)
            for tt in range(2):
                scale_shift(tok, tok_tab, tt, h2_ready)
            pool.wait_ge(res2_done, 8)
            pool.dma_start(residual_dram, tok[:]).then_inc(res_spilled, 16)

            def store_gelu(j, slot):
                pool.wait_ge(gelu_done, j.times(1, 1))
                dst = gelu_dram[ds(j.times(1), 1)].rearrange("n p f -> (n p) f")
                pool.dma_start(dst, gst[:, slot * T:(slot + 1) * T]).then_inc(gelu_stored[slot], 16)

            with pool.Fori(0, NKEYS // 4 - 1) as i:
                for s in range(4):
                    store_gelu(Pos(s, 4, i), s)
            for s in range(4):
                pool.wait_ge(gelu_stored[s], 16 * (NKEYS // 4 - 1))

            def load_gelu(j, slot):
                pool.wait_ge(w_ready, j.times(1, 1))
                src = gelu_dram[ds(j.times(1), 1)].rearrange("n p f -> (n p) f")
                pool.dma_start(gst[:, slot * T:(slot + 1) * T], src).then_inc(gelu_landed[slot], 16)

            for s in range(4):
                load_gelu(Pos(s), s)
            pool.wait_ge(tile_used, T_V)
            pool.wait_ge(res_spilled, 16)
            last_table = gains[2:3]
            with pool.Fori(0, 8) as i:
                for s in range(4):
                    load_gelu(Pos(4 + s, 4, i), s)
                pool.dma_start(fin[:, ds(i * 512, 512)], residual_dram[:, ds(i * 512, 512)]).then_inc(
                    fin_landed, 16)
                pool.dma_start(fin_tab[:, ds(i * 512, 512)],
                               last_table[:, ds(i * 512, 512)].to_broadcast([P, 512])).then_inc(fin_landed, 16)
            with pool.Fori(0, NKEYS // 4 - 10) as i:
                for s in range(4):
                    load_gelu(Pos(36 + s, 4, i), s)

        @block.tensor
        def _(pe):
            def turn_normed(n, x, upper_free=None):
                for half in range(2):
                    if half == 1 and upper_free is not None:
                        pe.wait_ge(*upper_free)
                    for tt in range(2):
                        if half == 0:
                            pe.wait_ge(ln_normed[tt], n + 1)
                        for c in range(KC // 2 * half, KC // 2 * (half + 1)):
                            a = tt * D + c * P
                            mm = pe.transpose(feature_bank(c, tt * P, (tt + 1) * P), x[:, a:a + P], ident[:])
                    mm.then_inc(ln_turned, 1)

            def products(t, slot, pieces, norm=None):
                pe.wait_ge(split_ready, t.times(1, 1))
                base = slot % RING * TILE
                for dst, col, act, start, stop in pieces:
                    if norm is not None and col % 4 == 0:
                        pe.wait_ge(ln_lo, norm + col // 4 + 1)
                    w_h = w_up[:, base + col * P:base + (col + 1) * P]
                    w_l = w_low[:, base + col * P:base + (col + 1) * P]
                    pe.matmul(dst, w_h, act[:, 0:T], start=start, stop=False, skip_group_check=True)
                    pe.matmul(dst, w_h, act[:, T:2 * T], start=False, stop=False,
                              skip_group_check=True)
                    mm = pe.matmul(dst, w_l, act[:, 0:T], start=False, stop=stop,
                                   skip_group_check=True)
                mm.then_inc(tile_used, 1)

            def products_by_token(t, slot, act, out_bank, start, stop, banks_free=None):
                pe.wait_ge(split_ready, t.times(1, 1))
                base = slot % RING * TILE
                for tt in range(2):
                    if tt == 1 and banks_free is not None:
                        pe.wait_ge(banks_free, KC)
                    for k, (part, w) in enumerate(((0, w_up), (0, w_low), (1, w_up))):
                        for n in range(2):
                            mm = pe.matmul(out_bank(tt, n), act[:, part * T + tt * P:part * T + (tt + 1) * P],
                                           w[:, base + n * 512:base + (n + 1) * 512],
                                           start=start and k == 0, stop=stop and k == 2,
                                           skip_group_check=True)
                mm.then_inc(tile_used, 1)

            def by_token(t, acts, banks_free=None, last_chunk=None):
                with pe.Fori(0, 2) as half:
                    for c in range(KC):
                        if c >= KC - 2 and last_chunk is not None:
                            pe.wait_ge(last_chunk, c + 1)
                        products_by_token(Pos(t + c, KC, half), t + c, chunk(acts, c),
                                          lambda tt, n: ps[:, ds(half * 1024 + (tt * D + n * 512), 512)],
                                          c == 0, c == KC - 1, banks_free if c == 0 else None)

            def chunk(acts, c):
                return acts[:, c * 2 * T:(c + 1) * 2 * T]

            def half_block(t, slot, dst, acts, first, last, k0=0, norm=None):
                products(t, slot, [(dst, c, chunk(acts, k0 + c), first and c == 0, last and c == 7)
                                   for c in range(8)], norm)

            def two_tiles(t, slot, dst, acts, norm=None):
                half_block(t, slot, dst, acts, True, False, norm=norm)
                half_block(t + 1, slot + 1, dst, acts, False, True, k0=8,
                           norm=None if norm is None else norm + 2)

            pe.wait_ge(consts_ready, 1)
            turn_normed(0, x_tok)

            def na_block(s, k, t, slot, parity):
                wait(pe, proj_taken, s.times(3, k - 1))
                first = s.i is None and s.const == 0 and k == 0
                if first:
                    pe.wait_ge(ln_part_a, 1)
                two_tiles(t, slot, bank((3 * parity + k) % 2, 0, T), xs, 0 if first else None)

            def qkv(parity, k):
                a = (parity * 3 + k) * T
                return na_qkv[:, a:a + T]

            def na_scores(s, parity):
                pe.wait_ge(proj_taken, s.times(3, 3))
                wait(pe, na_s_read, s.times(1))
                for e in range(2):
                    rows = slice(64 * e, 64 * e + 64)
                    for tq in range(2):
                        mm = pe.matmul(bank(2 + e, tq * T, (tq + 1) * T),
                                       qkv(parity, 0)[rows, tq * P:(tq + 1) * P],
                                       qkv(parity, 1)[rows, :], start=True, stop=True)
                mm.then_inc(na_qk, 1)
                wait(pe, na_v_copied, s.times(1))
                for tk in range(2):
                    mm = pe.transpose(bank(6, tk * P, (tk + 1) * P),
                                      qkv(parity, 2)[:, tk * P:(tk + 1) * P], ident[:])
                mm.then_inc(na_vt_done, 1)

            def na_turn(s):
                pe.wait_ge(na_probs, s.times(1, 1))
                wait(pe, na_pt_copied, s.times(2))
                for e in range(2):
                    for tk in range(2):
                        for tq in range(2):
                            a = (2 * e + tq) * T + tk * P
                            mm = pe.transpose(bank(4 + e, tk * T + tq * P, tk * T + (tq + 1) * P),
                                              na_s[:, a:a + P], ident[:])
                mm.then_inc(na_pt_done, 1)

            def na_values(s):
                pe.wait_ge(na_pt_copied, s.times(2, 2))
                pe.wait_ge(na_v_copied, s.times(1, 1))
                wait(pe, na_lo, s.times(1))
                for e in range(2):
                    for tk in range(2):
                        mm = pe.matmul(bank(7, 0, T, 64 * e, 64 * e + 64),
                                       na_v[:, tk * P + 64 * e:tk * P + 64 * e + 64],
                                       na_pt[:, (2 * e + tk) * T:(2 * e + tk + 1) * T],
                                       start=tk == 0, stop=tk == 1, skip_group_check=True)
                mm.then_inc(na_pv, 1)

            def na_step(s, slot, parity, prev2):
                t = Pos(s.const * 6, s.per * 6, s.i)
                if prev2:
                    na_values(s + -2)
                na_scores(s + -1, 1 - parity)
                na_block(s, 0, t, slot, parity)
                na_block(s, 1, t + 2, slot + 2, parity)
                na_turn(s + -1)
                na_block(s, 2, t + 4, slot + 4, parity)

            for k in range(3):
                na_block(Pos(0), k, Pos(2 * k), 2 * k, 0)
            na_step(Pos(1), 6, 1, False)
            na_step(Pos(2), 0, 0, True)
            na_step(Pos(3), 2, 1, True)
            with pe.Fori(0, (NA_PAIRS - 4) // 2) as i:
                na_step(Pos(4, 2, i), 0, 0, True)
                na_step(Pos(5, 2, i), 2, 1, True)

            def gla_block(b, t, slot, n):
                wait(pe, proj_taken, b.times(1, -1))
                two_tiles(t, slot, bank(n % 2, 0, T), xs)

            B0 = 3 * NA_PAIRS
            na_values(Pos(NA_PAIRS - 2))
            na_scores(Pos(NA_PAIRS - 1), 1)
            gla_block(Pos(B0), Pos(T_RANK), T_RANK, B0)
            gla_block(Pos(B0 + 1), Pos(T_GLA), T_GLA, B0 + 1)
            na_turn(Pos(NA_PAIRS - 1))
            gla_block(Pos(B0 + 2), Pos(T_GLA + 2), T_GLA + 2, B0 + 2)
            na_values(Pos(NA_PAIRS - 1))
            gla_block(Pos(B0 + 3), Pos(T_GLA + 4), T_GLA + 4, B0 + 3)
            gla_block(Pos(B0 + 4), Pos(T_GLA + 6), T_GLA + 6, B0 + 4)
            B1 = B0 + 5

            def decay_inputs(h):
                pe.wait_ge(up_landed, h.times(16, 16))
                pe.wait_ge(consts_ready, 2)
                pe.wait_ge(proj_taken, B0 + 1)
                for d in range(2):
                    for kb in range(NKB):
                        mm = pe.matmul(bank(2 + d, kb * T, (kb + 1) * T),
                                       g_up[32 * d:32 * d + 32, kb * P:(kb + 1) * P],
                                       g_rank[32 * d:32 * d + 32, :], start=True, stop=True)
                mm.then_inc(la_done, 1)

            def turn_outputs(h):
                pe.wait_ge(on_done, h.times(1, 1))
                if h.i is not None or h.const < GLA_HEADS - 1:
                    pe.wait_ge(z_done, h.times(1, 2))
                for vb in range(NVB):
                    for tt in range(2):
                        mm = pe.transpose(bank(2 + vb // 2, vb % 2 * T + tt * P, vb % 2 * T + (tt + 1) * P),
                                          g_on[:, tt * DV + vb * P:tt * DV + (vb + 1) * P], ident[:])
                mm.then_inc(ot_done, 1)

            def intra(h):
                pe.wait_ge(decayed, h.times(1, 1))
                wait(pe, gated, h.times(1))
                pe.wait_ge(z_done, h.times(1, 1))
                for d in range(2):
                    for tt in range(2):
                        for kb in range(NKB):
                            a = (d * NKB + kb) * T + tt * P
                            mm = pe.transpose(bank(2 + d, tt * DK + kb * P, tt * DK + (kb + 1) * P),
                                              g_ks[:, a:a + P], ident[:])
                mm.then_inc(kt_done, 1)
                for d in range(2):
                    for n in range(N_CHUNKS):
                        rows, tt = 64 * (n % 2), n // 2
                        dst = bank(4, (d * 2 + tt) * CHUNK, (d * 2 + tt + 1) * CHUNK, rows, rows + 64)
                        for kb in range(NKB):
                            a = (d * NKB + kb) * T + n * CHUNK
                            mm = pe.matmul(dst, g_ki[:, a:a + CHUNK], g_qd[:, a:a + CHUNK],
                                           start=kb == 0, stop=kb == NKB - 1, skip_group_check=True)
                mm.then_inc(att_done, 1)

            def turn_values(h, b):
                pe.wait_ge(proj_taken, b)
                pe.wait_ge(kt_copied, h.times(2, 2))
                for tt in range(2):
                    for vb in range(NVB):
                        mm = pe.transpose(bank(2 + tt, vb * P, (vb + 1) * P),
                                          g_vt[:, vb * T + tt * P:vb * T + (tt + 1) * P], ident[:])
                mm.then_inc(vt_done, 1)

            def recur(h, m):
                if m == 0:
                    pe.wait_ge(v_copied, h.times(2, 2))
                    pe.wait_ge(att_masked, h.times(1, 1))
                    wait(pe, on_done, h.times(1))
                    for tt in range(2):
                        pe.matmul(bank(6 + tt), zeros[:], zeros[:].unsqueeze(1).to_broadcast([P, 4, P]),
                                  start=True, stop=False, skip_group_check=True)
                    for n in range(N_CHUNKS):
                        r0, tt = 64 * (n % 2), n // 2
                        pe.matmul(bank(6 + tt, 0, DV, r0, r0 + 64),
                                  g_att[r0:r0 + 64, tt * CHUNK:(tt + 1) * CHUNK],
                                  g_v[r0:r0 + 64, tt * DV:(tt + 1) * DV],
                                  start=False, stop=False, skip_group_check=True)
                else:
                    pe.wait_ge(state_done, h.times(3, m))
                for d in range(2):
                    n = m if d == 0 else N_CHUNKS - 1 - m
                    r0, tt = 64 * (n % 2), n // 2
                    if m > 0:
                        for kb in range(NKB):
                            a = (d * NKB + kb) * T + n * CHUNK
                            mm = pe.matmul(bank(6 + tt, 0, DV, r0, r0 + 64), g_qd[:, a:a + CHUNK],
                                           g_state[:, (d * NKB + kb) * DV:(d * NKB + kb + 1) * DV],
                                           start=False, stop=False, skip_group_check=True)
                if m < N_CHUNKS - 1:
                    for d in range(2):
                        n = m if d == 0 else N_CHUNKS - 1 - m
                        r0, tt = 64 * (n % 2), n // 2
                        for kb in range(NKB):
                            a = (d * 2 + tt) * DK + kb * P
                            mm = pe.matmul(bank(2 + d * NKB + kb), g_kt[r0:r0 + 64, a:a + P],
                                           g_v[r0:r0 + 64, tt * DV:(tt + 1) * DV],
                                           start=True, stop=True, skip_group_check=True)
                    mm.then_inc(gain_done, 1)
                else:
                    mm.then_inc(o_done, 1)

            def gla_head(h, t, b, first):
                decay_inputs(h)
                for k in range(12):
                    if k == 3 and not first:
                        turn_outputs(h + -1)
                    if k == 6:
                        intra(h)
                    if k == 7:
                        turn_values(h, b.times(1, 4))
                    if k >= 9:
                        recur(h, k - 9)
                    gla_block(b + k, t + 2 * k, T_GLA + QK_TILES + 2 * k, B1 + k)
                recur(h, 3)

            gla_head(Pos(0), Pos(T_GLA + QK_TILES), Pos(B1), True)
            with pe.Fori(0, GLA_HEADS - 1) as i:
                gla_head(Pos(1, 1, i), Pos(T_GLA + QK_TILES + HEAD_TILES, HEAD_TILES, i),
                         Pos(B1 + 12, 12, i), False)
            H = GLA_HEADS - 1

            def merge_step(c, t, slot, parity):
                wait(pe, merged, c.times(1, -1))
                b = 4 * parity
                two_tiles(t, slot, bank(b, 0, T), xs)
                half_block(t + 2, slot + 2, bank(b + 1, 0, T), nas, True, True)
                two_tiles(t + 3, slot + 3, bank(b + 2, 0, T), xs)
                two_tiles(t + 5, slot + 5, bank(b + 3, 0, T), gls)

            pe.wait_ge(proj_taken, B1 + 12 * GLA_HEADS)
            half_block(Pos(T_FIRST), T_FIRST, bank(1, 0, T), nas, True, True)
            turn_outputs(Pos(H))
            half_block(Pos(T_FIRST + 1), T_FIRST + 1, bank(5, 0, T), nas, True, True)
            pe.wait_ge(o_lo, GLA_HEADS)
            for k in range(2):
                two_tiles(Pos(T_FIRST + 2 + 2 * k), T_FIRST + 2 + 2 * k, bank(4 * k + 3, 0, T), gls)
            for k in range(2, 4):
                merge_step(Pos(k), Pos(T_MERGE + 7 * k), T_MERGE + 7 * k, k % 2)
            with pe.Fori(0, KC // 4 - 1) as i:
                for k in range(4):
                    merge_step(Pos(4 + k, 4, i), Pos(T_MERGE + 28 + 7 * k, 28, i), T_MERGE + 7 * k, k % 2)

            pe.wait_ge(merged, KC - 1)
            pe.wait_ge(m_lo, KC - 2)
            by_token(T_OUT, ms, merged, m_lo)

            pe.wait_ge(p_lo, 1)
            for half in range(2):
                pe.wait_ge(res_done, 4 * (half + 1))
                for k in range(2):
                    products_by_token(Pos(T_PLE + 2 * half + k), T_PLE + 2 * half + k,
                                      ys[:, k * 2 * T:(k + 1) * 2 * T],
                                      lambda tt, n: bank(4 * tt + 2 * half + n), k == 0, k == 1)
            pe.wait_ge(ple_taken, 4)
            turn_normed(1, tok, (ple_taken, 8))
            pe.wait_ge(ln_part_a, 5)

            def query_block(c, t, slot, parity, norm=None):
                wait(pe, pq_taken, c.times(1, -1))
                two_tiles(t, slot, bank(parity, 0, T), xs, norm)

            def key_scores(c, parity):
                pe.wait_ge(pq_taken, c.times(1, 1))
                wait(pe, sc_taken, c.times(1, -1))
                for tt in range(2):
                    a = parity * T + tt * P
                    mm = pe.matmul(bank(2 + parity, tt * NKEYS, (tt + 1) * NKEYS), pq[:, a:a + P],
                                   key_t[:, ds(c.times(NKEYS), NKEYS)], start=True, stop=True)
                mm.then_inc(sc_done, 1)

            query_block(Pos(0), Pos(T_PQ), T_PQ, 0, norm=4)
            pe.wait_ge(keys_landed, 16)
            query_block(Pos(1), Pos(T_PQ + 2), T_PQ + 2, 1)
            key_scores(Pos(0), 0)

            def two_queries(c, t):
                query_block(c, t, T_PQ, 0)
                key_scores(c + -1, 1)
                query_block(c + 1, t + 2, T_PQ + 2, 1)
                key_scores(c, 0)

            two_queries(Pos(2), Pos(T_PQ + 4))
            with pe.Fori(0, KC // 2 - 2) as i:
                two_queries(Pos(4, 2, i), Pos(T_PQ + 8, 4, i))
            key_scores(Pos(KC - 1), 1)

            pe.wait_ge(sc_taken, HP)
            by_token(T_PGATE, xs)

            pe.wait_ge(gsig, 4)

            def hidden(j, t, slot, n):
                wait(pe, gelu_done, j.times(1, -1))
                two_tiles(t, slot, bank(n % 2, 0, T), xs)

            for n in range(4):
                hidden(Pos(n), Pos(T_U + 2 * n), T_U + 2 * n, n)
            with pe.Fori(0, 15) as i:
                for n in range(4):
                    hidden(Pos(4 + n, 4, i), Pos(T_U + 8 + 2 * n, 8, i), T_U + 2 * n, n)
            for n in range(2):
                hidden(Pos(64 + n), Pos(T_U + 128 + 2 * n), T_U + 2 * n, n)
            pe.wait_ge(ex_done, 1)
            pe.wait_ge(gsig, 8)
            for tt in range(2):
                for k, src in enumerate((ex[:, 0:2 * P], ex[:, 2 * P:4 * P], exg)):
                    mm = pe.transpose(bank(2 + k // 2, k % 2 * T + tt * P, k % 2 * T + (tt + 1) * P),
                                      src[:, tt * P:(tt + 1) * P], ident[:])
            mm.then_inc(ex_t_done, 1)

            def spread_gates(g, n):
                pe.wait_ge(hot_ready, g.times(8, 8))
                wait(pe, gate_taken, g.times(1, -1))
                for q in range(4):
                    mm = pe.matmul(bank(2 + n % 2, q * NKEYS, (q + 1) * NKEYS),
                                   hot0[:, q * NKEYS:(q + 1) * NKEYS], hot1[:, q * NKEYS:(q + 1) * NKEYS],
                                   start=True, stop=True)
                mm.then_inc(gate_mm, 1)

            def hidden_and_gates(j, t, slot, n, g, m):
                wait(pe, gelu_done, j.times(1, -1))
                half_block(t, slot, bank(n % 2, 0, T), xs, True, False)
                if n % 4 == 3:
                    spread_gates(g, m)
                half_block(t + 1, slot + 1, bank(n % 2, 0, T), xs, False, True, k0=8)
                spread_gates(g + 1 if n % 4 == 3 else g, m + 1 if n % 4 == 3 else m)

            hidden(Pos(66), Pos(T_U + 132), T_U + 4, 2)
            pe.wait_ge(ex_t_taken, 3)
            hidden_and_gates(Pos(67), Pos(T_U + 134), T_U + 6, 3, Pos(0), 0)
            with pe.Fori(0, 6) as i:
                for n in range(8):
                    m = n + n // 4
                    hidden_and_gates(Pos(68 + n, 8, i), Pos(T_U + 136 + 2 * n, 16, i), T_U + 2 * n, n,
                                     Pos(2 + m, 10, i), m)
            for n in range(2):
                hidden_and_gates(Pos(116 + n), Pos(T_U + 232 + 2 * n), T_U + 2 * n, n, Pos(62 + n), n)
            with pe.Fori(0, 2) as i:
                for n in range(4):
                    hidden(Pos(118 + n, 4, i), Pos(T_U + 236 + 2 * n, 8, i), T_U + 236 + 2 * n, n)
            for n in range(8, 10):
                hidden(Pos(118 + n), Pos(T_U + 236 + 2 * n), T_U + 236 + 2 * n, n)

            pe.wait_ge(gelu_done, NKEYS)
            pe.wait_ge(gate_taken, T // 4)
            def half_out(t, slot, parity, half, first=False):
                products_by_token(t, slot, ys[:, parity * 2 * T:(parity + 1) * 2 * T],
                                  lambda tt, n: bank(4 * tt + 2 * half + n), first, False)

            def expert_out(j, t, slot, parity, first=False):
                pe.wait_ge(w_lo, j.times(1, 1))
                for half in range(2):
                    half_out(t + half, slot + half, parity, half, first)

            expert_out(Pos(0), Pos(T_V), T_V, 0, True)
            expert_out(Pos(1), Pos(T_V + 2), T_V + 2, 1)
            with pe.Fori(0, NKEYS // 2 - 2) as i:
                expert_out(Pos(2, 2, i), Pos(T_V + 4, 4, i), T_V, 0)
                expert_out(Pos(3, 2, i), Pos(T_V + 6, 4, i), T_V + 2, 1)
            for n in range(4):
                if n < 2:
                    pe.wait_ge(w_lo, NKEYS - 1 + n)
                half_out(Pos(T_END - 4 + n), T_END - 4 + n, n % 2, n // 2)

        @block.scalar
        def _(act):
            def upper(t, slot):
                act.wait_ge(landed[slot % RING], t.over(RING).times(16, 16))
                s = slice(slot % RING * TILE, (slot % RING + 1) * TILE)
                act.activation(w_up[:, s], w_in[:, s], ACT.Copy).then_inc(hi_ready, 1)

            def hi(t, slot):
                if t.i is not None or t.const + AHEAD < T_END:
                    upper(t + AHEAD, slot + AHEAD)

            def std(n, tt):
                act.wait_ge(ln_var, 2 * n + tt + 1)
                act.activation(ln_sd[:, 2 * tt:2 * tt + 1], ln_mv[:, 2 * tt + 1:2 * tt + 2], ACT.Sqrt,
                               bias=eps_t[:]).then_inc(ln_std, 1)

            def features(n, dst):
                for g in range(5):
                    if g < 4:
                        act.wait_ge(ln_turned, 2 * n + g // 2 + 1)
                        for c in range(4 * g, 4 * g + 2):
                            ins = act.activation(dst[:, c * T:(c + 1) * T], feature_bank(c, 0, T),
                                                 ACT.Identity, scale=norm_gain(n, c), bias=norm_shift(n, c))
                        ins.then_inc(ln_part_a, 1)
                    if g > 0:
                        act.wait_ge(ln_part_a, 4 * n + g)
                        act.wait_ge(ln_part_d, 4 * n + g)
                        up = xs[:, (g - 1) * 8 * T:g * 8 * T].rearrange("p (c s t) -> p c s t", c=4, s=2)[:, :, 0, :]
                        src = dst[:, (g - 1) * 4 * T:g * 4 * T].rearrange("p (c t) -> p c t", c=4)
                        act.activation(up, src, ACT.Copy).then_inc(ln_hi, 1)

            act.wait_ge(consts_ready, 1)
            std(0, 0)
            act.wait_ge(ln_shift_ready, 1)
            act.activation(x_tok[:, 0:D], x_tok[:, 0:D], ACT.Identity, scale=ln_sd[:, 1:2],
                           bias=ln_shift[:]).then_inc(ln_normed[0], 1)
            std(0, 1)
            for k in range(AHEAD):
                upper(Pos(k), k)
            hi(Pos(0), 0)
            hi(Pos(1), 1)

            act.wait_ge(vec_landed, 16)
            features(0, x_feat)

            def na_take(s, k, t, parity):
                act.wait_ge(tile_used, t.times(1, 2))
                if k == 0:
                    wait(act, na_pv, s.times(1, -1))
                    if s.i is None and s.const < 2:
                        act.wait_ge(ln_lo, 4)
                a = (parity * 3 + k) * T
                act.activation(na_qkv[:, a:a + T], bank((3 * parity + k) % 2, 0, T), ACT.Identity,
                               bias=vec[:, ds(s.times(3, V_NA + k), 1)]).then_inc(proj_taken, 1)

            def na_exps(s):
                act.wait_ge(na_negmax, s.times(1, 1))
                for k in range(4):
                    act.activation(na_s[:, k * T:(k + 1) * T], na_s[:, k * T:(k + 1) * T], ACT.Exp,
                                   bias=na_small[:, 4 + k:5 + k],
                                   accum_out=na_small[:, 8 + k:9 + k]).then_inc(na_exp, 1)
                act.wait_ge(na_vt_done, s.times(1, 1))
                wait(act, na_pv, s.times(1))
                act.activation(na_v[:], bank(6, 0, 2 * P), ACT.Copy).then_inc(na_v_copied, 1)

            def na_norm(s):
                act.wait_ge(na_rinv, s.times(1, 1))
                act.wait_ge(na_exp, s.times(4, 4))
                for k in range(4):
                    ins = act.activation(na_s[:, k * T:(k + 1) * T], na_s[:, k * T:(k + 1) * T],
                                         ACT.Copy, scale=na_small[:, 12 + k:13 + k])
                ins.then_inc(na_probs, 1)

            def na_out(s):
                act.wait_ge(na_pv, s.times(1, 1))
                act.activation(nas[:, ds(s.times(2 * T), T)], bank(7, 0, T), ACT.Copy).then_inc(na_hi, 1)

            def na_step(s, slot, parity, prev2):
                t = Pos(s.const * 6, s.per * 6, s.i)
                hi(t, slot)
                na_take(s + -1, 2, t + -2, 1 - parity)
                if prev2:
                    na_out(s + -2)
                hi(t + 1, slot + 1)
                na_exps(s + -1)
                hi(t + 2, slot + 2)
                na_take(s, 0, t, parity)
                hi(t + 3, slot + 3)
                na_norm(s + -1)
                hi(t + 4, slot + 4)
                na_take(s, 1, t + 2, parity)
                hi(t + 5, slot + 5)

            hi(Pos(2), 2)
            na_take(Pos(0), 0, Pos(0), 0)
            hi(Pos(3), 3)
            hi(Pos(4), 4)
            na_take(Pos(0), 1, Pos(2), 0)
            hi(Pos(5), 5)
            na_step(Pos(1), 6, 1, False)
            with act.Fori(0, (NA_PAIRS - 2) // 2) as i:
                na_step(Pos(2, 2, i), 0, 0, True)
                na_step(Pos(3, 2, i), 2, 1, True)

            B0 = 3 * NA_PAIRS
            B1 = B0 + 5
            chain = Chain(act, gla_act, 6)

            def take(dst, n, t, col):
                act.wait_ge(tile_used, t.times(1, 2))
                act.activation(dst, bank(n % 2, 0, T), ACT.Identity,
                               bias=vec[:, ds(col.times(1), 1)]).then_inc(proj_taken, 1)

            def take_gate(vb, n, t, col):
                act.wait_ge(tile_used, t.times(1, 2))
                a, b = vb * T, (vb + 1) * T
                act.activation(g_x[:, a:b], bank(n % 2, 0, T), ACT.Identity,
                               bias=vec[:, ds(col.times(1), 1)])
                act.activation(g_sg[:, a:b], bank(n % 2, 0, T), ACT.Sigmoid,
                               bias=vec[:, ds(col.times(1), 1)]).then_inc(proj_taken, 1)

            def decay_logs(h, part):
                if part == 0:
                    chain.begin(h)
                    act.wait_ge(la_done, h.times(1, 1))
                    for k in range(4):
                        chain.step(act.activation(g_z[:, k * T:(k + 1) * T],
                                                  bank(2 + k // 2, k % 2 * T, (k % 2 + 1) * T), ACT.Identity,
                                                  bias=vec[:, ds(h.times(4, V_DECAY + k), 1)]))
                elif part == 1:
                    chain.step(act.activation(g_a[:], g_z[:], ACT.Abs))
                    chain.step(act.activation(g_a[:], g_a[:], ACT.Exp, scale=-1.0))
                else:
                    act.activation(g_a[:], g_a[:], ACT.Ln, bias=1.0).then_inc(z_done, 1)
                    chain.end()

            def decay_exps(h, part):
                if part == 0:
                    act.wait_ge(gap_done, h.times(1, 1))
                    wait(act, o_done, h.times(1))
                    act.activation(g_qd[:], g_c[:], ACT.Exp, scale=1.0 / 16).then_inc(exp_done, 1)
                elif part == 1:
                    act.activation(g_ki[:], g_c[:], ACT.Exp, scale=-1.0 / 16).then_inc(exp_done, 1)
                else:
                    act.activation(g_ks[:], g_a[:], ACT.Exp, scale=1.0 / 16)
                    c = g_c[:].rearrange("p (d k c) -> p d k c", d=2, c=CHUNK)
                    dec = g_dec[:].rearrange("p (d k c) -> p d k c", d=2, c=1)
                    act.activation(dec[:, 0], c[:, 0, :, CHUNK - 1:CHUNK], ACT.Exp, scale=1.0 / 16)
                    act.activation(dec[:, 1], c[:, 1, :, 0:1], ACT.Exp, scale=1.0 / 16).then_inc(exp_done, 1)

            def keys_taken(h):
                act.wait_ge(kt_done, h.times(1, 1))
                for d in range(2):
                    act.activation(g_kt[:, d * 2 * DK:(d + 1) * 2 * DK], bank(2 + d),
                                   ACT.Copy).then_inc(kt_copied, 1)

            def values_taken(h):
                act.wait_ge(vt_done, h.times(1, 1))
                for tt in range(2):
                    act.activation(g_v[:, tt * DV:(tt + 1) * DV], bank(2 + tt), ACT.Copy).then_inc(v_copied, 1)

            def out_rms(h):
                act.wait_ge(o_done, h.times(1, 1))
                for tt in range(2):
                    ins = act.activation(g_on[:, tt * DV:(tt + 1) * DV], bank(6 + tt), ACT.Square,
                                         accum_out=g_small[:, tt:tt + 1])
                ins.then_inc(rms_done, 1)
                act.wait_ge(rms_done, h.times(2, 1))
                act.activation(g_small[:, 2:4], g_small[:, 0:2], ACT.Sqrt, bias=eps_t[:],
                               scale=1.0 / DV).then_inc(rms_done, 1)

            def out_hi(h):
                act.wait_ge(gated, h.times(1, 1))
                dst = gls[:, ds(h.times(NVB * 2 * T), NVB * 2 * T)].rearrange(
                    "p (c s t) -> p c s t", c=NVB, s=2)[:, :, 0, :]
                act.activation(dst, g_ot[:].rearrange("p (c t) -> p c t", c=NVB), ACT.Copy).then_inc(o_hi, 1)

            NL = NA_PAIRS - 1
            hi(Pos(T_RANK), T_RANK)
            na_take(Pos(NL), 2, Pos(T_RANK - 2), NL % 2)
            na_out(Pos(NL - 1))
            hi(Pos(T_RANK + 1), T_RANK + 1)
            na_exps(Pos(NL))
            hi(Pos(T_RANK + 2), T_RANK + 2)
            na_norm(Pos(NL))
            hi(Pos(T_RANK + 3), T_RANK + 3)

            def gla_take(h, k, n, t):
                col = Pos(V_GLA + k + GLA_BLOCKS * h.const, GLA_BLOCKS * h.per, h.i)
                if k < 2:
                    take(g_q[:, k * T:(k + 1) * T], n, t, col)
                elif k < 4:
                    take(g_k[:, (k - 2) * T:(k - 1) * T], n, t, col)
                elif k < 8:
                    take(g_vt[:, (k - 4) * T:(k - 3) * T], n, t, col)
                else:
                    take_gate(k - 8, n, t, col)

            act.wait_ge(h_spilled, 32)
            take(g_rank[:], B0, Pos(T_RANK), Pos(V_RANK))
            hi(Pos(T_GLA + 2), T_GLA + 2)
            gla_take(Pos(0), 0, B0 + 1, Pos(T_GLA))
            hi(Pos(T_GLA + 3), T_GLA + 3)
            hi(Pos(T_GLA + 4), T_GLA + 4)
            gla_take(Pos(0), 1, B0 + 2, Pos(T_GLA + 2))
            na_out(Pos(NL))
            hi(Pos(T_GLA + 5), T_GLA + 5)
            hi(Pos(T_GLA + 6), T_GLA + 6)
            gla_take(Pos(0), 2, B0 + 3, Pos(T_GLA + 4))
            hi(Pos(T_GLA + 7), T_GLA + 7)

            def early_gate(k, n, t):
                act.wait_ge(tile_used, t.times(1, 2))
                act.activation(g_early[:, k * T:(k + 1) * T], bank(n % 2, 0, T), ACT.Sigmoid,
                               bias=vec[:, V_GATES + k:V_GATES + k + 1]).then_inc(proj_taken, 1)

            def gla_head(h, t, last, first):
                s0 = T_GLA + QK_TILES
                for k in range(12):
                    if k == 8:
                        values_taken(h)
                    hi(t + 2 * k, s0 + 2 * k)
                    if k == 0:
                        gla_take(h, 3, B1 - 1, t + -2)
                    elif k <= 8:
                        gla_take(h, 3 + k, B1 + k - 1, t + 2 * (k - 1))
                    elif last:
                        early_gate(k - 9, B1 + k - 1, t + 2 * (k - 1))
                    else:
                        gla_take(h + 1, k - 9, B1 + k - 1, t + 2 * (k - 1))
                    if k == 1:
                        decay_logs(h, 1)
                    if k == 3:
                        decay_exps(h, 0)
                    if k == 4:
                        decay_exps(h, 2)
                    hi(t + 2 * k + 1, s0 + 2 * k + 1)
                    if k == 0:
                        if not first:
                            out_rms(h + -1)
                        decay_logs(h, 0)
                    if k == 1:
                        decay_logs(h, 2)
                    if k == 3:
                        decay_exps(h, 1)
                    if k == 4 and not first:
                        out_hi(h + -1)
                    if k == 6:
                        keys_taken(h)

            s_h = T_GLA + QK_TILES
            gla_head(Pos(0), Pos(s_h), False, True)
            with act.Fori(0, GLA_HEADS - 2) as i:
                gla_head(Pos(1, 1, i), Pos(s_h + HEAD_TILES, HEAD_TILES, i), False, False)
            H = GLA_HEADS - 1
            gla_head(Pos(H), Pos(s_h + H * HEAD_TILES), True, False)
            hi(Pos(T_FIRST), T_FIRST)
            early_gate(3, B1 + 11, Pos(T_FIRST - 2))
            hi(Pos(T_FIRST + 1), T_FIRST + 1)
            out_rms(Pos(H))
            hi(Pos(T_FIRST + 2), T_FIRST + 2)
            out_hi(Pos(H))
            for k in range(3, 6):
                hi(Pos(T_FIRST + k), T_FIRST + k)

            def sigmoid(dst, parity, n, t, col, done, c, freed):
                act.wait_ge(tile_used, t.times(1, 2))
                wait(act, freed, c.times(1, -1))
                act.activation(dst[:, parity * T:(parity + 1) * T], bank(4 * parity + n, 0, T),
                               ACT.Sigmoid, bias=vec[:, ds(col.times(1), 1)]).then_inc(done, 1)

            def merged_hi(c, parity):
                act.wait_ge(merged, c.times(1, 1))
                act.activation(ms[:, ds(c.times(2 * T), T)], m_m[:, parity * T:(parity + 1) * T],
                               ACT.Copy).then_inc(m_hi, 1)

            def merge_step(c, t, slot, parity):
                for k in range(MERGE_TILES):
                    hi(t + k, slot + k)
                    if k == 3:
                        sigmoid(m_sa, parity, 0, t, Pos(V_GATES + 2 * c.const, 2 * c.per, c.i),
                                sig_a, c, a_gated)
                        merged_hi(c + -1, 1 - parity)
                    if k == 6:
                        sigmoid(m_sb, parity, 2, t + 3, Pos(V_GATES + 1 + 2 * c.const, 2 * c.per, c.i),
                                sig_b, c, merged)

            merged_hi(Pos(0), 0)
            for k in range(2, 4):
                merge_step(Pos(k), Pos(T_MERGE + 7 * k), T_MERGE + 7 * k, k % 2)
            with act.Fori(0, KC // 4 - 1) as i:
                for k in range(4):
                    merge_step(Pos(4 + k, 4, i), Pos(T_MERGE + 28 + 7 * k, 28, i), T_MERGE + 7 * k, k % 2)
            hi(Pos(T_OUT), T_OUT)
            hi(Pos(T_OUT + 1), T_OUT + 1)
            merged_hi(Pos(KC - 1), 1)

            for k in range(2, 4):
                hi(Pos(T_OUT + k), T_OUT + k)
            act.wait_ge(p_landed, 16)
            p_dst = ys[:].rearrange("p (c s t) -> p c s t", c=2, s=2)[:, :, 0, :]
            act.activation(p_dst, p_in[:].rearrange("p (c t) -> p c t", c=2), ACT.Copy).then_inc(p_hi, 1)
            with act.Fori(0, 7) as i:
                for k in range(4):
                    hi(Pos(T_OUT + 4 + k, 4, i), T_OUT + k)

            def take_ple(half):
                act.wait_ge(tile_used, T_PLE + 2 * (half + 1))
                for tt in range(2):
                    for n in range(2):
                        a = tt * D + half * 1024 + n * 512
                        act.activation(ple[:, a:a + 512], bank(4 * tt + 2 * half + n),
                                       ACT.Copy).then_inc(ple_taken, 1)

            for k in range(3):
                hi(Pos(T_PLE + k), T_PLE + k)
            std(1, 0)
            take_ple(0)
            std(1, 1)
            hi(Pos(T_PLE + 3), T_PLE + 3)
            take_ple(1)
            hi(Pos(T_PQ), T_PQ)
            hi(Pos(T_PQ + 1), T_PQ + 1)
            features(1, h_feat)

            def take_query(c, t, parity):
                act.wait_ge(tile_used, t.times(1, 2))
                wait(act, sc_done, c.times(1, -1))
                act.activation(pq[:, parity * T:(parity + 1) * T], bank(parity, 0, T),
                               ACT.Copy).then_inc(pq_taken, 1)

            def take_scores(c, parity):
                act.wait_ge(sc_done, c.times(1, 1))
                for tt in range(2):
                    ins = act.activation(sc[:, ds(c.times(NKEYS, tt * HP * NKEYS), NKEYS)],
                                         bank(2 + parity, tt * NKEYS, (tt + 1) * NKEYS), ACT.Copy)
                ins.then_inc(sc_taken, 1)

            hi(Pos(T_PQ + 2), T_PQ + 2)
            take_query(Pos(0), Pos(T_PQ), 0)
            hi(Pos(T_PQ + 3), T_PQ + 3)

            def two_queries(c, t):
                hi(t + 2, T_PQ)
                take_query(c, t, 1)
                take_scores(c + -1, 0)
                hi(t + 3, T_PQ + 1)
                hi(t + 4, T_PQ + 2)
                take_query(c + 1, t + 2, 0)
                take_scores(c, 1)
                hi(t + 5, T_PQ + 3)

            two_queries(Pos(1), Pos(T_PQ + 2))
            with act.Fori(0, KC // 2 - 2) as i:
                two_queries(Pos(3, 2, i), Pos(T_PQ + 6, 4, i))
            hi(Pos(T_PGATE), T_PGATE)
            take_query(Pos(KC - 1), Pos(T_PQ + 30), 1)
            take_scores(Pos(KC - 2), 0)
            take_scores(Pos(KC - 1), 1)

            def take_ple_gate(half, n):
                act.wait_ge(tile_used, T_PGATE + KC * (half + 1))
                q = 4 * half + n
                wait(act, res2_done, q - 1)
                act.activation(sgm[:, q % 2 * 512:(q % 2 + 1) * 512], bank(4 * (n // 2) + 2 * half + n % 2),
                               ACT.Sigmoid).then_inc(gsig, 1)

            for k in range(1, 4):
                hi(Pos(T_PGATE + k), T_PGATE + k)
            with act.Fori(0, 3) as i:
                for k in range(4):
                    hi(Pos(T_PGATE + 4 + k, 4, i), T_PGATE + k)
            for k in range(16, 32):
                hi(Pos(T_PGATE + k), T_PGATE + k)
                if 17 <= k < 21:
                    take_ple_gate(0, k - 17)

            def gelu(j, t, n):
                act.wait_ge(tile_used, t.times(1, 2))
                wait(act, gelu_stored[n], j.over(4).times(16))
                act.activation(gst[:, n * T:(n + 1) * T], bank(n % 2, 0, T), ACT.Gelu).then_inc(gelu_done, 1)

            def unit_scores(u):
                if u.i is not None or u.const > 0:
                    act.wait_ge(tk_chain, u.times(TOP_STEPS, TOP_KEY_STEPS - TOP_STEPS))
                act.activation(tk_in[:], sc[:, ds(u.times(2 * NKEYS), 2 * NKEYS)], ACT.Copy).then_inc(tk_loaded, 1)

            def take_gates(g, n):
                act.wait_ge(gate_mm, g.times(1, 1))
                act.activation(gates[:, ds(g.times(4 * NKEYS), 4 * NKEYS)], bank(2 + n % 2),
                               ACT.Copy).then_inc(gate_taken, 1)

            def weight_hi(j, parity):
                act.wait_ge(w_ready, j.times(1, 1))
                if j.i is not None or j.const >= 2:
                    act.wait_ge(tile_used, j.times(2, T_V - 2))
                act.activation(ys[:, parity * 2 * T:parity * 2 * T + T],
                               wexp[:, parity * T:(parity + 1) * T], ACT.Copy).then_inc(w_hi, 1)

            def hidden_steps(j, t, unit, first=False, last=False):
                for n in range(4):
                    hi(t + 2 * n, T_U + 2 * n)
                    if first:
                        take_ple_gate(1, n)
                    if n > 0 or not first:
                        gelu(j + (n - 1), t + (2 * n - 2), (n - 1) % 4)
                    hi(t + 2 * n + 1, T_U + 2 * n + 1)
                    if n == 3 and not last:
                        unit_scores(unit + 1)

            act.wait_ge(sc_taken, HP)
            unit_scores(Pos(0))
            hidden_steps(Pos(0), Pos(T_U), Pos(0), first=True)
            hidden_steps(Pos(4), Pos(T_U + 8), Pos(1))
            with act.Fori(0, 13) as i:
                hidden_steps(Pos(8, 4, i), Pos(T_U + 16, 8, i), Pos(2, 1, i))
            hidden_steps(Pos(60), Pos(T_U + 120), Pos(15), last=True)

            def column(j, t, n, groups=()):
                hi(t, T_U + 2 * n)
                gelu(j + -1, t + -2, (n - 1) % 4)
                for g, m in groups[:1]:
                    take_gates(g, m)
                hi(t + 1, T_U + 2 * n + 1)
                for g, m in groups[1:]:
                    take_gates(g, m)

            column(Pos(64), Pos(T_U + 128), 0)
            act.wait_ge(tk_chain, HP * TOP_STEPS)
            act.activation(exg[:], exg[:], ACT.Exp).then_inc(tk_exp, 1)
            column(Pos(65), Pos(T_U + 130), 1)
            column(Pos(66), Pos(T_U + 132), 2)
            act.wait_ge(ex_t_done, 1)
            for k, dst in enumerate((idx0_t, idx1_t, gate_t)):
                act.activation(dst[:], bank(2 + k // 2, k % 2 * T, (k % 2 + 1) * T),
                               ACT.Copy).then_inc(ex_t_taken, 1)
            column(Pos(67), Pos(T_U + 134), 3)
            act.wait_ge(res_spilled, 16)
            with act.Fori(0, 6) as i:
                for n in range(8):
                    m = n - 1 + (n - 1) // 4
                    before = [(Pos(2 + m, 10, i), m % 2)]
                    if n % 4 == 0:
                        before.append((Pos(3 + m, 10, i), (m + 1) % 2))
                    column(Pos(68 + n, 8, i), Pos(T_U + 136 + 2 * n, 16, i), n % 4, before)
            column(Pos(116), Pos(T_U + 232), 0, [(Pos(60), 0), (Pos(61), 1)])
            column(Pos(117), Pos(T_U + 234), 1, [(Pos(62), 0)])
            column(Pos(118), Pos(T_U + 236), 2, [(Pos(63), 1)])
            for n in range(119, 128):
                column(Pos(n), Pos(T_U + 2 * n), n % 4)
                if n >= 126:
                    weight_hi(Pos(n - 126), n - 126)
            hi(Pos(T_V), T_V)
            gelu(Pos(127), Pos(T_U + 254), 3)
            hi(Pos(T_V + 1), T_V + 1)

            for k in range(2 + AHEAD, 4):
                upper(Pos(T_V + k), T_V + k)
            with act.Fori(0, NKEYS // 2 - 1) as i:
                for k in range(2):
                    upper(Pos(T_V + 4 + 2 * k, 4, i), T_V + 2 * k)
                    weight_hi(Pos(2 + k, 2, i), k)
                    upper(Pos(T_V + 5 + 2 * k, 4, i), T_V + 2 * k + 1)
            for tt in range(2):
                std(2, tt)

        @block.vector
        def _(dve):
            def lower(t, slot):
                dve.wait_ge(hi_ready, t.times(1, 1))
                s = slice(slot % RING * TILE, (slot % RING + 1) * TILE)
                dve.tensor_tensor(w_low[:, s], w_in[:, s], w_up[:, s].bitcast(F32),
                                  ALU.subtract).then_inc(split_ready, 1)

            def lo(t, slot):
                if t.i is not None or t.const + AHEAD < T_END:
                    lower(t + AHEAD, slot + AHEAD)

            ln_c = Line(dve, ln_chain)

            def stats(x, tt, q):
                return dve.bn_stats(ln_st[:, (tt * 4 + q) * 6:(tt * 4 + q + 1) * 6],
                                    x[:, tt * D + q * 512:tt * D + (q + 1) * 512])

            def mean_var(tt):
                dve.bn_aggr(ln_mv[:, 2 * tt:2 * tt + 2], ln_st[:, tt * 24:(tt + 1) * 24]).then_inc(ln_var, 1)

            def inverse_std(n, tt):
                dve.wait_ge(ln_std, 2 * n + tt + 1)
                dve.wait_ge(ln_var, 2 * n + tt + 1)
                ln_c.step(dve.reciprocal(ln_sd[:, 2 * tt + 1:2 * tt + 2], ln_sd[:, 2 * tt:2 * tt + 1]))

            def shift():
                inverse_std(0, 0)
                dve.scalar_tensor_tensor(out=ln_shift[:], in0=ln_mv[:, 0:1], scalar=-1.0, in1=ln_sd[:, 1:2],
                                         op0=ALU.mult, op1=ALU.mult).then_inc(ln_shift_ready, 1)

            def normalize(n, x, tt):
                inverse_std(n, tt)
                v = x[:, tt * D:(tt + 1) * D]
                dve.tensor_scalar(v, v, ln_mv[:, 2 * tt:2 * tt + 1], ln_sd[:, 2 * tt + 1:2 * tt + 2],
                                  ALU.subtract, ALU.mult).then_inc(ln_normed[tt], 1)

            def features(n, dst):
                for g in range(5):
                    if g < 4:
                        dve.wait_ge(ln_turned, 2 * n + g // 2 + 1)
                        for c in range(4 * g + 2, 4 * g + 4):
                            ins = dve.tensor_scalar(dst[:, c * T:(c + 1) * T], feature_bank(c, 0, T),
                                                    norm_gain(n, c), norm_shift(n, c), ALU.mult, ALU.add)
                        ins.then_inc(ln_part_d, 1)
                    if g > 0:
                        dve.wait_ge(ln_hi, 4 * n + g)
                        dve.wait_ge(ln_part_d, 4 * n + g)
                        d = xs[:, (g - 1) * 8 * T:g * 8 * T].rearrange("p (c s t) -> p c s t", c=4, s=2)
                        v = dst[:, (g - 1) * 4 * T:g * 4 * T].rearrange("p (c t) -> p c t", c=4)
                        dve.tensor_tensor(d[:, :, 1, :], v, d[:, :, 0, :].bitcast(F32),
                                          ALU.subtract).then_inc(ln_lo, 1)

            for tt in range(2):
                for q in range(4):
                    dve.wait_ge(x_landed[4 * tt + q], 16)
                    ins = stats(x_tok, tt, q)
                ln_c.step(ins)
                mean_var(tt)
                if tt == 0:
                    shift()
            normalize(0, x_tok, 1)
            for k in range(AHEAD):
                lower(Pos(k), k)
            dve.wait_ge(vec_landed, 16)
            features(0, x_feat)
            lo(Pos(0), 0)
            lo(Pos(1), 1)

            na_c = Chain(dve, na_chain, 1)

            def na_softmax(s, parity):
                na_c.begin(s)
                dve.wait_ge(na_qk, s.times(1, 1))
                dve.wait_ge(bias_landed[parity], s.over(2).times(16, 16) if s.i is not None
                            else 16 * (s.const // 2 + 1))
                wait(dve, na_pt_done, s.times(1))
                for e in range(2):
                    a, b = e * 2 * T, (e + 1) * 2 * T
                    ins = dve.scalar_tensor_tensor(out=na_s[:, a:b], in0=bank(2 + e), scalar=NA_DIM ** -0.5,
                                                   in1=na_bias[:, parity * 4 * T + a:parity * 4 * T + b],
                                                   op0=ALU.mult, op1=ALU.add)
                ins.then_inc(na_s_read, 1)
                dve.wait_ge(na_s_read, s.times(1, 1))
                na_c.step(dve.tensor_reduce(na_small[:, 0:4], na_s[:].rearrange("p (k t) -> p k t", k=4),
                                            AX.X, ALU.max))
                dve.tensor_scalar(na_small[:, 4:8], na_small[:, 0:4], -1.0, None, ALU.mult).then_inc(na_negmax, 1)
                na_c.end()

            def na_recip(s):
                dve.wait_ge(na_exp, s.times(4, 4))
                dve.reciprocal(na_small[:, 12:16], na_small[:, 8:12]).then_inc(na_rinv, 1)

            def na_take_turned(s):
                dve.wait_ge(na_pt_done, s.times(1, 1))
                wait(dve, na_pv, s.times(1))
                for e in range(2):
                    dve.tensor_copy(na_pt[:, e * 2 * T:(e + 1) * 2 * T], bank(4 + e)).then_inc(na_pt_copied, 1)

            def na_out_lo(s):
                dve.wait_ge(na_hi, s.times(1, 1))
                dve.tensor_tensor(nas[:, ds(s.times(2 * T, T), T)], bank(7, 0, T),
                                  nas[:, ds(s.times(2 * T), T)].bitcast(F32), ALU.subtract).then_inc(na_lo, 1)

            def na_step(s, slot, parity, prev2):
                t = Pos(s.const * 6, s.per * 6, s.i)
                lo(t, slot)
                if prev2:
                    na_out_lo(s + -2)
                na_softmax(s + -1, 1 - parity)
                lo(t + 1, slot + 1)
                lo(t + 2, slot + 2)
                na_recip(s + -1)
                lo(t + 3, slot + 3)
                lo(t + 4, slot + 4)
                lo(t + 5, slot + 5)
                na_take_turned(s + -1)

            for k in range(2, 6):
                lo(Pos(k), k)
            na_step(Pos(1), 6, 1, False)
            with dve.Fori(0, (NA_PAIRS - 2) // 2) as i:
                na_step(Pos(2, 2, i), 0, 0, True)
                na_step(Pos(3, 2, i), 2, 1, True)
            NL = NA_PAIRS - 1
            lo(Pos(T_RANK), T_RANK)
            na_out_lo(Pos(NL - 1))
            na_softmax(Pos(NL), NL % 2)
            lo(Pos(T_RANK + 1), T_RANK + 1)
            lo(Pos(T_RANK + 2), T_RANK + 2)
            na_recip(Pos(NL))
            lo(Pos(T_RANK + 3), T_RANK + 3)
            na_take_turned(Pos(NL))
            lo(Pos(T_RANK + 4), T_RANK + 4)
            lo(Pos(T_RANK + 5), T_RANK + 5)
            lo(Pos(T_RANK + 6), T_RANK + 6)
            na_out_lo(Pos(NL))
            for k in range(7, 10):
                lo(Pos(T_RANK + k), T_RANK + k)

            B1 = 3 * NA_PAIRS + 5
            gc = Chain(dve, gla_dve, 4)

            def cumulate(h, part):
                if part == 0:
                    gc.begin(h)
                    dve.wait_ge(z_done, h.times(1, 1))
                    dve.wait_ge(consts_ready, 2)
                    gc.step(dve.scalar_tensor_tensor(out=g_z[:], in0=g_z[:], scalar=0.0, in1=g_a[:],
                                                     op0=ALU.min, op1=ALU.subtract))
                    gc.step(dve.tensor_tensor_scan(g_c[:, 0:2 * T], g_reset[:], g_z[:, 0:2 * T], 0.0,
                                                   ALU.mult, ALU.add))
                    return
                back = g_c[:, 2 * T:4 * T]
                gc.step(dve.tensor_tensor_scan(back[:, ::-1], g_reset[:], g_z[:, 2 * T:4 * T][:, ::-1], 0.0,
                                               ALU.mult, ALU.add))
                for d in range(2):
                    c = g_c[:, d * 2 * T:(d + 1) * 2 * T].rearrange("p (k c) -> p k c", c=CHUNK)
                    a = g_a[:, d * 2 * T:(d + 1) * 2 * T].rearrange("p (k c) -> p k c", c=CHUNK)
                    whole = c[:, :, CHUNK - 1:CHUNK] if d == 0 else c[:, :, 0:1]
                    ins = dve.tensor_tensor(a, whole.to_broadcast([P, 2 * N_CHUNKS, CHUNK]), c, ALU.subtract)
                    if d == 0:
                        gc.step(ins)
                ins.then_inc(gap_done, 1)
                gc.end()

            def decay(h, part):
                dve.wait_ge(exp_done, h.times(3, part + 1))
                def both(x):
                    return x[:].unsqueeze(1).to_broadcast([P, 2, 2 * T])

                def dirs(x):
                    return x[:].rearrange("p (d k) -> p d k", d=2)

                if part == 0:
                    dve.scalar_tensor_tensor(out=dirs(g_qd), in0=both(g_q), scalar=DK ** -0.5, in1=dirs(g_qd),
                                             op0=ALU.mult, op1=ALU.mult)
                elif part == 1:
                    dve.tensor_tensor(dirs(g_ki), both(g_k), dirs(g_ki), ALU.mult)
                else:
                    dve.tensor_tensor(dirs(g_ks), both(g_k), dirs(g_ks), ALU.mult).then_inc(decayed, 1)

            at = Chain(dve, sem("gla_mask_chain"), 1, nop=True)

            def mask_att(h):
                at.begin(h)
                dve.wait_ge(att_done, h.times(1, 1))
                at.step(dve.tensor_copy(g_att[:], bank(4, 2 * CHUNK, 4 * CHUNK)))
                dve.copy_predicated(g_att[:], g_mask[:], bank(4, 0, 2 * CHUNK)).then_inc(att_masked, 1)
                at.end()

            def update_states(h, m):
                dve.wait_ge(gain_done, h.times(3, m + 1))
                if m > 0:
                    dve.wait_ge(state_done, h.times(3, m))
                for d in range(2):
                    n = m if d == 0 else N_CHUNKS - 1 - m
                    for kb in range(NKB):
                        q = d * NKB + kb
                        st = g_state[:, q * DV:(q + 1) * DV]
                        if m == 0:
                            ins = dve.tensor_copy(st, bank(2 + q))
                        else:
                            k = q * N_CHUNKS + n
                            ins = dve.scalar_tensor_tensor(out=st, in0=st, scalar=g_dec[:, k:k + 1],
                                                           in1=bank(2 + q), op0=ALU.mult, op1=ALU.add)
                ins.then_inc(state_done, 1)

            nc_ = Chain(dve, sem("gla_norm_chain"), 1)

            def norm_out(h):
                nc_.begin(h)
                dve.wait_ge(rms_done, h.times(2, 2))
                nc_.step(dve.reciprocal(g_small[:, 4:6], g_small[:, 2:4]))
                for tt in range(2):
                    ins = dve.tensor_scalar(g_on[:, tt * DV:(tt + 1) * DV], bank(6 + tt),
                                            g_small[:, 4 + tt:5 + tt], None, ALU.mult)
                ins.then_inc(on_done, 1)
                nc_.end()

            def gate_silu(h):
                gs.begin(h)
                dve.wait_ge(proj_taken, h.times(12, B1 + 8))
                gs.step(dve.tensor_tensor(g_x[:], g_x[:], g_sg[:], ALU.mult))
                gs.end()

            gs = Chain(dve, sem("gla_silu_chain"), 1)

            def gate_out(h):
                dve.wait_ge(ot_done, h.times(1, 1))
                for vb in range(NVB):
                    a, b = vb * T, (vb + 1) * T
                    ins = dve.scalar_tensor_tensor(
                        out=g_ot[:, a:b], in0=bank(2 + vb // 2, vb % 2 * T, (vb % 2 + 1) * T),
                        scalar=vec[:, V_NORM + vb:V_NORM + vb + 1], in1=g_x[:, a:b],
                        op0=ALU.mult, op1=ALU.mult)
                ins.then_inc(gated, 1)

            def out_lo(h):
                dve.wait_ge(o_hi, h.times(1, 1))
                dve.wait_ge(gated, h.times(1, 1))
                d = gls[:, ds(h.times(NVB * 2 * T), NVB * 2 * T)].rearrange("p (c s t) -> p c s t", c=NVB, s=2)
                dve.tensor_tensor(d[:, :, 1, :], g_ot[:].rearrange("p (c t) -> p c t", c=NVB),
                                  d[:, :, 0, :].bitcast(F32), ALU.subtract).then_inc(o_lo, 1)


            def gla_head(h, t, first):
                s0 = T_GLA + QK_TILES
                for k in range(12):
                    lo(t + 2 * k, s0 + 2 * k)
                    if k == 1 and not first:
                        norm_out(h + -1)
                    if k == 2:
                        cumulate(h, 0)
                    if k in (4, 5):
                        decay(h, 2 * (k - 4))
                    if k == 8:
                        gate_silu(h)
                    lo(t + 2 * k + 1, s0 + 2 * k + 1)
                    if k == 2:
                        cumulate(h, 1)
                    if k == 3 and not first:
                        gate_out(h + -1)
                    if k == 4:
                        decay(h, 1)
                    if k == 5 and not first:
                        out_lo(h + -1)
                    if k == 6:
                        mask_att(h)
                    if k >= 9:
                        update_states(h, k - 9)

            s_h = T_GLA + QK_TILES
            gla_head(Pos(0), Pos(s_h), True)
            with dve.Fori(0, GLA_HEADS - 1) as i:
                gla_head(Pos(1, 1, i), Pos(s_h + HEAD_TILES, HEAD_TILES, i), False)
            H = GLA_HEADS - 1
            lo(Pos(T_FIRST), T_FIRST)
            lo(Pos(T_FIRST + 1), T_FIRST + 1)
            norm_out(Pos(H))
            gate_out(Pos(H))
            lo(Pos(T_FIRST + 2), T_FIRST + 2)
            out_lo(Pos(H))

            mc = Chain(dve, m_chain, 1)

            def gate_of(c, parity, early, buffer, done):
                if c.i is None and c.const < 2:
                    dve.wait_ge(proj_taken, B1 + 12 * GLA_HEADS)
                    return g_early[:, (2 * c.const + early) * T:(2 * c.const + early + 1) * T]
                dve.wait_ge(done, c.times(1, -1))
                return buffer[:, parity * T:(parity + 1) * T]

            def gate_a(c, used, parity):
                dve.wait_ge(tile_used, used.times(1))
                gate = gate_of(c, parity, 0, m_sa, sig_a)
                dve.tensor_tensor(m_a[:, parity * T:(parity + 1) * T], bank(4 * parity + 1, 0, T), gate,
                                  ALU.mult).then_inc(a_gated, 1)

            def gate_b(c, used, parity):
                mc.begin(c)
                dve.wait_ge(tile_used, used.times(1))
                gate = gate_of(c, parity, 1, m_sb, sig_b)
                dve.wait_ge(a_gated, c.times(1, 1))
                wait(dve, m_lo, c.times(1, -1))
                a, b = parity * T, (parity + 1) * T
                mc.step(dve.tensor_tensor(m_m[:, a:b], bank(4 * parity + 3, 0, T), gate, ALU.mult))
                dve.tensor_tensor(m_m[:, a:b], m_m[:, a:b], m_a[:, a:b], ALU.add).then_inc(merged, 1)
                mc.end()

            def merged_lo(c, parity):
                dve.wait_ge(m_hi, c.times(1, 1))
                dve.wait_ge(merged, c.times(1, 1))
                dve.tensor_tensor(ms[:, ds(c.times(2 * T, T), T)], m_m[:, parity * T:(parity + 1) * T],
                                  ms[:, ds(c.times(2 * T), T)].bitcast(F32), ALU.subtract).then_inc(m_lo, 1)

            def merge_step(c, t, slot, parity):
                for k in range(MERGE_TILES):
                    lo(t + k, slot + k)
                    if k == 1:
                        gate_b(c + -1, t, 1 - parity)
                    if k == 4:
                        merged_lo(c + -1, 1 - parity)
                        gate_a(c, t + 3, parity)

            lo(Pos(T_FIRST + 3), T_FIRST + 3)
            for c in range(2):
                gate_a(Pos(c), Pos(T_FIRST + 1 + c), c)
            lo(Pos(T_FIRST + 4), T_FIRST + 4)
            gate_b(Pos(0), Pos(T_FIRST + 4), 0)
            lo(Pos(T_FIRST + 5), T_FIRST + 5)
            merged_lo(Pos(0), 0)
            for k in range(2, 4):
                merge_step(Pos(k), Pos(T_MERGE + 7 * k), T_MERGE + 7 * k, k % 2)
            with dve.Fori(0, KC // 4 - 1) as i:
                for k in range(4):
                    merge_step(Pos(4 + k, 4, i), Pos(T_MERGE + 28 + 7 * k, 28, i), T_MERGE + 7 * k, k % 2)
            lo(Pos(T_OUT), T_OUT)
            lo(Pos(T_OUT + 1), T_OUT + 1)
            gate_b(Pos(KC - 1), Pos(T_OUT), 1)
            merged_lo(Pos(KC - 1), 1)

            def add_out(half, tt, n):
                dve.wait_ge(tile_used, T_OUT + KC * (half + 1))
                v = tok[:, tt * D + (2 * half + n) * 512:tt * D + (2 * half + n + 1) * 512]
                dve.scalar_tensor_tensor(out=v, in0=v, scalar=ALPHA, in1=bank(4 * tt + 2 * half + n),
                                         op0=ALU.mult, op1=ALU.add).then_inc(res_done, 1)

            def out_stats(half, tt):
                dve.wait_ge(res_done, 4 * half + 2 * tt + 2)
                for n in range(2):
                    ins = stats(tok, tt, 2 * half + n)
                ln_c.step(ins)

            for k in range(2, 4):
                lo(Pos(T_OUT + k), T_OUT + k)
            dve.wait_ge(p_hi, 1)
            p_dst = ys[:].rearrange("p (c s t) -> p c s t", c=2, s=2)
            dve.tensor_tensor(p_dst[:, :, 1, :], p_in[:].rearrange("p (c t) -> p c t", c=2),
                              p_dst[:, :, 0, :].bitcast(F32), ALU.subtract).then_inc(p_lo, 1)
            with dve.Fori(0, 3) as i:
                for k in range(4):
                    lo(Pos(T_OUT + 4 + k, 4, i), T_OUT + k)
            dve.wait_ge(h_back, 128)
            for k in range(16, 32):
                lo(Pos(T_OUT + k), T_OUT + k)
                if 17 <= k < 21:
                    add_out(0, (k - 17) // 2, (k - 17) % 2)
                if k in (21, 22):
                    out_stats(0, k - 21)
            lo(Pos(T_PLE), T_PLE)
            lo(Pos(T_PLE + 1), T_PLE + 1)
            for tt in range(2):
                for n in range(2):
                    add_out(1, tt, n)
            out_stats(1, 0)
            mean_var(0)
            lo(Pos(T_PLE + 2), T_PLE + 2)
            out_stats(1, 1)
            mean_var(1)
            normalize(1, tok, 0)
            normalize(1, tok, 1)
            lo(Pos(T_PLE + 3), T_PLE + 3)
            lo(Pos(T_PQ), T_PQ)
            lo(Pos(T_PQ + 1), T_PQ + 1)
            features(1, h_feat)

            lo(Pos(T_PQ + 2), T_PQ + 2)
            lo(Pos(T_PQ + 3), T_PQ + 3)
            with dve.Fori(0, KC // 2 - 1) as i:
                for k in range(4):
                    lo(Pos(T_PQ + 4 + k, 4, i), T_PQ + k)
            r2 = Line(dve, res2_chain)

            def add_ple(half, n):
                q = 4 * half + n
                dve.wait_ge(gsig, q + 1)
                dve.wait_ge(h2_ready, n // 2 + 1)
                a, b = q % 2 * 512, (q % 2 + 1) * 512
                v = slice(n // 2 * D + (2 * half + n % 2) * 512, n // 2 * D + (2 * half + n % 2 + 1) * 512)
                r2.step(dve.tensor_tensor(ple_g[:, a:b], ple[:, v], sgm[:, a:b], ALU.mult))
                dve.scalar_tensor_tensor(out=tok[:, v], in0=tok[:, v], scalar=ALPHA, in1=ple_g[:, a:b],
                                         op0=ALU.mult, op1=ALU.add).then_inc(res2_done, 1)

            with dve.Fori(0, 4) as i:
                for k in range(4):
                    lo(Pos(T_PGATE + k, 4, i), T_PGATE + k)
            for k in range(16, 32):
                lo(Pos(T_PGATE + k), T_PGATE + k)
                if 17 <= k < 21:
                    add_ple(0, k - 17)

            tk = Chain(dve, tk_chain, TOP_STEPS, nop=True)

            def best8(scores, values, index):
                tk.step(dve.max(values, scores))
                tk.step(dve.max_index(index, values, scores))

            def drop8(scores, rest, values):
                tk.step(dve.match_replace(rest, values[:, 0:8], scores, LOWEST))

            def key_columns(half):
                return slice(half * NKEYS, (half + 1) * NKEYS), slice(half * TOPK, (half + 1) * TOPK)

            def best_keys(u, half):
                a, b = key_columns(half)
                dve.wait_ge(tk_loaded, u.times(1, 1))
                dve.nop(nofuse=True)
                best8(tk_in[:, a], tk_v[:, b][:, 0:8], tk_i[:, b][:, 0:8])

            def drop_keys(half):
                a, b = key_columns(half)
                drop8(tk_in[:, a], tk_w[:, a], tk_v[:, b])

            def next_keys(half):
                a, b = key_columns(half)
                best8(tk_w[:, a], tk_v[:, b][:, 8:16], tk_i[:, b][:, 8:16])

            def grid(x):
                return x.rearrange("p (a b) -> p a b", a=TOPK)

            def pair_sums():
                a = tk_v[:, 0:TOPK].unsqueeze(2).to_broadcast([P, TOPK, TOPK])
                b = tk_v[:, TOPK:2 * TOPK].unsqueeze(1).to_broadcast([P, TOPK, TOPK])
                tk.step(dve.tensor_tensor(grid(tk_c[:]), a, b, ALU.add))
                dve.tensor_copy(tk_if[:], tk_i[:])

            def best_pairs():
                best8(tk_c[:], tk_cv[:, 0:8], tk_cp[:, 0:8])

            def pair_ranks():
                dve.tensor_scalar(tk_ab[:, 0:TOPK], tk_cp[:], 4, None, ALU.logical_shift_right)
                tk.step(dve.tensor_scalar(tk_ab[:, TOPK:2 * TOPK], tk_cp[:], 15, None, ALU.bitwise_and))

            halves = tk_eq[:].rearrange("p (h a b) -> p h a b", h=2, a=TOPK)

            def match_ranks():
                tk.step(dve.tensor_copy(tk_abf[:], tk_ab[:]))
                r = tk_abf[:].rearrange("p (h a) -> p h a", h=2).unsqueeze(3).to_broadcast([P, 2, TOPK, TOPK])
                ranks = iota_top[:].unsqueeze(1).unsqueeze(1).to_broadcast([P, 2, TOPK, TOPK])
                tk.step(dve.tensor_tensor(halves, r, ranks, ALU.is_equal))

            def look_up(u):
                index = tk_if[:].rearrange("p (h b) -> p h b", h=2).unsqueeze(2).to_broadcast([P, 2, TOPK, TOPK])
                tk.step(dve.tensor_tensor(halves, halves, index, ALU.mult))
                dst = ex[:].rearrange("p (h c) -> p h c", h=2)[:, :, ds(u.times(TOPK), TOPK)]
                tk.step(dve.tensor_reduce(dst, halves, AX.X, ALU.add))

            def minus_best(u):
                tk.step(dve.tensor_scalar(exg[:, ds(u.times(TOPK), TOPK)], tk_cv[:], tk_cv[:, 0:1], None,
                                          ALU.subtract))

            def top_unit(u, t, first=False):
                tk.begin(u)
                for k in range(8):
                    lo(t + k, T_U + k)
                    if first and k % 2 == 0:
                        add_ple(1, k // 2)
                    if k in (0, 2):
                        best_keys(u, k // 2)
                    if k in (1, 2):
                        drop_keys(k - 1)
                    if k in (1, 3):
                        next_keys(k // 2)
                    if k == 3:
                        pair_sums()
                    if k == 4:
                        best_pairs()
                        drop8(tk_c[:], tk_cw[:], tk_cv)
                    if k == 5:
                        best8(tk_cw[:], tk_cv[:, 8:16], tk_cp[:, 8:16])
                        minus_best(u)
                        pair_ranks()
                    if k == 6:
                        match_ranks()
                    if k == 7:
                        look_up(u)
                tk.end()

            dve.wait_ge(sc_taken, HP)
            top_unit(Pos(0), Pos(T_U), True)
            with dve.Fori(0, 15) as i:
                top_unit(Pos(1, 1, i), Pos(T_U + 8, 8, i))

            def hot(g):
                wait(dve, gate_mm, g.times(1))
                for q in range(4):
                    a, b = q * NKEYS, (q + 1) * NKEYS
                    col = ds(g.times(4, q), 1)
                    dve.tensor_scalar(hot0[:, a:b], iota_key[:], idx0_t[:, col], gate_t[:, col],
                                      ALU.is_equal, ALU.mult).then_inc(hot_ready, 1)
                    dve.tensor_scalar(hot1[:, a:b], iota_key[:], idx1_t[:, col], None,
                                      ALU.is_equal).then_inc(hot_ready, 1)

            def column(t, n, g):
                lo(t, T_U + 2 * n)
                if n % 4 == 3:
                    hot(g)
                lo(t + 1, T_U + 2 * n + 1)
                hot(g + 1 if n % 4 == 3 else g)

            for k in range(6):
                lo(Pos(T_U + 128 + k), T_U + k)
                if k == 1:
                    sm = Line(dve, sem("gate_sum_chain"))
                    by_unit = exg[:].rearrange("p (u k) -> p u k", u=HP)
                    dve.wait_ge(tk_exp, 1)
                    sm.step(dve.tensor_reduce(tk_sum[:, 0:HP], by_unit, AX.X, ALU.add))
                    sm.step(dve.reciprocal(tk_sum[:, HP:2 * HP], tk_sum[:, 0:HP]))
                    dve.tensor_tensor(by_unit, by_unit, tk_sum[:, HP:2 * HP].unsqueeze(2).to_broadcast([P, HP, TOPK]),
                                      ALU.mult).then_inc(ex_done, 1)
            dve.wait_ge(ex_t_taken, 3)
            column(Pos(T_U + 134), 3, Pos(0))
            with dve.Fori(0, 6) as i:
                for n in range(8):
                    column(Pos(T_U + 136 + 2 * n, 16, i), n, Pos(2 + n + n // 4, 10, i))
            for n in range(2):
                column(Pos(T_U + 232 + 2 * n), n, Pos(62 + n))
            for k in range(T_U + 236, T_V - 8):
                lo(Pos(k), k)

            by_column = gates[:].rearrange("p (t j) -> p t j", j=NKEYS)

            def weigh(j, slot):
                if j.i is None and j.const < 4:
                    column = NKEYS - 4 + j.const
                    dve.wait_ge(gelu_done, column + 1)
                else:
                    column = j.times(1, -4)
                    dve.wait_ge(gelu_landed[slot], j.over(4).times(16))
                parity = slot % 2
                wait(dve, w_lo, j.times(1, -1))
                dve.tensor_tensor(wexp[:, parity * T:(parity + 1) * T].unsqueeze(2),
                                  gst[:, slot * T:(slot + 1) * T].unsqueeze(2),
                                  by_column[:, :, ds(column, 1)], ALU.mult).then_inc(w_ready, 1)

            def weight_lo(j, parity):
                dve.wait_ge(w_hi, j.times(1, 1))
                dve.wait_ge(w_ready, j.times(1, 1))
                a = parity * 2 * T
                dve.tensor_tensor(ys[:, a + T:a + 2 * T], wexp[:, parity * T:(parity + 1) * T],
                                  ys[:, a:a + T].bitcast(F32), ALU.subtract).then_inc(w_lo, 1)

            for k in range(8):
                lo(Pos(T_V - 8 + k), T_V - 8 + k)
                if k == 4:
                    dve.wait_ge(gate_taken, T // 4)
                    weigh(Pos(0), 0)
                if k == 6:
                    weigh(Pos(1), 1)
                    weight_lo(Pos(0), 0)
                if k == 7:
                    weight_lo(Pos(1), 1)
            lo(Pos(T_V), T_V)
            lo(Pos(T_V + 1), T_V + 1)
            weigh(Pos(2), 2)
            for k in range(2 + AHEAD, 4):
                lower(Pos(T_V + k), T_V + k)

            def four_columns(j, t):
                for k in range(4):
                    lower(t + 2 * k, T_V + 2 * k)
                    weight_lo(j + k, k % 2)
                    lower(t + (2 * k + 1), T_V + 2 * k + 1)
                    weigh(j + (k + 1), (3 + k) % 4)

            four_columns(Pos(2), Pos(T_V + 4))
            with dve.Fori(0, NKEYS // 4 - 2) as i:
                four_columns(Pos(6, 4, i), Pos(T_V + 12, 8, i))
            lower(Pos(T_END - 4), T_END - 4)
            weight_lo(Pos(NKEYS - 2), 0)
            weigh(Pos(NKEYS - 1), 3)
            lower(Pos(T_END - 3), T_END - 3)
            weight_lo(Pos(NKEYS - 1), 1)
            lower(Pos(T_END - 2), T_END - 2)
            lower(Pos(T_END - 1), T_END - 1)

            dve.wait_ge(fin_landed, 16 * 16)
            for half in range(2):
                dve.wait_ge(tile_used, T_END - 2 + 2 * half)
                for tt in range(2):
                    for n in range(2):
                        v = fin[:, tt * D + (2 * half + n) * 512:tt * D + (2 * half + n + 1) * 512]
                        dve.tensor_tensor(v, v, bank(4 * tt + 2 * half + n), ALU.add).then_inc(fin_added, 1)
                    dve.wait_ge(fin_added, 4 * half + 2 * tt + 2)
                    for n in range(2):
                        ins = stats(fin, tt, 2 * half + n)
                    ln_c.step(ins)
                    if half == 1:
                        mean_var(tt)
            for tt in range(2):
                inverse_std(2, tt)
                v = fin[:, tt * D:(tt + 1) * D]
                ln_c.step(dve.scalar_tensor_tensor(out=v, in0=v, scalar=ln_mv[:, 2 * tt:2 * tt + 1],
                                                   in1=fin_tab[:, 0:D], op0=ALU.subtract, op1=ALU.mult))
                for half in range(2):
                    a, b = half * 1024, (half + 1) * 1024
                    dve.scalar_tensor_tensor(out=v[:, a:b], in0=v[:, a:b], scalar=ln_sd[:, 2 * tt + 1:2 * tt + 2],
                                             in1=fin_tab[:, D + a:D + b], op0=ALU.mult,
                                             op1=ALU.add).then_inc(out_ready, 1)


def _block(w):
    return w.reshape(2, 8, P, P).transpose(0, 2, 1, 3).reshape(2, P, TILE)


def _half(w):
    return w.reshape(8, P, P).transpose(1, 0, 2).reshape(1, P, TILE)


def _by_token(w):
    return w.reshape(-1, P, 2, TILE).transpose(2, 0, 1, 3).reshape(-1, P, TILE)


def _layout(a):
    import numpy as np

    w, b = a["w_in"][0], a["b_in"][0]
    naq, nak, nav = 0, 1024, 2048
    gq, gk, gv, gg = 3072, 4096, 5120, 7168
    lrf, lrb, ga, gb = 9216, 9232, 9248, 11296
    cols = []
    for s in range(NA_PAIRS):
        cols += [naq + s * P, nak + s * P, nav + s * P]
    w_rank = np.zeros((D, P), w.dtype)
    b_rank = np.zeros(P, b.dtype)
    for k, at in enumerate((lrf, lrb)):
        w_rank[:, 32 * k:32 * k + RANK] = w[:, at:at + RANK]
        b_rank[32 * k:32 * k + RANK] = b[at:at + RANK]
    qk = [[gq + h * DK + k * P for k in range(2)] + [gk + h * DK + k * P for k in range(2)]
          for h in range(GLA_HEADS)]
    vg = [[gv + h * DV + k * P for k in range(4)] + [gg + h * DV + k * P for k in range(4)]
          for h in range(GLA_HEADS)]
    stream = np.empty((T_END, P, TILE), w.dtype)
    at = 0

    def put(tiles):
        nonlocal at
        stream[at:at + len(tiles)] = tiles
        at += len(tiles)

    for c in cols:
        put(_block(w[:, c:c + P]))
    put(_block(w_rank))
    for c in qk[0]:
        put(_block(w[:, c:c + P]))
    early = [ga, gb, ga + P, gb + P]
    for h in range(GLA_HEADS):
        for c in vg[h] + (qk[h + 1] if h + 1 < GLA_HEADS else early):
            put(_block(w[:, c:c + P]))
    assert at == T_FIRST
    for c in range(2):
        put(_half(a["w_proj_a"][0][:, c * P:(c + 1) * P]))
    for c in range(2):
        put(_block(a["w_proj_b"][0][:, c * P:(c + 1) * P]))
    for c in range(2, KC):
        s = slice(c * P, (c + 1) * P)
        put(_block(w[:, ga + c * P:ga + (c + 1) * P]))
        put(_half(a["w_proj_a"][0][:, s]))
        put(_block(w[:, gb + c * P:gb + (c + 1) * P]))
        put(_block(a["w_proj_b"][0][:, s]))
    put(_by_token(a["w_out"][0]))
    put(_by_token(a["w_ple"][0]))
    for c in range(KC):
        put(_block(a["peer_wq"][0][:, c * P:(c + 1) * P]))
    put(_by_token(a["w_ple_gate"][0]))
    assert at == T_U
    u = a["peer_u"][0].reshape(NKEYS, NKEYS, 2, 8, P)
    stream[T_U:T_V] = u.transpose(1, 2, 4, 3, 0).reshape(2 * NKEYS, P, TILE)
    v = a["peer_v"][0].reshape(NKEYS, NKEYS, 2, TILE)
    v = np.roll(v, 4, axis=1)
    stream[T_V:T_END] = v.transpose(1, 2, 0, 3).reshape(2 * NKEYS, P, TILE)
    stream[[T_END - 3, T_END - 2]] = stream[[T_END - 2, T_END - 3]]

    vectors = np.zeros((P, V_COLS), b.dtype)
    for k, name in enumerate(("ln_emb_g", "ln_emb_b", "ln_a_g", "ln_a_b")):
        vectors[:, V_LN + k * KC:V_LN + (k + 1) * KC] = a[name].reshape(KC, P).T
    for k, c in enumerate(cols):
        vectors[:, V_NA + k] = b[c:c + P]
    vectors[:, V_RANK] = b_rank
    for h in range(GLA_HEADS):
        for k, c in enumerate(qk[h] + vg[h]):
            vectors[:, V_GLA + h * GLA_BLOCKS + k] = b[c:c + P]
        for k, name in enumerate(("gla_gk_bias_f", "gla_gk_bias_b")):
            part = a[name][0].reshape(GLA_HEADS, NKB, P)[h]
            vectors[:, V_DECAY + 4 * h + 2 * k:V_DECAY + 4 * h + 2 * k + 2] = part.T
    for c in range(KC):
        for k, base in enumerate((ga, gb)):
            vectors[:, V_GATES + 2 * c + k] = b[base + c * P:base + (c + 1) * P]
    vectors[:, V_NORM:V_NORM + NVB] = a["gla_norm_g"][0].reshape(NVB, P).T

    rows = T // GRID_W
    q, k = np.arange(T), np.arange(T)
    qr, qc, kr, kc = q // GRID_W, q % GRID_W, k // GRID_W, k % GRID_W
    start = np.clip(qc - WIN_C // 2, 0, GRID_W - WIN_C)
    seen = (kc[None] >= start[:, None]) & (kc[None] < start[:, None] + WIN_C)
    assert rows <= WIN_R
    dr = kr[None] - qr[:, None] + WIN_R - 1
    dc = np.where(seen, kc[None] - qc[:, None] + WIN_C - 1, 0)
    table = a["na_rpb"][0][:, dr, dc]
    table = np.where(seen[None], table, np.float32(MASKED)).astype(b.dtype)
    rpb = table.reshape(NA_PAIRS, 2, 2, P, T).transpose(0, 3, 1, 2, 4).reshape(NA_PAIRS, P, 4 * T)

    up = np.zeros((GLA_HEADS, 64, DK), w.dtype)
    for k, name in enumerate(("gla_gk_up_f", "gla_gk_up_b")):
        up[:, 32 * k:32 * k + RANK] = a[name][0].reshape(RANK, GLA_HEADS, DK).transpose(1, 0, 2)
    keys = a["peer_sub_keys"][0].reshape(HP, NKEYS, P).transpose(2, 0, 1).reshape(P, HP * NKEYS)
    gains = np.stack([a[n].reshape(D) for n in ("ln_emb_g", "ln_emb_b", "ln_a_g", "ln_a_b", "ln_b_g",
                                                "ln_b_b")]).reshape(3, 2 * D)
    p_t = a["p"][0, 0].T.reshape(2, P, T).transpose(1, 0, 2).reshape(P, 2 * T)
    return {"stream": stream, "vectors": vectors, "gains": gains,
            "x_in": a["x"].reshape(2, P, D), "p_t": p_t, "rpb": rpb, "decay_up": up, "keys": keys}


def kernel(**inputs):
    import numpy as np
    import concourse.bacc as bacc
    from concourse.bass_utils import run_bass_kernel_spmd

    laid = {n: np.ascontiguousarray(v) for n, v in
            _layout({n: np.asarray(v) for n, v in inputs.items()}).items()}
    nc = bacc.Bacc("TRN2", target_bir_lowering=False, num_devices=1)
    args = {n: nc.dram_tensor(n, v.shape, mybir.dt.from_np(v.dtype), kind="ExternalInput").ap()
            for n, v in laid.items()}
    out = nc.dram_tensor("out", (2, P, D), mybir.dt.float32, kind="ExternalOutput").ap()
    encoder_layer(nc, out=out, **args)
    r = run_bass_kernel_spmd(nc, [laid], core_ids=[0])
    return np.asarray(r.results[0]["out"]).reshape(1, T, D)
```
